# Optimizing a Trainium2 kernel written in Bass

```python
import math
import jax, jax.numpy as jnp
from jax import lax
import numpy as np

D_MODEL = 1024
BATCH = 1
SEQ = 512
DEPTH = 1
DEC_BATCH = 8
DEC_SEQ = 8
PAST_LEN = 2048
PAGE_SIZE = 128

HEAD_DIM = 64
MIX_WIDTH = D_MODEL
A_WIDTH = MIX_WIDTH // 2
B_WIDTH = MIX_WIDTH - A_WIDTH
A_HEADS = A_WIDTH // HEAD_DIM
B_HEADS = B_WIDTH // (2 * HEAD_DIM)
B_VDIM = 2 * HEAD_DIM
DILATIONS = ((128, 1), (512, 4), (2048, 16))
WINDOW_MAX = 2048
BAND_BLOCK = 128
D_FF = ((8 * D_MODEL // 3 + 127) // 128) * 128
ROPE_THETA = 10000.0
LN_EPS = 1e-5
RMS_EPS = 1e-5
DEEPNORM_ALPHA = (2.0 * DEPTH) ** 0.25
DEEPNORM_BETA = (8.0 * DEPTH) ** -0.25
FFN_RES = 0.5
N_ADA = 9
QKV_SPLITS = (A_WIDTH, 2 * A_WIDTH, 3 * A_WIDTH,
              3 * A_WIDTH + 2 * B_HEADS * HEAD_DIM,
              3 * A_WIDTH + 4 * B_HEADS * HEAD_DIM)
QKV_WIDTH = 3 * A_WIDTH + 4 * B_HEADS * HEAD_DIM + B_HEADS * B_VDIM

kernel_name = "hybrid_dilated_diff_attn_decoder_step"

def layer_norm(x, g, b):
    xf = x.astype(jnp.float32)
    mu = jnp.mean(xf, -1, keepdims=True)
    var = jnp.mean(jnp.square(xf - mu), -1, keepdims=True)
    y = (xf - mu) * lax.rsqrt(var + LN_EPS)
    return (y * g.astype(jnp.float32) + b.astype(jnp.float32)).astype(x.dtype)

def rope(x, pos):
    e = x.shape[-1]
    inv = ROPE_THETA ** (-jnp.arange(0, e, 2, dtype=jnp.float32) / e)
    ang = pos.astype(jnp.float32)[:, None] * inv[None, :]
    shape = (pos.shape[0],) + (1,) * (x.ndim - 3) + (e // 2,)
    cos = jnp.cos(ang).reshape(shape)
    sin = jnp.sin(ang).reshape(shape)
    xf = x.astype(jnp.float32)
    x1, x2 = xf[..., : e // 2], xf[..., e // 2:]
    return jnp.concatenate([x1 * cos - x2 * sin, x2 * cos + x1 * sin], -1).astype(x.dtype)

def swiglu(h, w_in, w_out):
    g, u = jnp.split(h @ w_in, 2, axis=-1)
    return (jax.nn.silu(g) * u) @ w_out

def project_heads(h, w_qkv, pos):
    b, L = h.shape[0], h.shape[1]
    aq, ak, av, bq, bk, bv = jnp.split(h @ w_qkv, list(QKV_SPLITS), axis=-1)
    aq = rope(aq.reshape(b, L, A_HEADS, HEAD_DIM), pos)
    ak = rope(ak.reshape(b, L, A_HEADS, HEAD_DIM), pos)
    av = av.reshape(b, L, A_HEADS, HEAD_DIM)
    bq = rope(bq.reshape(b, L, B_HEADS, 2, HEAD_DIM), pos)
    bk = rope(bk.reshape(b, L, B_HEADS, 2, HEAD_DIM), pos)
    bv = bv.reshape(b, L, B_HEADS, B_VDIM)
    return aq, ak, av, bq, bk, bv

def dilated_band_attention(q, k, v, dilation, span):
    b, L, h, e = q.shape
    unit = dilation * BAND_BLOCK
    lp = -(-L // unit) * unit
    nb = lp // unit
    pad = ((0, 0), (0, lp - L), (0, 0), (0, 0))

    def to_bands(t):
        t = jnp.pad(t, pad).reshape(b, lp // dilation, dilation, h, e)
        return jnp.swapaxes(t, 1, 2).reshape(b, dilation, nb, BAND_BLOCK, h, e)

    def band(t):
        tp = jnp.pad(t, ((0, 0), (0, 0), (1, 0), (0, 0), (0, 0), (0, 0)))
        return jnp.concatenate([tp[:, :, :-1], tp[:, :, 1:]], axis=3)

    qb = to_bands(q).astype(jnp.float32)
    kband = band(to_bands(k)).astype(jnp.float32)
    vband = band(to_bands(v)).astype(jnp.float32)
    s = jnp.einsum('brnqhe,brnkhe->brnhqk', qb, kband) * (e ** -0.5)
    qi = jnp.arange(BAND_BLOCK)[:, None]
    kj = jnp.arange(2 * BAND_BLOCK)[None, :]
    dist = qi + BAND_BLOCK - kj
    key_sub = jnp.arange(nb)[:, None, None] * BAND_BLOCK + kj[None] - BAND_BLOCK
    valid = (dist >= 0)[None] & (dist <= span)[None] & (key_sub >= 0)
    s = jnp.where(valid[None, None, :, None], s, -jnp.inf)
    lse = jax.nn.logsumexp(s, axis=-1)
    p = jnp.exp(s - lse[..., None])
    o = jnp.einsum('brnhqk,brnkhe->brnqhe', p, vband)
    o = jnp.swapaxes(o.reshape(b, dilation, lp // dilation, h, e), 1, 2).reshape(b, lp, h, e)[:, :L]
    lse = jnp.transpose(lse, (0, 1, 2, 4, 3)).reshape(b, dilation, lp // dilation, h)
    lse = jnp.swapaxes(lse, 1, 2).reshape(b, lp, h)[:, :L]
    return o, lse

def dilated_gather_attention(q, kcat, vcat, dilation, span):
    b, s_new, h, e = q.shape
    w = kcat.shape[1] - s_new
    idx = w + jnp.arange(s_new)[:, None] - dilation * jnp.arange(span + 1)[None, :]
    valid = idx >= 0
    kg = jnp.take(kcat, jnp.clip(idx, 0), axis=1).astype(jnp.float32)
    vg = jnp.take(vcat, jnp.clip(idx, 0), axis=1).astype(jnp.float32)
    sc = jnp.einsum('bqhe,bqjhe->bhqj', q.astype(jnp.float32), kg) * (e ** -0.5)
    sc = jnp.where(valid[None, None], sc, -jnp.inf)
    lse = jax.nn.logsumexp(sc, axis=-1)
    p = jnp.exp(sc - lse[..., None])
    o = jnp.einsum('bhqj,bqjhe->bqhe', p, vg)
    return o, jnp.swapaxes(lse, 1, 2)

def merge_by_denominator(outs, lses):
    wts = jax.nn.softmax(jnp.stack(lses, 0), axis=0)
    return jnp.sum(wts[..., None] * jnp.stack(outs, 0), axis=0)

def diff_attention_rows(q, q_pos, k, v, lam):
    e = q.shape[-1]
    s = jnp.einsum('bqhce,bkhce->bhcqk', q.astype(jnp.float32), k.astype(jnp.float32)) * (e ** -0.5)
    mask = jnp.arange(k.shape[1])[None, :] <= q_pos[:, None]
    a = jax.nn.softmax(jnp.where(mask, s, -jnp.inf), axis=-1)
    attn = a[:, :, 0] - lam * a[:, :, 1]
    return jnp.einsum('bhqk,bkhe->bqhe', attn, v.astype(jnp.float32))

def diff_head_norm(o, g, lam_init):
    o = o * lax.rsqrt(jnp.mean(o * o, -1, keepdims=True) + RMS_EPS) * g.astype(jnp.float32)
    return o * (1.0 - lam_init)

def prompt_mixer(h, w_qkv, lam, lam_init, subln_g):
    b, L, _ = h.shape
    pos = jnp.arange(L, dtype=jnp.int32)
    aq, ak, av, bq, bk, bv = project_heads(h, w_qkv, pos)
    outs, lses = [], []
    for window, dil in DILATIONS:
        o, lse = dilated_band_attention(aq, ak, av, dil, window // dil)
        outs.append(o)
        lses.append(lse)
    a_out = merge_by_denominator(outs, lses)
    nq = L // BAND_BLOCK
    qb = jnp.swapaxes(bq.reshape(b, nq, BAND_BLOCK, B_HEADS, 2, HEAD_DIM), 0, 1)
    pb = pos.reshape(nq, BAND_BLOCK)
    ob = lax.map(lambda xs: diff_attention_rows(xs[0], xs[1], bk, bv, lam), (qb, pb))
    b_out = jnp.swapaxes(ob, 0, 1).reshape(b, L, B_HEADS, B_VDIM)
    b_out = diff_head_norm(b_out, subln_g, lam_init)
    mixed = jnp.concatenate([a_out.reshape(b, L, A_WIDTH), b_out.reshape(b, L, B_WIDTH)], -1).astype(h.dtype)
    wb = min(WINDOW_MAX, L)
    state = (ak[:, L - wb:], av[:, L - wb:],
             bk.reshape(b, L // PAGE_SIZE, PAGE_SIZE, B_HEADS, 2, HEAD_DIM),
             bv.reshape(b, L // PAGE_SIZE, PAGE_SIZE, B_HEADS, B_VDIM))
    return mixed, state

def sample_mixer(h, win_k, win_v, pool_k, pool_v, page_table, w_qkv, lam, lam_init, subln_g):
    b, s_new, _ = h.shape
    pos = PAST_LEN + jnp.arange(s_new, dtype=jnp.int32)
    aq, ak, av, bq, bk, bv = project_heads(h, w_qkv, pos)
    kcat = jnp.concatenate([win_k, ak.astype(win_k.dtype)], axis=1)
    vcat = jnp.concatenate([win_v, av.astype(win_v.dtype)], axis=1)
    outs, lses = [], []
    for window, dil in DILATIONS:
        o, lse = dilated_gather_attention(aq, kcat, vcat, dil, window // dil)
        outs.append(o)
        lses.append(lse)
    a_out = merge_by_denominator(outs, lses)
    past_k = pool_k[page_table].reshape(b, PAST_LEN, B_HEADS, 2, HEAD_DIM)
    past_v = pool_v[page_table].reshape(b, PAST_LEN, B_HEADS, B_VDIM)
    k_all = jnp.concatenate([past_k, bk.astype(past_k.dtype)], axis=1)
    v_all = jnp.concatenate([past_v, bv.astype(past_v.dtype)], axis=1)
    b_out = diff_head_norm(diff_attention_rows(bq, pos, k_all, v_all, lam), subln_g, lam_init)
    mixed = jnp.concatenate([a_out.reshape(b, s_new, A_WIDTH), b_out.reshape(b, s_new, B_WIDTH)], -1).astype(h.dtype)
    return mixed, (ak, av, bk, bv)

def decoder_layer(x, c, mixer, ln_g, ln_b, w_ada, b_ada, f1_in, f1_out, f2_in, f2_out, w_o):
    mod = (jax.nn.silu(c) @ w_ada + b_ada).reshape(c.shape[0], N_ADA, 1, D_MODEL)
    sh1, sc1, g1, sh2, sc2, g2, sh3, sc3, g3 = [mod[:, i] for i in range(N_ADA)]
    h = x * (1.0 + sc1) + sh1
    x = layer_norm(DEEPNORM_ALPHA * x + FFN_RES * g1 * swiglu(h, f1_in, f1_out), ln_g[0], ln_b[0])
    h = x * (1.0 + sc2) + sh2
    mixed, state = mixer(h)
    x = layer_norm(DEEPNORM_ALPHA * x + g2 * (mixed @ w_o), ln_g[1], ln_b[1])
    h = x * (1.0 + sc3) + sh3
    x = layer_norm(DEEPNORM_ALPHA * x + FFN_RES * g3 * swiglu(h, f2_in, f2_out), ln_g[2], ln_b[2])
    return x, state

def setup_inputs(seed: int = 0) -> dict:
    key = jax.random.key(seed)
    ks = jax.random.split(key, 24)
    f32 = jnp.float32
    n_pages = PAST_LEN // PAGE_SIZE
    n_pool = (DEC_BATCH * n_pages * 5) // 4
    w_buf = min(WINDOW_MAX, PAST_LEN)

    def nrm(k, shape, scale=1.0):
        return jax.random.normal(k, shape, f32) * scale

    perm = jax.random.permutation(ks[8], n_pool)
    page_table = perm[: DEC_BATCH * n_pages].reshape(DEC_BATCH, n_pages).astype(jnp.int32)
    return {
        "x_prompt": nrm(ks[0], (BATCH, SEQ, D_MODEL)),
        "x_sample": nrm(ks[1], (DEC_BATCH, DEC_SEQ, D_MODEL)),
        "c_prompt": nrm(ks[2], (BATCH, D_MODEL)),
        "c_sample": nrm(ks[3], (DEC_BATCH, D_MODEL)),
        "cache_win_k": nrm(ks[4], (DEPTH, DEC_BATCH, w_buf, A_HEADS, HEAD_DIM)),
        "cache_win_v": nrm(ks[5], (DEPTH, DEC_BATCH, w_buf, A_HEADS, HEAD_DIM)),
        "cache_diff_k": nrm(ks[6], (DEPTH, n_pool, PAGE_SIZE, B_HEADS, 2, HEAD_DIM)),
        "cache_diff_v": nrm(ks[7], (DEPTH, n_pool, PAGE_SIZE, B_HEADS, B_VDIM)),
        "page_table": page_table,
        "ln_g": 1.0 + nrm(ks[9], (DEPTH, 3, D_MODEL), 0.02),
        "ln_b": nrm(ks[10], (DEPTH, 3, D_MODEL), 0.02),
        "w_ada": nrm(ks[11], (DEPTH, D_MODEL, N_ADA * D_MODEL), D_MODEL ** -0.5),
        "b_ada": nrm(ks[12], (DEPTH, N_ADA * D_MODEL), 0.02),
        "ffn1_w_in": nrm(ks[13], (DEPTH, D_MODEL, 2 * D_FF), D_MODEL ** -0.5),
        "ffn1_w_out": nrm(ks[14], (DEPTH, D_FF, D_MODEL), DEEPNORM_BETA * D_FF ** -0.5),
        "ffn2_w_in": nrm(ks[15], (DEPTH, D_MODEL, 2 * D_FF), D_MODEL ** -0.5),
        "ffn2_w_out": nrm(ks[16], (DEPTH, D_FF, D_MODEL), DEEPNORM_BETA * D_FF ** -0.5),
        "w_qkv": nrm(ks[17], (DEPTH, D_MODEL, QKV_WIDTH), D_MODEL ** -0.5),
        "w_o": nrm(ks[18], (DEPTH, MIX_WIDTH, D_MODEL), DEEPNORM_BETA * MIX_WIDTH ** -0.5),
        "diff_lambda": nrm(ks[19], (DEPTH, 4, HEAD_DIM), 0.1),
        "subln_g": 1.0 + nrm(ks[20], (DEPTH, B_VDIM), 0.02),
    }

def reference(x_prompt, x_sample, c_prompt, c_sample, cache_win_k, cache_win_v, cache_diff_k,
              cache_diff_v, page_table, ln_g, ln_b, w_ada, b_ada, ffn1_w_in, ffn1_w_out,
              ffn2_w_in, ffn2_w_out, w_qkv, w_o, diff_lambda, subln_g):
    yp, ys = x_prompt, x_sample
    st_p, st_s = [], []
    for l in range(DEPTH):
        lam_init = 0.8 - 0.6 * math.exp(-0.3 * l)
        lp = diff_lambda[l].astype(jnp.float32)
        lam = jnp.exp(jnp.sum(lp[0] * lp[1])) - jnp.exp(jnp.sum(lp[2] * lp[3])) + lam_init
        common = (ln_g[l], ln_b[l], w_ada[l], b_ada[l], ffn1_w_in[l], ffn1_w_out[l],
                  ffn2_w_in[l], ffn2_w_out[l], w_o[l])
        wq, sg = w_qkv[l], subln_g[l]
        yp, sp = decoder_layer(yp, c_prompt, lambda h: prompt_mixer(h, wq, lam, lam_init, sg), *common)
        ys, ss = decoder_layer(
            ys, c_sample,
            lambda h: sample_mixer(h, cache_win_k[l], cache_win_v[l], cache_diff_k[l], cache_diff_v[l],
                                   page_table, wq, lam, lam_init, sg),
            *common)
        st_p.append(sp)
        st_s.append(ss)
    new_win_k_prompt = jnp.stack([s[0] for s in st_p])
    new_win_v_prompt = jnp.stack([s[1] for s in st_p])
    new_diff_k_prompt = jnp.stack([s[2] for s in st_p])
    new_diff_v_prompt = jnp.stack([s[3] for s in st_p])
    new_win_k_sample = jnp.stack([s[0] for s in st_s])
    new_win_v_sample = jnp.stack([s[1] for s in st_s])
    new_diff_k_sample = jnp.stack([s[2] for s in st_s])
    new_diff_v_sample = jnp.stack([s[3] for s in st_s])
    return (yp, ys, new_win_k_prompt, new_win_v_prompt, new_win_k_sample, new_win_v_sample,
            new_diff_k_prompt, new_diff_v_prompt, new_diff_k_sample, new_diff_v_sample)


_drawn_inputs = setup_inputs


def setup_inputs(seed=0):
    import zlib

    import numpy as np

    out = dict(_drawn_inputs(seed))
    spreads = {}
    factors = {'diff_lambda': 3.619, 'subln_g': 29.619, 'cache_win_k': 3.828, 'cache_win_v': 3.541}
    for name, (base, spread) in spreads.items():
        noise = np.random.default_rng([zlib.crc32(name.encode()), seed]).standard_normal(out[name].shape)
        drawn = base * np.exp(spread * noise) if base else spread * noise
        out[name] = __import__('jax').numpy.asarray(drawn.astype(out[name].dtype))
    for name, factor in factors.items():
        out[name] = (out[name] * factor).astype(out[name].dtype)
    return out
```

```python
import math
from contextlib import ExitStack

import concourse.bass as bass
import numpy as np
from concourse import mybir

F32 = mybir.dt.float32
F32R = mybir.dt.float32r
I32 = mybir.dt.int32
ALU = mybir.AluOpType
ACT = mybir.ActivationFunctionType
AX_X = mybir.AxisListType.X
ds = bass.ds

P = 128
D = 1024
DB = D // P
NPR = 512
PT_ = NPR // P
NB = 8
NS = 8
NSM = NB * NS
T = NPR + NSM
TH = T // 2
FF = 2816
FB = FF // P
HB = FB // 2
NC_ = 1 + NB
NM = 9
QW = 512
E = 64
PAST = 2048
PAGE = 128
NPAGE = PAST // PAGE
ALPHA = 2.0 ** 0.25
LN_EPS = 1e-5
RMS_EPS = 1e-5
LAM_INIT = 0.8 - 0.6 * math.exp(0.0)
SCALE = E ** -0.5
MASKED = -1e30
WCH = HB * P
DENSE = 512
A_NEAR = DENSE // P
A_FAR = 8
FARW = (PAST - DENSE) // 16
A_KEYS = A_FAR * FARW + A_NEAR * P
A_CHUNKS = (4, 4, 2, 2)
B_CHUNKS = (4, 4, 4, 4)
SW = PAST + NSM


def constants():
    inv = (np.float32(10000.0) ** (-np.arange(0, E, 2, dtype=np.float32) / np.float32(E))).astype(np.float32)
    pos = np.concatenate([np.arange(NPR), np.tile(PAST + np.arange(NS), NB)]).astype(np.float32)
    ang = pos[:, None] * inv[None, :]
    rope = np.zeros((P, PT_ + 1, 2, E // 2), np.float32)
    for t in range(PT_ + 1):
        rows = min(P, T - t * P)
        rope[:rows, t, 0] = np.cos(ang[t * P:t * P + rows])
        rope[:rows, t, 1] = np.sin(ang[t * P:t * P + rows])

    def log_count(delta):
        n = ((delta >= 0) & (delta <= 128)).astype(int)
        n += (delta >= 0) & (delta <= 512) & (delta % 4 == 0)
        n += (delta >= 0) & (delta <= 2048) & (delta % 16 == 0)
        return np.where(n > 0, np.log(np.maximum(n, 1)), MASKED).astype(np.float32)

    row, col = np.arange(P)[:, None], np.arange(NPR)[None, :]
    delta = row + (NPR - P) - col
    causal = np.where(delta >= 0, 0.0, MASKED).astype(np.float32)
    far = (np.arange(A_FAR)[:, None] + 16 * np.arange(FARW)[None, :]).ravel()
    near = (PAST - DENSE + np.arange(A_NEAR)[:, None] + A_NEAR * np.arange(P)[None, :]).ravel()
    keys = np.concatenate([far, near])
    query = (np.arange(P) % NS)[:, None]
    past = log_count(PAST + query - keys[None, :])
    new = np.full((P, 2, NB, NSM), MASKED, np.float32)
    own = query - np.arange(NS)[None, :]
    for b in range(NB):
        new[:, 0, b, b * NS:(b + 1) * NS] = log_count(own)
        new[:, 1, b, b * NS:(b + 1) * NS] = np.where(own >= 0, 0.0, MASKED)
    return {
        "ident": np.eye(P, dtype=np.float32), "rope": rope.reshape(P, -1),
        "mask_a": log_count(delta), "mask_b": causal, "past_a": past, "new_ab": new.reshape(P, -1),
    }


def build(nc, x_prompt, x_sample, c_prompt, c_sample, win_k, win_v, diff_k, diff_v, page_table, ln_g, ln_b,
          w_ada, b_ada, f1_in, f1_out, f2_in, f2_out, w_qkv, w_o, diff_lambda, subln_g,
          ident_d, rope_d, mask_a_d, mask_b_d, past_a_d, new_ab_d,
          y_prompt, y_sample, wkp, wvp, wks, wvs, dkp, dvp, dks, dvs):
    with ExitStack() as ctx:
        sems = {}

        def sem(name):
            if name not in sems:
                sems[name] = ctx.enter_context(nc.semaphore(name))
            return sems[name]

        at = [nc.sbuf_base + (-nc.sbuf_base) % 64]

        def place(name, shape, dt=F32, offset=None):
            size = int(np.prod(shape[1:])) * 4
            where = at[0] if offset is None else offset
            if offset is None:
                at[0] += (size + 63) // 64 * 64
            assert where + size <= nc.sbuf_usable_end, name
            return nc.alloc_sbuf_tensor_at(name, shape, dt, offset=where), where + (size + 63) // 64 * 64

        ident, _ = place("ident", [P, P])
        one_d, _ = place("one_d", [P, P])
        one_v, _ = place("one_v", [P, P])
        modT, _ = place("modT", [P, NM, DB, NC_])
        colT, _ = place("colT", [P, 128])
        stat, _ = place("stat", [P, 64])
        pages, _ = place("pages", [1, NB * NPAGE], I32)
        xT, _ = place("xT", [P, DB, T])
        w32, _ = place("w32", [P, 2, WCH])
        whi, _ = place("whi", [P, 2, WCH], F32R)
        wlo, _ = place("wlo", [P, 2, WCH], F32R)
        tmp, _ = place("tmp", [P, 4, T])
        hreg = at[0]
        hhi, _ = place("hhi", [P, DB, T], F32R)
        hlo, hend = place("hlo", [P, DB, T], F32R)
        freg = at[0]
        ffhi, _ = place("ffhi", [P, FB, T], F32R)
        fflo, fend = place("fflo", [P, FB, T], F32R)
        xtok, o = place("xtok", [P, PT_ + 1, D], offset=freg)
        wada, o = place("wada", [P, 4, DB // 2, D], offset=o)
        assert o <= fend
        ctok, o = place("ctok", [NC_, D], offset=hreg)
        csil, o = place("csil", [NC_, D], offset=o)
        cT, o = place("cT", [P, DB, 32], offset=o)
        rows, o = place("rows", [P, P], offset=o)
        modrow, o = place("modrow", [P, 2, 256], offset=o)
        lamb, o = place("lamb", [P, 4, E], offset=o)
        lamp, o = place("lamp", [P, 2, E], offset=o)
        assert o <= hend
        QT, o = place("QT", [P, 8, T], offset=freg)
        KT, o = place("KT", [P, 8, T], offset=o)
        V, o = place("V", [P, 2, PT_ + 1, QW], offset=o)
        QB, o = place("QB", [P, 2, 4, 32], offset=o)
        PTo = o
        rot, o = place("rot", [P, PT_ + 1, QW], offset=o)
        rab, o = place("rab", [P, 2, QW], offset=o)
        PTp, o2 = place("PTp", [P, PT_, NPR], offset=PTo)
        PTd, o3 = place("PTd", [P, NPAGE + 1, P], offset=PTo)
        new_ab, o4 = place("new_ab", [P, 2, NB, NSM], offset=o3)
        o = max(o, o2, o4)
        kv01, o = place("kv01", [P, 2, 4, QW], offset=o)
        ropet, o = place("ropet", [P, PT_ + 1, 2, E // 2], offset=o)
        mask_a, o = place("mask_a", [P, NPR], offset=o)
        mask_b, o = place("mask_b", [P, NPR], offset=o)
        past_a, o = place("past_a", [P, A_KEYS], offset=o)
        assert o <= fend
        kv23, o = place("kv23", [P, 2, 4, QW], offset=hreg)
        KC, o = place("KC", [P, 4, QW], offset=o)
        S, o = place("S", [P, SW], offset=o)
        On, o = place("On", [P, P], offset=o)
        assert o <= hend
        ytok, o = place("ytok", [P, PT_ + 1, D], offset=freg)

        def kv(slot):
            return kv01[:, slot] if slot < 2 else kv23[:, slot - 2]

        ps = ctx.enter_context(nc.psum_tensor("ps", [P, 8, 512], F32))

        block = ctx.enter_context(nc.Block())

        def pairs(eng, n, body, tail=0):
            body(0, 0)
            body(1, 1)
            with eng.Fori(1, n // 2 - tail) as i:
                body(2 * i, 0)
                body(2 * i + 1, 1)
            for s in range(n - 2 * tail, n):
                body(s, s % 2)

        class Weights:
            def __init__(self, name, chunks, width, before, run=0):
                self.chunks, self.width, self.before, self.base = chunks, width, before, run * chunks
                self.landed = [sem(f"{name}_landed{slot}") for slot in range(2)]
                self.hi, self.lo, self.used = sem(name + "_hi"), sem(name + "_lo"), sem(name + "_used")

        in1 = Weights("w_in", 2 * FB, DB * P, None)
        out1 = Weights("w_out", 2 * DB, HB * P, in1)
        qkv = Weights("w_qkv", 24, 2 * QW, out1)
        wo = Weights("w_o", DB, DB * P, qkv)
        in3 = Weights("w_in", 2 * FB, DB * P, wo, run=1)
        out3 = Weights("w_out", 2 * DB, HB * P, in3, run=1)

        def load_chunk(ph, c, slot, src, nk):
            if not (isinstance(c, int) and c < 2):
                nc.sync.wait_ge(ph.lo, ph.base + c - 1)
            elif ph.before:
                nc.sync.wait_ge(ph.before.lo, ph.before.base + ph.before.chunks - 1 + c)
            dst = w32[:, slot, 0:ph.width].rearrange("p (k n) -> p k n", k=nk)
            nc.sync.dma_start(dst, src).then_inc(ph.landed[slot], 16)

        def split_hi(ph, c, slot):
            n = c // 2 * 16 if isinstance(c, int) else (c - slot) * 8
            nc.scalar.wait_ge(ph.landed[slot], 8 * ph.base + n + 16)
            if not (isinstance(c, int) and c < 2):
                nc.scalar.wait_ge(ph.used, ph.base + c - 1)
            elif ph.before:
                nc.scalar.wait_ge(ph.before.used, ph.before.base + ph.before.chunks - 1 + c)
            w = ph.width
            nc.scalar.activation(whi[:, slot, 0:w], w32[:, slot, 0:w], ACT.Copy).then_inc(ph.hi, 1)

        def split_lo(ph, c, slot):
            nc.vector.wait_ge(ph.hi, ph.base + c + 1)
            w = ph.width
            nc.vector.tensor_tensor(wlo[:, slot, 0:w], w32[:, slot, 0:w], whi[:, slot, 0:w].bitcast(F32),
                                    ALU.subtract).then_inc(ph.lo, 1)

        def chunk_products(ph, slot, nk, xhi, xlo, k0, kall, banks):
            pe = nc.tensor
            m = None
            for k in range(nk):
                kk = k0 + k
                wh = whi[:, slot, k * P:(k + 1) * P]
                wl = wlo[:, slot, k * P:(k + 1) * P]
                for n, (w, x) in enumerate(((wh, xhi), (wh, xlo), (wl, xhi))):
                    for h in range(2):
                        m = pe.matmul(ps[:, banks + h, 0:TH], w, x[:, kk, h * TH:(h + 1) * TH],
                                      start=(kk == 0 and n == 0), stop=(kk == kall - 1 and n == 2))
            m.then_inc(ph.used, 1)

        def modulate_vector(st, i_shift, i_scale):
            eng = nc.vector
            def lo(d):
                eng.wait_ge(sem("step_hhi"), st * DB + d + 1)
                eng.tensor_tensor(hlo[:, d, :], tmp[:, d % 2, :], hhi[:, d, :].bitcast(F32),
                                  ALU.subtract).then_inc(sem("step_hlo"), 1)
            for d in range(DB):
                if st > 0:
                    eng.wait_ge(sem("step_x"), (st - 1) * DB + d + 1)
                else:
                    eng.wait_ge(sem("x_copied"), d + 1)
                    eng.wait_ge(sem("xs_copied"), 1)
                if d >= 2:
                    eng.wait_ge(sem("step_hlo"), st * DB + d - 1)
                eng.tensor_scalar(tmp[:, d % 2, 0:NPR], xT[:, d, 0:NPR], modT[:, i_scale, d, 0:1],
                                  modT[:, i_shift, d, 0:1], ALU.mult, ALU.add).then_inc(sem("step_h"), 1)
                hs = tmp[:, d % 2, NPR:T].rearrange("p (b s) -> p b s", s=NS)
                xs = xT[:, d, NPR:T].rearrange("p (b s) -> p b s", s=NS)
                eng.tensor_tensor(hs, xs, modT[:, i_scale, d, 1:NC_].unsqueeze(2).to_broadcast([P, NB, NS]),
                                  ALU.mult).then_inc(sem("step_hm"), 1)
                eng.wait_ge(sem("step_hm"), st * DB + d + 1)
                eng.tensor_tensor(hs, hs, modT[:, i_shift, d, 1:NC_].unsqueeze(2).to_broadcast([P, NB, NS]),
                                  ALU.add).then_inc(sem("step_h"), 1)
                if d >= 1:
                    lo(d - 1)
            lo(DB - 1)

        def modulate_scalar(st):
            eng = nc.scalar
            for d in range(DB):
                eng.wait_ge(sem("step_h"), st * 2 * DB + 2 * d + 2)
                eng.activation(hhi[:, d, :], tmp[:, d % 2, :], ACT.Copy).then_inc(sem("step_hhi"), 1)

        def scale_residual(st):
            eng = nc.gpsimd
            eng.wait_ge(sem("step_h"), st * 2 * DB + 2 * DB)
            for d in range(DB):
                eng.tensor_scalar(xT[:, d, :], xT[:, d, :], ALPHA, None, ALU.mult).then_inc(sem("step_xa"), 1)

        def project_tensor(st, ph, nk_chunk, n_half, xhi, xlo):
            pe = nc.tensor
            kall = nk_chunk * n_half
            def body(d, par):
                if not (isinstance(d, int) and d < 2):
                    pe.wait_ge(sem("step_res"), st * DB + d - 1)
                for hh in range(n_half):
                    slot = hh if n_half == 2 else par
                    pe.wait_ge(ph.lo, ph.base + n_half * d + hh + 1)
                    chunk_products(ph, slot, nk_chunk, xhi, xlo, hh * nk_chunk, kall, 2 * par)
            pairs(pe, DB, body)
            for d in range(DB):
                pe.wait_ge(sem("step_res"), st * DB + d + 1)
                for h in range(2):
                    m = pe.matmul(ps[:, 4 + h, 0:TH], one_d[:], xT[:, d, h * TH:(h + 1) * TH],
                                  start=(d == 0), stop=(d == DB - 1))
            m.then_inc(sem("step_mean"), 1)
            for d in range(DB):
                pe.wait_ge(sem("step_sq"), st * DB + d + 1)
                for h in range(2):
                    m = pe.matmul(ps[:, 6 + h, 0:TH], one_d[:], tmp[:, d % 2, h * TH:(h + 1) * TH],
                                  start=(d == 0), stop=(d == DB - 1))
                m.then_inc(sem("step_var"), 1)

        def project_vector(st, ph, n_half, i_gate):
            eng = nc.vector
            n = DB * n_half
            split_lo(ph, 0, 0)
            split_lo(ph, 1, 1)
            for d in range(DB):
                if n_half == 2 and 2 * d + 2 < n:
                    split_lo(ph, 2 * d + 2, 0)
                eng.wait_ge(ph.used, ph.base + n_half * (d + 1))
                eng.wait_ge(sem("step_xa"), st * DB + d + 1)
                b = 2 * (d % 2)
                gate = modT[:, i_gate, d, 0:1]
                eng.scalar_tensor_tensor(out=xT[:, d, 0:TH], in0=ps[:, b, 0:TH], scalar=gate, in1=xT[:, d, 0:TH],
                                         op0=ALU.mult, op1=ALU.add)
                eng.scalar_tensor_tensor(out=xT[:, d, TH:NPR], in0=ps[:, b + 1, 0:NPR - TH], scalar=gate,
                                         in1=xT[:, d, TH:NPR], op0=ALU.mult, op1=ALU.add)
                if d >= 1:
                    eng.wait_ge(sem("step_res"), st * DB + d)
                gs = tmp[:, 2, 0:NSM].rearrange("p (b s) -> p b s", s=NS)
                eng.tensor_tensor(gs, ps[:, b + 1, NPR - TH:TH].rearrange("p (b s) -> p b s", s=NS),
                                  modT[:, i_gate, d, 1:NC_].unsqueeze(2).to_broadcast([P, NB, NS]),
                                  ALU.mult).then_inc(sem("step_gs"), 1)
                eng.wait_ge(sem("step_gs"), st * DB + d + 1)
                eng.tensor_tensor(xT[:, d, NPR:T], xT[:, d, NPR:T], tmp[:, 2, 0:NSM],
                                  ALU.add).then_inc(sem("step_res"), 1)
                if n_half == 2 and 2 * d + 3 < n:
                    split_lo(ph, 2 * d + 3, 1)
                if n_half == 1 and d + 2 < n:
                    split_lo(ph, d + 2, d % 2)
            eng.wait_ge(sem("step_mean"), st + 1)
            halves = lambda ap: ap.rearrange("p (h t) -> p h t", h=2)
            for d in range(DB):
                eng.tensor_tensor(halves(xT[:, d, :]), halves(xT[:, d, :]), ps[:, 4:6, 0:TH],
                                  ALU.subtract).then_inc(sem("step_cen"), 1)
            eng.wait_ge(sem("step_var"), st * DB + DB)
            eng.tensor_scalar(halves(tmp[:, 2, :]), ps[:, 6:8, 0:TH], LN_EPS, None, ALU.add).then_inc(sem("step_ve"), 1)
            eng.wait_ge(sem("step_std"), st + 1)
            eng.reciprocal(tmp[:, 3, :], tmp[:, 3, :]).then_inc(sem("step_rs"), 1)
            eng.wait_ge(sem("step_rs"), st + 1)
            for d in range(DB):
                eng.tensor_tensor(xT[:, d, :], xT[:, d, :], tmp[:, 3, :], ALU.mult).then_inc(sem("step_nrm"), 1)

        def project_scalar(st, ph, n_half, i_ln):
            eng = nc.scalar
            for c in range(DB * n_half):
                split_hi(ph, c, c % 2)
            for d in range(DB):
                eng.wait_ge(sem("step_cen"), st * DB + d + 1)
                if d >= 2:
                    eng.wait_ge(sem("step_var"), st * DB + d - 1)
                eng.activation(tmp[:, d % 2, :], xT[:, d, :], ACT.Square).then_inc(sem("step_sq"), 1)
            eng.wait_ge(sem("step_ve"), st + 1)
            eng.activation(tmp[:, 3, :], tmp[:, 2, :], ACT.Sqrt).then_inc(sem("step_std"), 1)
            for d in range(DB):
                eng.wait_ge(sem("step_nrm"), st * DB + d + 1)
                g = colT[:, 72 + i_ln * DB + d:73 + i_ln * DB + d]
                b = colT[:, 96 + i_ln * DB + d:97 + i_ln * DB + d]
                eng.activation(xT[:, d, :], xT[:, d, :], ACT.Identity, bias=b, scale=g).then_inc(sem("step_x"), 1)

        def ffn_in_tensor(st, ffn, ph):
            pe = nc.tensor
            pe.wait_ge(sem("step_hlo"), st * DB + DB)
            def body(j, par):
                for gu in range(2):
                    if not (isinstance(j, int) and j < 2):
                        pe.wait_ge(sem("ffn_mul" if gu else "ffn_silu"), ffn * FB + j - 1)
                    pe.wait_ge(ph.lo, ph.base + 2 * j + gu + 1)
                    chunk_products(ph, gu, DB, hhi, hlo, 0, DB, 4 * par + 2 * gu)
            pairs(pe, FB, body)

        def ffn_in_scalar(st, ffn, ph):
            eng = nc.scalar
            split_hi(ph, 0, 0)
            split_hi(ph, 1, 1)
            def body(j, par):
                last = isinstance(j, int) and j == FB - 1
                if not last:
                    split_hi(ph, 2 * j + 2, 0)
                eng.wait_ge(ph.used, ph.base + 2 * j + 1)
                if not (isinstance(j, int) and j < 2):
                    eng.wait_ge(sem("ffn_mul"), ffn * FB + j - 1)
                eng.activation(tmp[:, par, :].rearrange("p (h t) -> p h t", h=2), ps[:, 4 * par:4 * par + 2, 0:TH],
                               ACT.Silu).then_inc(sem("ffn_silu"), 1)
                if not last:
                    split_hi(ph, 2 * j + 3, 1)
                eng.wait_ge(sem("ffn_mul"), ffn * FB + j + 1)
                eng.activation(ffhi[:, ds(j, 1), :].rearrange("p a t -> p (a t)"), tmp[:, 2 + par, :],
                               ACT.Copy).then_inc(sem("ffn_ffhi"), 1)
            pairs(eng, FB, body, tail=1)

        def ffn_in_vector(st, ffn, ph):
            eng = nc.vector
            split_lo(ph, 0, 0)
            split_lo(ph, 1, 1)
            def body(j, par):
                last = isinstance(j, int) and j == FB - 1
                if not last:
                    split_lo(ph, 2 * j + 2, 0)
                eng.wait_ge(ph.used, ph.base + 2 * j + 2)
                eng.wait_ge(sem("ffn_silu"), ffn * FB + j + 1)
                if not (isinstance(j, int) and j < 2):
                    eng.wait_ge(sem("ffn_fflo"), ffn * FB + j - 1)
                half = lambda ap: ap.rearrange("p (h t) -> p h t", h=2)
                eng.tensor_tensor(half(tmp[:, 2 + par, :]), half(tmp[:, par, :]), ps[:, 4 * par + 2:4 * par + 4, 0:TH],
                                  ALU.mult).then_inc(sem("ffn_mul"), 1)
                if not last:
                    split_lo(ph, 2 * j + 3, 1)
                eng.wait_ge(sem("ffn_ffhi"), ffn * FB + j + 1)
                eng.tensor_tensor(fflo[:, ds(j, 1), :].rearrange("p a t -> p (a t)"), tmp[:, 2 + par, :],
                                  ffhi[:, ds(j, 1), :].rearrange("p a t -> p (a t)").bitcast(F32),
                                  ALU.subtract).then_inc(sem("ffn_fflo"), 1)
            pairs(eng, FB, body, tail=1)

        def ffn_loads(ph_in, ph_out, w_in, w_out):
            eng = nc.sync
            wi = w_in.rearrange("l (k p) n -> p (l k) n", p=P)
            wo_ = w_out.rearrange("l (k p) n -> p (l k) n", p=P)
            def body(j, par):
                for gu in range(2):
                    load_chunk(ph_in, 2 * j + gu, gu, wi[:, :, ds(j * P + gu * FF, P)], DB)
            pairs(eng, FB, body)
            for d in range(DB):
                for hh in range(2):
                    load_chunk(ph_out, 2 * d + hh, hh, wo_[:, hh * HB:(hh + 1) * HB, d * P:(d + 1) * P], HB)

        def start_sync():
            eng = nc.sync
            eng.dma_start(ctok[0:1, :], c_prompt).then_inc(sem("c_landed"), 16)
            eng.dma_start(ctok[1:NC_, :], c_sample).then_inc(sem("c_landed"), 16)
            eng.dma_start(ident[:], ident_d).then_inc(sem("ident_landed"), 16)
            eng.dma_start(rows[0:72, :], b_ada.rearrange("l (r c) -> (l r) c", c=P)).then_inc(sem("rows_landed"), 16)
            eng.dma_start(rows[72:96, :], ln_g.rearrange("l i (r c) -> (l i r) c", c=P)).then_inc(sem("rows_landed"), 16)
            eng.dma_start(rows[96:120, :], ln_b.rearrange("l i (r c) -> (l i r) c", c=P)).then_inc(sem("rows_landed"), 16)
            eng.dma_start(rows[120:121, :], subln_g).then_inc(sem("rows_landed"), 16)
            wa = w_ada.rearrange("l (k p) n -> p (l k) n", p=P)
            for i in range(NM):
                for kh in range(2):
                    n = 2 * i + kh
                    if n >= 4:
                        eng.wait_ge(sem("ada_used"), n - 3)
                    eng.dma_start(wada[:, n % 4], wa[:, kh * 4:kh * 4 + 4, i * D:(i + 1) * D]).then_inc(sem(f"ada_landed{n % 4}"), 16)
                if i == 1:
                    eng.dma_start(xtok[:, 0:PT_, :], x_prompt.rearrange("b (t p) d -> p (b t) d", p=P)).then_inc(sem("x_landed"), 16)
                    eng.dma_start(xtok[0:NSM, PT_, :], x_sample.rearrange("b s d -> (b s) d")).then_inc(sem("x_landed"), 16)
                    eng.dma_start(lamb[:].rearrange("p a b -> p (a b)"),
                                  diff_lambda.rearrange("l a e -> l (a e)").to_broadcast([P, 4 * E])).then_inc(sem("lam_landed"), 16)
                    eng.dma_start(pages[:], page_table.rearrange("b n -> (b n)").unsqueeze(0)).then_inc(sem("pages"), 16)

        def start_pool():
            eng = nc.gpsimd
            eng.memset(cT[:], 0.0).then_inc(sem("pool_set"), 1)
            eng.memset(one_d[:], 1.0 / D).then_inc(sem("pool_set"), 1)
            eng.memset(one_v[:], 1.0 / P).then_inc(sem("pool_set"), 1)

        def start_tensor():
            pe = nc.tensor
            pe.wait_ge(sem("ident_landed"), 16)
            pe.wait_ge(sem("csil"), 1)
            for k in range(DB):
                m = pe.transpose(ps[:, 0, k * 16:k * 16 + NC_], csil[:, k * P:(k + 1) * P], ident[0:NC_, 0:NC_])
            m.then_inc(sem("c_turned"), 1)
            pe.wait_ge(sem("rows_landed"), 64)
            pe.transpose(ps[:, 7, 0:121], rows[0:121, :], ident[0:121, 0:121]).then_inc(sem("rows_turned"), 1)
            pe.wait_ge(sem("cT"), 1)

            def turn_x(k):
                if k >= 2:
                    pe.wait_ge(sem("x_copied"), k - 1)
                for t in range(PT_):
                    m = pe.transpose(ps[:, 4 + k % 2, t * P:(t + 1) * P], xtok[:, t, k * P:(k + 1) * P], ident[:])
                m.then_inc(sem("x_turned"), 1)

            for i in range(NM):
                if i >= 2:
                    pe.wait_ge(sem("mod_row"), i - 1)
                for k in range(DB):
                    if k % 4 == 0:
                        n = 2 * i + k // 4
                        pe.wait_ge(sem(f"ada_landed{n % 4}"), 16 * (n // 4 + 1))
                    for j in range(4):
                        m = pe.matmul(ps[32 * j:32 * j + 32, i % 2, 0:256], cT[:, k, :],
                                      wada[:, n % 4, k % 4, j * 256:(j + 1) * 256], start=(k == 0), stop=(k == DB - 1),
                                      tile_position=(0, 32 * j))
                    if k % 4 == 3:
                        m.then_inc(sem("ada_used"), 1)
                if i == 1:
                    pe.wait_ge(sem("x_landed"), 32)
                if 1 <= i:
                    turn_x(i - 1)
                if i == 1:
                    for k in range(DB):
                        m = pe.transpose(ps[:, 6, k * NSM:(k + 1) * NSM], xtok[0:NSM, PT_, k * P:(k + 1) * P], ident[0:NSM, 0:NSM])
                    m.then_inc(sem("xs_turned"), 1)
                pe.wait_ge(sem("mod_row"), i + 1)
                if i >= 2:
                    pe.wait_ge(sem("mod_bias"), i - 1)
                for h in range(2):
                    m = pe.transpose(ps[:, 2 + i % 2, h * P:(h + 1) * P], modrow[:, i % 2, h * P:(h + 1) * P], ident[:])
                m.then_inc(sem("mod_turned"), 1)

        def start_scalar():
            eng = nc.scalar
            eng.wait_ge(sem("c_landed"), 32)
            eng.activation(csil[:], ctok[:], ACT.Silu).then_inc(sem("csil"), 1)
            eng.wait_ge(sem("pool_set"), 1)
            eng.wait_ge(sem("c_turned"), 1)
            eng.activation(cT[:, :, 0:NC_], ps[:, 0, 0:DB * 16].rearrange("p (k c) -> p k c", c=16)[:, :, 0:NC_],
                           ACT.Copy).then_inc(sem("cT"), 1)
            eng.wait_ge(sem("lam_dots"), 1)
            eng.activation(stat[:, 0:2], stat[:, 0:2], ACT.Exp).then_inc(sem("lam_exp"), 1)
            for i in range(NM):
                eng.wait_ge(sem("ada_used"), 2 * i + 2)
                if i >= 2:
                    eng.wait_ge(sem("mod_turned"), i - 1)
                eng.activation(modrow[:, i % 2, :], ps[:, i % 2, 0:256], ACT.Copy).then_inc(sem("mod_row"), 1)
                if i >= 1:
                    k = i - 1
                    eng.wait_ge(sem("x_turned"), k + 1)
                    eng.activation(xT[:, k, 0:NPR], ps[:, 4 + k % 2, :], ACT.Copy).then_inc(sem("x_copied"), 1)

        def start_vector():
            eng = nc.vector
            eng.wait_ge(sem("lam_landed"), 16)
            l4 = lamb[:].rearrange("p (a b) e -> p a b e", b=2)
            eng.tensor_tensor(lamp[:], l4[:, :, 0, :], l4[:, :, 1, :], ALU.mult).then_inc(sem("lam_mul"), 1)
            eng.wait_ge(sem("lam_mul"), 1)
            eng.reduce_sum(stat[:, 0:2], lamp[:], AX_X).then_inc(sem("lam_dots"), 1)
            eng.wait_ge(sem("rows_turned"), 1)
            eng.tensor_copy(colT[:, 0:121], ps[:, 7, 0:121]).then_inc(sem("cols"), 1)
            eng.wait_ge(sem("cols"), 1)
            eng.wait_ge(sem("xs_turned"), 1)
            eng.tensor_copy(xT[:, :, NPR:T], ps[:, 6, :].rearrange("p (k s) -> p k s", s=NSM)).then_inc(sem("xs_copied"), 1)
            eng.wait_ge(sem("lam_exp"), 1)
            eng.tensor_tensor(stat[:, 2:3], stat[:, 1:2], stat[:, 0:1], ALU.subtract).then_inc(sem("lam_sub"), 1)
            eng.wait_ge(sem("lam_sub"), 1)
            eng.tensor_scalar(stat[:, 3:4], stat[:, 2:3], -LAM_INIT, None, ALU.add).then_inc(sem("lam"), 1)
            eng.tensor_scalar(stat[:, 4:5], colT[:, 120:121], 1.0 - LAM_INIT, None, ALU.mult).then_inc(sem("lam"), 1)
            for i in range(NM):
                eng.wait_ge(sem("mod_turned"), i + 1)
                src = ps[:, 2 + i % 2, 0:256].rearrange("p (h j c) -> p j h c", h=2, j=4)[:, :, :, 0:NC_]
                dst = modT[:, i, :, :].rearrange("p (j h) c -> p j h c", h=2)
                b = colT[:, i * DB:(i + 1) * DB].rearrange("p (j h) -> p j h", h=2).unsqueeze(3).to_broadcast([P, 4, 2, NC_])
                eng.tensor_tensor(dst, src, b, ALU.add).then_inc(sem("mod_bias"), 1)
                eng.wait_ge(sem("mod_bias"), i + 1)
                a, m = {0: (0.0, 1.0), 1: (1.0, 1.0), 2: (0.0, (0.5, 1.0, 0.5)[i // 3])}[i % 3]
                eng.tensor_scalar(modT[:, i, :, :], modT[:, i, :, :], a, m, ALU.add, ALU.mult).then_inc(sem("mods"), 1)
            eng.wait_ge(sem("mods"), NM)

        ROTS = (0, 1, 3, 4)
        VS = (2, 5)

        def qkv_bank(g, t):
            return (5 * g + t) % 6

        def tokens(t):
            return P if t < PT_ else NSM

        def qkv_sync():
            eng = nc.sync
            w = w_qkv.rearrange("l (k p) n -> p (l k) n", p=P)
            outs = {1: (wkp, wks), 2: (wvp, wvs), 4: (dkp, dks), 5: (dvp, dvs)}
            def flat(ap):
                names = "abcdefg"[:len(ap.shape)]
                lead = names[:-2] if ap is not dkp and ap is not dks else names[:-3]
                rest = names[len(lead):]
                return ap.rearrange(f"{' '.join(names)} -> ({' '.join(lead)}) ({' '.join(rest)})")
            def store(g):
                op, os_ = (flat(a) for a in outs[g])
                ready = "rot" if g in ROTS else "vout"
                base = (ROTS if g in ROTS else VS).index(g) * (PT_ + 1)
                for t in range(PT_ + 1):
                    eng.wait_ge(sem(ready), (base + t + 1) * (2 if g in ROTS else 1))
                    n = tokens(t)
                    src = rot[0:n, t, :] if g in ROTS else V[0:n, VS.index(g), t, :]
                    dst = op[t * P:(t + 1) * P, :] if t < PT_ else os_
                    eng.dma_start(dst, src).then_inc(sem(f"kept{g}"), 16)
            for g in range(6):
                for c in range(4):
                    load_chunk(qkv, 4 * g + c, c % 2, w[:, 2 * c:2 * c + 2, g * QW:(g + 1) * QW], 2)
                if g == 0:
                    eng.wait_ge(out1.used, 2 * DB)
                    eng.dma_start(ropet[:].rearrange("p a b c -> p (a b c)"), rope_d).then_inc(sem("tables"), 16)
                    eng.dma_start(mask_a[:], mask_a_d).then_inc(sem("tables"), 16)
                    eng.dma_start(mask_b[:], mask_b_d).then_inc(sem("tables"), 16)
                    eng.dma_start(past_a[:], past_a_d).then_inc(sem("tables"), 16)
                if g - 1 in outs:
                    store(g - 1)
            store(5)

        def turn_rot(g, t):
            pe = nc.tensor
            r = ROTS.index(g) * (PT_ + 1) + t
            pe.wait_ge(sem("rot"), 2 * r + 2)
            if r >= 2:
                pe.wait_ge(sem("qk_copied"), r - 1)
            n = tokens(t)
            for f in range(4):
                m = pe.transpose(ps[:, 6 + r % 2, f * P:f * P + n], rot[0:n, t, f * P:(f + 1) * P], ident[0:n, 0:n])
            m.then_inc(sem("qk_turned"), 1)

        def tile_summed(eng, g, t):
            if t < PT_:
                eng.wait_ge(sem("qkv_sum"), PT_ * g + t + 1)
            else:
                eng.wait_ge(qkv.used, 4 * g + 4)

        def qkv_tensor():
            pe = nc.tensor
            pe.wait_ge(sem("step_hlo"), 1 * DB + DB)
            for g in range(7):
                for c in range(4):
                    if g < 6:
                        slot = c % 2
                        pe.wait_ge(qkv.lo, 4 * g + c + 1)
                        for t in range(PT_ + 1):
                            n = tokens(t)
                            if c == 0 and 5 * g + t >= 6:
                                g0, t0 = divmod(5 * g + t - 6, 5)
                                if g0 in ROTS:
                                    pe.wait_ge(sem("qkv_read"), ROTS.index(g0) * (PT_ + 1) + t0 + 1)
                                else:
                                    pe.wait_ge(sem("vout"), VS.index(g0) * (PT_ + 1) + t0 + 1)
                            for k in range(2):
                                kk = 2 * c + k
                                wh = whi[:, slot, k * QW:(k + 1) * QW]
                                wl = wlo[:, slot, k * QW:(k + 1) * QW]
                                for x, w, n3 in ((hhi, wh, 0), (hlo, wh, 1), (hhi, wl, 2)):
                                    m = pe.matmul(ps[0:n, qkv_bank(g, t), :], x[:, kk, t * P:t * P + n], w,
                                                  start=(kk == 0 and n3 == 0), stop=(kk == DB - 1 and n3 == 2))
                            if c == 3 and t < PT_:
                                m.then_inc(sem("qkv_sum"), 1)
                        m.then_inc(qkv.used, 1)
                    if g - 1 in ROTS and c in (1, 2):
                        for t in ((0, 1, 2), (3, 4))[c - 1]:
                            turn_rot(g - 1, t)

        def qkv_scalar():
            eng = nc.scalar
            def copy_turned(g, t):
                r = ROTS.index(g) * (PT_ + 1) + t
                eng.wait_ge(sem("qk_turned"), r + 1)
                n = tokens(t)
                dst = (QT if g in (0, 3) else KT)[:, 4 * (g // 3):4 * (g // 3) + 4, t * P:t * P + n]
                src = ps[:, 6 + r % 2, :].rearrange("p (f t) -> p f t", f=4)[:, :, 0:n]
                eng.activation(dst, src, ACT.Copy, scale=(SCALE if g in (0, 3) else 1.0)).then_inc(sem("qk_copied"), 1)
            def copy_v(g, t):
                n = tokens(t)
                tile_summed(eng, g, t)
                eng.activation(V[0:n, VS.index(g), t, :], ps[0:n, qkv_bank(g, t), :], ACT.Copy).then_inc(sem("vout"), 1)
            for g in range(6):
                if g - 1 in VS:
                    for t in range(PT_ + 1):
                        copy_v(g - 1, t)
                for c in range(4):
                    split_hi(qkv, 4 * g + c, c % 2)
                    if g - 1 in ROTS and c == 3:
                        for t in range(PT_ + 1):
                            copy_turned(g - 1, t)
            for t in range(PT_ + 1):
                copy_v(5, t)

        def qkv_vector():
            eng = nc.vector
            def rotate(g, t):
                r = ROTS.index(g) * (PT_ + 1) + t
                n = tokens(t)
                tile_summed(eng, g, t)
                if r >= 1:
                    eng.wait_ge(sem("rot"), 2 * r)
                src = ps[0:n, qkv_bank(g, t), :].rearrange("p (h e) -> p h e", e=E // 2)
                tab = lambda i: ropet[0:n, t, i, :].unsqueeze(1).to_broadcast([n, 2 * 8, E // 2])
                half = lambda i: rab[0:n, i, :].rearrange("p (h e) -> p h e", e=E // 2)
                eng.tensor_tensor(half(0), src, tab(0), ALU.mult).then_inc(sem("rope_cos"), 1)
                eng.tensor_tensor(half(1), src, tab(1), ALU.mult).then_inc(sem("qkv_read"), 1)
                eng.wait_ge(sem("rope_cos"), r + 1)
                eng.wait_ge(sem("qkv_read"), r + 1)
                if r >= 5:
                    g0 = ROTS[ROTS.index(g) - 1]
                    eng.wait_ge(sem("qk_turned"), r - 4)
                    if g0 in (1, 4):
                        eng.wait_ge(sem(f"kept{g0}"), 16 * (PT_ + 1))
                q = lambda i: rab[0:n, i, :].rearrange("p (h two e) -> p h two e", two=2, e=E // 2)
                o = rot[0:n, t, :].rearrange("p (h two e) -> p h two e", two=2, e=E // 2)
                eng.tensor_tensor(o[:, :, 0, :], q(0)[:, :, 0, :], q(1)[:, :, 1, :], ALU.subtract).then_inc(sem("rot"), 1)
                eng.tensor_tensor(o[:, :, 1, :], q(0)[:, :, 1, :], q(1)[:, :, 0, :], ALU.add).then_inc(sem("rot"), 1)
            for g in range(6):
                for c in range(4):
                    split_lo(qkv, 4 * g + c, c % 2)
                    if g == 1 and c == 0:
                        eng.wait_ge(sem("tables"), 4 * 16)
                    if g - 1 in ROTS and c < 2:
                        for t in ((0, 1, 2, 3), (4,))[c]:
                            rotate(g - 1, t)

        STEPS = [(f, h, q) for f in range(4) for h in range(2) for q in range(PT_)]
        STEPS += [(f, h, q) for f in range(4, 8) for q in range(PT_) for h in range(2)]
        TURNS = [n for n, (f, h, q) in enumerate(STEPS) if f < 4 or h == 1]
        TURN_OF = {n: sum(m < n for m in TURNS) for n in range(len(STEPS))}
        HEADS = [(f, h) for f in range(4) for h in range(2)] + [(f, None) for f in range(4, 8)]

        def prob(n, w):
            return S[:, n % 4 * NPR:n % 4 * NPR + w]

        def turned(hd):
            return PTp if hd % 2 == 0 else KC

        def prompt_tensor():
            pe = nc.tensor
            pe.wait_ge(sem("qk_copied"), 4 * (PT_ + 1))
            pe.wait_ge(sem("vout"), 2 * (PT_ + 1))

            def score(n):
                f, h, q = STEPS[n]
                r = slice(h * E, (h + 1) * E)
                w = (q + 1) * P
                if n >= 2:
                    pe.wait_ge(sem("p_max"), n - 1)
                pe.matmul(ps[:, n % 2, 0:w], QT[r, f, q * P:(q + 1) * P], KT[r, f, 0:w], start=True,
                          stop=True).then_inc(sem("p_score"), 1)

            def turn(n):
                f, h, q = STEPS[n]
                r = TURN_OF[n]
                pe.wait_ge(sem("p_norm"), r + 1)
                if r >= 2:
                    pe.wait_ge(sem("p_copied"), r - 1)
                src = n if f < 4 else n - 1
                for kt in range(q + 1):
                    m = pe.transpose(ps[:, 2 + r % 2, kt * P:(kt + 1) * P], S[:, src % 4 * NPR + kt * P:src % 4 * NPR + (kt + 1) * P],
                                     ident[:])
                m.then_inc(sem("p_turn"), 1)

            def values(hd):
                f, h = HEADS[hd]
                pe.wait_ge(sem("p_copied"), PT_ * (hd + 1))
                if hd >= 2:
                    pe.wait_ge(sem("p_out"), hd - 1)
                for kt in range(PT_):
                    if h is None:
                        out, v = ps[:, 4 + hd % 2, kt * P:NPR], V[:, 1, kt, (f - 4) * P:(f - 3) * P]
                    else:
                        out = ps[h * E:(h + 1) * E, 4 + hd % 2, kt * P:NPR]
                        v = V[:, 0, kt, f * P + h * E:f * P + (h + 1) * E]
                    m = pe.matmul(out, v, turned(hd)[:, kt, kt * P:NPR], start=(kt == 0), stop=(kt == PT_ - 1),
                                  skip_group_check=True)
                m.then_inc(sem("p_pv"), 1)

            done = 0
            for n in range(len(STEPS) + 4):
                if n < len(STEPS):
                    score(n)
                if 2 <= n < len(STEPS) + 2 and n - 2 in TURNS:
                    turn(n - 2)
                if n >= 4 and done < len(HEADS) and TURNS[PT_ * done + PT_ - 1] == n - 4:
                    values(done)
                    done += 1

        def prompt_vector():
            eng = nc.vector
            col = lambda k, n: stat[:, k + n % 4:k + n % 4 + 1]

            def top(n):
                f, h, q = STEPS[n]
                w = (q + 1) * P
                mask = (mask_a if f < 4 else mask_b)[:, NPR - w:NPR]
                eng.wait_ge(sem("p_score"), n + 1)
                if n >= 4:
                    eng.wait_ge(sem("p_turn"), TURN_OF[n - 4] + 1)
                if n >= 1:
                    eng.wait_ge(sem("p_neg"), n)
                eng.tensor_tensor_reduce(out=prob(n, w), in0=ps[:, n % 2, 0:w], in1=mask, scale=1.0, scalar=MASKED,
                                         op0=ALU.add, op1=ALU.max, accum_out=col(8, n)).then_inc(sem("p_max"), 1)
                eng.wait_ge(sem("p_max"), n + 1)
                eng.tensor_scalar(col(12, n), col(8, n), -1.0, None, ALU.mult).then_inc(sem("p_neg"), 1)

            def norm(n):
                f, h, q = STEPS[n]
                w = (q + 1) * P
                eng.wait_ge(sem("p_exp"), n + 1)
                eng.reciprocal(col(20, n), col(16, n)).then_inc(sem("p_rl"), 1)
                eng.wait_ge(sem("p_rl"), n + 1)
                if f < 4:
                    eng.tensor_scalar(prob(n, w), prob(n, w), col(20, n), None, ALU.mult).then_inc(sem("p_norm"), 1)
                elif h == 1:
                    k = (n - 4 * 2 * PT_) // 2
                    eng.tensor_scalar(prob(n, w), prob(n, w), col(20, n), stat[:, 3:4], ALU.mult,
                                      ALU.mult).then_inc(sem("p_second"), 1)
                    eng.wait_ge(sem("p_second"), k + 1)
                    eng.scalar_tensor_tensor(out=prob(n - 1, w), in0=prob(n - 1, w), scalar=col(20, n - 1), in1=prob(n, w),
                                             op0=ALU.mult, op1=ALU.add).then_inc(sem("p_norm"), 1)

            def out(hd):
                f, h = HEADS[hd]
                r = slice(0, P) if h is None else slice(h * E, (h + 1) * E)
                eng.wait_ge(sem("p_pv"), hd + 1)
                eng.tensor_copy(QT[r, f, 0:NPR], ps[r, 4 + hd % 2, :]).then_inc(sem("p_out"), 1)

            done = 0
            for n in range(len(STEPS) + 6):
                if n < len(STEPS):
                    top(n)
                if 1 <= n <= len(STEPS):
                    norm(n - 1)
                if n >= 6 and done < len(HEADS) and TURNS[PT_ * done + PT_ - 1] <= n - 6:
                    out(done)
                    done += 1
            while done < len(HEADS):
                out(done)
                done += 1

        def prompt_scalar():
            eng = nc.scalar
            col = lambda k, n: stat[:, k + n % 4:k + n % 4 + 1]

            def exp(n):
                w = (STEPS[n][2] + 1) * P
                eng.wait_ge(sem("p_neg"), n + 1)
                eng.activation(prob(n, w), prob(n, w), ACT.Exp, bias=col(12, n), scale=1.0,
                               accum_out=col(16, n)).then_inc(sem("p_exp"), 1)

            def copy(n):
                r = TURN_OF[n]
                hd, q = r // PT_, r % PT_
                eng.wait_ge(sem("p_turn"), r + 1)
                if hd >= 2:
                    eng.wait_ge(sem("p_pv"), hd - 1)
                src = ps[:, 2 + r % 2, 0:(q + 1) * P].rearrange("p (k t) -> p k t", t=P)
                eng.activation(turned(hd)[:, 0:q + 1, q * P:(q + 1) * P], src, ACT.Copy).then_inc(sem("p_copied"), 1)

            for g in (1, 4):
                eng.wait_ge(sem(f"kept{g}"), 16 * (PT_ + 1))
            for n in range(len(STEPS) + 3):
                if n < len(STEPS):
                    exp(n)
                if 2 <= n and n - 3 in TURNS:
                    copy(n - 3)

        CH = (A_CHUNKS, B_CHUNKS)
        WID = (A_KEYS, PAST)
        GRP = ([(0, 4), None, (4, 4), (8, 4)], [(0, 4), None, (4, 4), (8, 4), (12, 4)])
        G = (len(GRP[0]), len(GRP[1]))
        GALL = sum(G)
        DMAS = ((1, 1, 1, 1), (4, 4, 4, 4))
        PER_SLOT = [16 * 2 * (DMAS[0][c] + DMAS[1][c]) for c in range(4)]

        def keys_of(m, tile):
            return FARW if m == 0 and tile < A_FAR else P

        def key0(m, tile):
            return tile * P if m else min(tile, A_FAR) * FARW + max(tile - A_FAR, 0) * P

        def tile0(m, c):
            return sum(CH[m][:c])

        def chunk_keys(m, c):
            return CH[m][c] * keys_of(m, tile0(m, c))

        def landed_at(m, is_v, c):
            return 16 * (2 * DMAS[0][c] * m + DMAS[m][c] * (1 + is_v))

        def positive(n):
            return not isinstance(n, int) or n > 0

        def over_sequences(eng, body):
            body(0)
            with eng.Fori(1, NB) as b:
                body(b)

        def decode_sync():
            eng = nc.sync
            far = [w[:, :, 0:PAST - DENSE].rearrange("l b (g j) h e -> (l b) g j (h e)", j=16) for w in (win_k, win_v)]
            near = [w[:, :, PAST - DENSE:PAST].rearrange("l b (p t) h e -> (l b) p t (h e)", t=A_NEAR) for w in (win_k, win_v)]
            pool = [diff_k.rearrange("l n p h c e -> (l n) p (h c e)"), diff_v.rearrange("l n p h v -> (l n) p (h v)")]

            def body(b):
                for m in range(2):
                    for is_v in range(2):
                        tile = 0
                        for c in range(4):
                            n = CH[m][c]
                            if m == 1:
                                page = [eng.value_load(pages[0:1, ds(b * NPAGE + tile + i, 1)], min_val=0,
                                                       max_val=diff_k.shape[1] - 1) for i in range(n)]
                            if is_v:
                                eng.wait_ge(sem("d_kt"), 8 * b + 4 * m + c + 1)
                            else:
                                if positive(8 * b + 4 * m + c - 3):
                                    eng.wait_ge(sem("d_pv"), 8 * b + 4 * m + c - 3)
                            s = sem(f"kv_landed{c}")
                            if m == 0 and tile < A_FAR:
                                src = far[is_v][ds(b, 1), :, tile:tile + n, :].rearrange("a g j c -> (a g) j c")
                                eng.dma_start(kv(c)[0:FARW, 0:n, :], src).then_inc(s, 16)
                            elif m == 0:
                                t0 = tile - A_FAR
                                src = near[is_v][ds(b, 1), :, t0:t0 + n, :].rearrange("a p t c -> (a p) t c")
                                eng.dma_start(kv(c)[:, 0:n, :], src).then_inc(s, 16)
                            else:
                                for i in range(n):
                                    src = pool[is_v][ds(page[i], 1), :, :].rearrange("a p c -> (a p) c")
                                    eng.dma_start(kv(c)[:, i, :], src).then_inc(s, 16)
                            tile += n
            eng.wait_ge(qkv.used, 24)
            eng.wait_ge(sem("pages"), 16)
            eng.wait_ge(sem("qk_turned"), 4 * (PT_ + 1))
            eng.wait_ge(sem("kept1"), 16 * (PT_ + 1))
            eng.wait_ge(sem("kept4"), 16 * (PT_ + 1))
            eng.dma_start(new_ab[:].rearrange("p a b c -> p (a b c)"), new_ab_d).then_inc(sem("new_masks"), 16)
            over_sequences(eng, body)

        def decode_pool():
            eng = nc.gpsimd
            eng.memset(QB[:], 0.0).then_inc(sem("d_zero"), 1)
            eng.wait_ge(sem("d_zero"), 1)
            eng.wait_ge(sem("qk_copied"), 4 * (PT_ + 1))

            def body(b):
                for m in range(2):
                    if positive(10 * b + 5 * m - 5):
                        eng.wait_ge(sem("d_sc"), 10 * b + 5 * m - 5)
                    for h in range(2):
                        r = slice(h * E, (h + 1) * E)
                        eng.tensor_copy(QB[r, m, :, h * NS:(h + 1) * NS],
                                        QT[r, 4 * m:4 * m + 4, ds(b * NS + NPR, NS)]).then_inc(sem("d_qb"), 1)
            over_sequences(eng, body)

        def decode_tensor():
            pe = nc.tensor

            def body(b):
                for m in range(2):
                    def turn(c):
                        nt, kw = CH[m][c], keys_of(m, tile0(m, c))
                        pe.wait_ge(sem(f"kv_landed{c}"), PER_SLOT[c] * b + landed_at(m, 0, c))
                        if positive(16 * b + 8 * m + 2 * c):
                            pe.wait_ge(sem("d_kca"), 16 * b + 8 * m + 2 * c)
                        if positive(16 * b + 8 * m + 2 * c):
                            pe.wait_ge(sem("d_kcv"), 16 * b + 8 * m + 2 * c)
                        for f in range(4):
                            for i in range(nt):
                                mm = pe.transpose(ps[:, f, i * kw:(i + 1) * kw], kv(c)[0:kw, i, f * P:(f + 1) * P], ident[0:kw, 0:kw])
                            if f == 3:
                                mm.then_inc(sem("d_kt"), 1)

                    def scores(c):
                        w = NSM if c < 0 else chunk_keys(m, c)
                        if c >= 0:
                            pe.wait_ge(sem("d_kca"), 16 * b + 8 * m + 2 * c + 2)
                            pe.wait_ge(sem("d_kcv"), 16 * b + 8 * m + 2 * c + 2)
                        if positive(10 * b + 5 * m + c + 1):
                            pe.wait_ge(sem("d_smax"), 10 * b + 5 * m + c + 1)
                        for f in range(4):
                            rhs = KT[:, 4 * m + f, NPR:T] if c < 0 else KC[:, f, 0:w]
                            mm = pe.matmul(ps[32 * f:32 * f + 32, 4, 0:w], QB[:, m, f, :], rhs, start=True, stop=True,
                                           tile_position=(0, 32 * f))
                        mm.then_inc(sem("d_sc"), 1)

                    pe.wait_ge(sem("d_qb"), 4 * b + 2 * m + 2)
                    scores(-1)
                    turn(0)
                    for c in range(4):
                        if c < 3:
                            turn(c + 1)
                        scores(c)
                    g0 = G[0] if m else 0
                    pe.wait_ge(sem("d_exp"), 2 * b + m + 1)
                    if positive(GALL * b + g0):
                        pe.wait_ge(sem("d_ptc"), GALL * b + g0)
                    for g in range(G[m]):
                        if g >= 2:
                            pe.wait_ge(sem("d_ptc"), GALL * b + g0 + g - 1)
                        bank = 6 + (g0 + g) % 2
                        if GRP[m][g] is None:
                            mm = pe.transpose(ps[0:NSM, bank, 0:P], S[:, WID[m]:WID[m] + NSM], ident[:])
                        else:
                            t0, nt = GRP[m][g]
                            kw = keys_of(m, t0)
                            for i in range(nt):
                                o = key0(m, t0 + i)
                                mm = pe.transpose(ps[0:kw, bank, i * P:(i + 1) * P], S[:, o:o + kw], ident[0:P, 0:P])
                        mm.then_inc(sem("d_pt"), 1)
                    if positive(4 * b + 2 * m):
                        pe.wait_ge(sem("d_out"), 4 * b + 2 * m)
                    pe.wait_ge(sem("d_ptc"), GALL * b + g0 + 2)
                    tile = 0
                    for c in range(4):
                        pe.wait_ge(sem(f"kv_landed{c}"), PER_SLOT[c] * b + landed_at(m, 1, c))
                        for i in range(CH[m][c]):
                            for g, grp in enumerate(GRP[m]):
                                if g >= 2 and tile == grp[0]:
                                    pe.wait_ge(sem("d_ptc"), GALL * b + g0 + g + 1)
                            kw = keys_of(m, tile)
                            last = tile == sum(CH[m]) - 1
                            for f in range(4):
                                mm = pe.matmul(ps[32 * f:32 * f + 32, 5, 0:P], PTd[0:kw, tile, 32 * f:32 * f + 32],
                                               kv(c)[0:kw, i, f * P:(f + 1) * P], start=(tile == 0), stop=last,
                                               tile_position=(0, 32 * f), skip_group_check=True)
                            if tile == 0:
                                for f in range(4):
                                    pe.matmul(ps[32 * f:32 * f + 32, 5, 0:P], PTd[0:NSM, NPAGE, 32 * f:32 * f + 32],
                                              V[0:NSM, m, PT_, f * P:(f + 1) * P], start=False, stop=False,
                                              tile_position=(0, 32 * f), skip_group_check=True)
                            tile += 1
                        mm.then_inc(sem("d_pv"), 1)
                    pe.wait_ge(sem("d_on"), 2 * b + m + 1)
                    pe.transpose(ps[:, 5, P:2 * P], On[:], ident[:]).then_inc(sem("d_ot"), 1)
            over_sequences(pe, body)

        def decode_scalar():
            eng = nc.scalar

            def body(b):
                for m in range(2):
                    for c in range(4):
                        w = chunk_keys(m, c)
                        eng.wait_ge(sem("d_kt"), 8 * b + 4 * m + c + 1)
                        eng.wait_ge(sem("d_sc"), 10 * b + 5 * m + c + 1)
                        for f in (0, 2):
                            eng.activation(KC[:, f, 0:w], ps[:, f, 0:w], ACT.Copy).then_inc(sem("d_kca"), 1)
                    eng.wait_ge(sem("d_neg"), 2 * b + m + 1)
                    w = WID[m] + NSM
                    eng.activation(S[:, 0:w], S[:, 0:w], ACT.Exp, bias=stat[:, 41:42], scale=1.0,
                                   accum_out=stat[:, 42:43]).then_inc(sem("d_exp"), 1)
                    for g in range(G[m]):
                        gi = (G[0] if m else 0) + g
                        eng.wait_ge(sem("d_pt"), GALL * b + gi + 1)
                        if positive(8 * b + 4 * m):
                            eng.wait_ge(sem("d_pv"), 8 * b + 4 * m)
                        if GRP[m][g] is None:
                            eng.activation(PTd[0:NSM, NPAGE, :], ps[0:NSM, 6 + gi % 2, 0:P], ACT.Copy).then_inc(sem("d_ptc"), 1)
                        else:
                            t0, nt = GRP[m][g]
                            kw = keys_of(m, t0)
                            eng.activation(PTd[0:kw, t0:t0 + nt, :], ps[0:kw, 6 + gi % 2, 0:nt * P].rearrange("p (t r) -> p t r", r=P),
                                           ACT.Copy).then_inc(sem("d_ptc"), 1)
            over_sequences(eng, body)

        def decode_vector():
            eng = nc.vector
            eng.wait_ge(sem("p_out"), len(HEADS))

            def body(b):
                for m in range(2):
                    def evac(c):
                        w = chunk_keys(m, c)
                        eng.wait_ge(sem("d_kt"), 8 * b + 4 * m + c + 1)
                        eng.wait_ge(sem("d_sc"), 10 * b + 5 * m + c + 1)
                        for f in (1, 3):
                            eng.tensor_copy(KC[:, f, 0:w], ps[:, f, 0:w]).then_inc(sem("d_kcv"), 1)

                    def top(c):
                        w = chunk_keys(m, c)
                        o = key0(m, tile0(m, c))
                        bias = past_a[:, o:o + w] if m == 0 else tmp[:, 0, 0:w]
                        eng.tensor_tensor_reduce(out=S[:, o:o + w], in0=ps[:, 4, 0:w], in1=bias, scale=1.0, scalar=MASKED,
                                                 op0=ALU.add, op1=ALU.max, accum_out=stat[:, 32 + c:33 + c]).then_inc(sem("d_smax"), 1)

                    if positive(GALL * b + (G[0] if m else 0)):
                        eng.wait_ge(sem("d_pt"), GALL * b + (G[0] if m else 0))
                    if positive(2 * b + m):
                        eng.wait_ge(sem("d_neg"), 2 * b + m)
                    eng.wait_ge(sem("d_sc"), 10 * b + 5 * m + 1)
                    o = WID[m]
                    eng.tensor_tensor(S[:, o:o + NSM], ps[:, 4, 0:NSM], new_ab[:, m, ds(b, 1), :].rearrange("p a k -> p (a k)"),
                                      ALU.add).then_inc(sem("d_smax"), 1)
                    evac(0)
                    for c in range(3):
                        evac(c + 1)
                        top(c)
                    eng.wait_ge(sem("d_smax"), 10 * b + 5 * m + 4)
                    eng.wait_ge(sem("d_sc"), 10 * b + 5 * m + 5)
                    eng.reduce_max(stat[:, 36:37], S[:, o:o + NSM], AX_X).then_inc(sem("d_mnew"), 1)
                    top(3)
                    eng.wait_ge(sem("d_smax"), 10 * b + 5 * m + 5)
                    eng.wait_ge(sem("d_mnew"), 2 * b + m + 1)
                    eng.reduce_max(stat[:, 40:41], stat[:, 32:37], AX_X).then_inc(sem("d_mall"), 1)
                    eng.wait_ge(sem("d_mall"), 2 * b + m + 1)
                    eng.tensor_scalar(stat[:, 41:42], stat[:, 40:41], -1.0, None, ALU.mult).then_inc(sem("d_neg"), 1)
                    eng.wait_ge(sem("d_exp"), 2 * b + m + 1)
                    eng.reciprocal(stat[:, 43:44], stat[:, 42:43]).then_inc(sem("d_rl"), 1)
                    eng.wait_ge(sem("d_rl"), 2 * b + m + 1)
                    eng.wait_ge(sem("d_pv"), 8 * b + 4 * m + 4)
                    eng.tensor_scalar(On[:], ps[:, 5, 0:P], stat[:, 43:44], None, ALU.mult).then_inc(sem("d_on"), 1)
                    eng.wait_ge(sem("d_ot"), 2 * b + m + 1)
                    turned_o = ps[:, 5, P:2 * P].rearrange("p (f x) -> p f x", f=4)
                    cols = ds(b * NS + NPR, NS)
                    if m == 0:
                        for h in range(2):
                            r = slice(h * E, (h + 1) * E)
                            eng.tensor_copy(QT[r, 0:4, cols], turned_o[r, :, h * NS:(h + 1) * NS]).then_inc(sem("d_out"), 1)
                    else:
                        part = tmp[:, 1, 0:4 * NS].rearrange("p (f q) -> p f q", f=4)
                        eng.tensor_scalar(part, turned_o[:, :, NS:2 * NS], stat[:, 3:4], None, ALU.mult).then_inc(sem("d_out"), 1)
                        eng.wait_ge(sem("d_out"), 4 * b + 3)
                        eng.tensor_tensor(QT[:, 4:8, cols], part, turned_o[:, :, 0:NS], ALU.add).then_inc(sem("d_out"), 1)
            eng.memset(tmp[:, 0, :], 0.0).then_inc(sem("d_zeros"), 1)
            eng.wait_ge(sem("d_zeros"), 1)
            eng.wait_ge(sem("new_masks"), 16)
            over_sequences(eng, body)

        def mix_tensor():
            pe = nc.tensor
            for i in range(4):
                pe.wait_ge(sem("m_sq"), i + 1)
                for h in range(2):
                    m = pe.matmul(ps[:, 2 * i + h, 0:TH], one_v[:], tmp[:, i % 2, h * TH:(h + 1) * TH], start=True, stop=True)
                m.then_inc(sem("m_mean"), 1)

        def mix_scalar():
            eng = nc.scalar
            eng.wait_ge(sem("d_out"), 4 * NB)
            for i in range(4):
                if i >= 2:
                    eng.wait_ge(sem("m_mean"), i - 1)
                eng.activation(tmp[:, i % 2, :], QT[:, 4 + i, :], ACT.Square).then_inc(sem("m_sq"), 1)
            for i in range(4):
                eng.wait_ge(sem("m_ve"), i + 1)
                eng.activation(tmp[:, 2 + i % 2, :], tmp[:, 2 + i % 2, :], ACT.Sqrt).then_inc(sem("m_std"), 1)
            for d in range(DB):
                if d >= 4:
                    eng.wait_ge(sem("m_rms"), d - 3)
                eng.activation(hhi[:, d, :], QT[:, d, :], ACT.Copy).then_inc(sem("m_hhi"), 1)

        def mix_vector():
            eng = nc.vector
            for i in range(4):
                eng.wait_ge(sem("m_mean"), i + 1)
                if i >= 2:
                    eng.wait_ge(sem("m_rms"), i - 1)
                eng.tensor_scalar(tmp[:, 2 + i % 2, :].rearrange("p (h t) -> p h t", h=2), ps[:, 2 * i:2 * i + 2, 0:TH],
                                  RMS_EPS, None, ALU.add).then_inc(sem("m_ve"), 1)
                eng.wait_ge(sem("m_std"), i + 1)
                eng.reciprocal(tmp[:, 2 + i % 2, :], tmp[:, 2 + i % 2, :]).then_inc(sem("m_rs"), 1)
                eng.wait_ge(sem("m_rs"), i + 1)
                eng.scalar_tensor_tensor(out=QT[:, 4 + i, :], in0=QT[:, 4 + i, :], scalar=stat[:, 4:5], in1=tmp[:, 2 + i % 2, :],
                                         op0=ALU.mult, op1=ALU.mult).then_inc(sem("m_rms"), 1)
            for d in range(DB):
                eng.wait_ge(sem("m_hhi"), d + 1)
                eng.tensor_tensor(hlo[:, d, :], QT[:, d, :], hhi[:, d, :].bitcast(F32), ALU.subtract).then_inc(sem("m_hlo"), 1)

        def end_tensor():
            pe = nc.tensor
            pe.wait_ge(sem("step_x"), 2 * DB + DB)
            for t in range(PT_ + 1):
                n = tokens(t)
                for kg in range(2):
                    i = 2 * t + kg
                    if i >= 8:
                        pe.wait_ge(sem("y_copied"), i - 7)
                    for k in range(4):
                        m = pe.transpose(ps[0:n, i % 8, k * P:(k + 1) * P], xT[:, 4 * kg + k, t * P:t * P + n], ident[:])
                    m.then_inc(sem("y_turned"), 1)

        def end_vector():
            eng = nc.vector
            for i in range(2 * (PT_ + 1)):
                t, kg = divmod(i, 2)
                n = tokens(t)
                eng.wait_ge(sem("y_turned"), i + 1)
                eng.tensor_copy(ytok[0:n, t, kg * 512:(kg + 1) * 512], ps[0:n, i % 8, :]).then_inc(sem("y_copied"), 1)

        def end_sync():
            eng = nc.sync
            for t in range(PT_ + 1):
                eng.wait_ge(sem("y_copied"), 2 * t + 2)
                dst = y_prompt[0, t * P:(t + 1) * P, :] if t < PT_ else y_sample.rearrange("b s d -> (b s) d")
                eng.dma_start(dst, ytok[0:tokens(t), t, :]).then_inc(sem("y_kept"), 16)
            eng.wait_ge(sem("y_kept"), 16 * (PT_ + 1))
            for g in (1, 2, 4, 5):
                eng.wait_ge(sem(f"kept{g}"), 16 * (PT_ + 1))

        @block.sync
        def _(sp):
            start_sync()
            wo_v = w_o.rearrange("l (k p) n -> p (l k) n", p=P)
            ffn_loads(in1, out1, f1_in, f1_out)
            qkv_sync()
            decode_sync()
            for d in range(DB):
                load_chunk(wo, d, d % 2, wo_v[:, :, d * P:(d + 1) * P], DB)
            ffn_loads(in3, out3, f2_in, f2_out)
            end_sync()

        @block.gpsimd
        def _(pool):
            start_pool()
            scale_residual(0)
            scale_residual(1)
            decode_pool()
            scale_residual(2)

        @block.scalar
        def _(act):
            start_scalar()
            modulate_scalar(0)
            ffn_in_scalar(0, 0, in1)
            project_scalar(0, out1, 2, 0)
            modulate_scalar(1)
            qkv_scalar()
            prompt_scalar()
            decode_scalar()
            mix_scalar()
            project_scalar(1, wo, 1, 1)
            modulate_scalar(2)
            ffn_in_scalar(2, 1, in3)
            project_scalar(2, out3, 2, 2)

        @block.vector
        def _(dve):
            start_vector()
            modulate_vector(0, 0, 1)
            ffn_in_vector(0, 0, in1)
            project_vector(0, out1, 2, 2)
            modulate_vector(1, 3, 4)
            qkv_vector()
            prompt_vector()
            decode_vector()
            mix_vector()
            project_vector(1, wo, 1, 5)
            modulate_vector(2, 6, 7)
            ffn_in_vector(2, 1, in3)
            project_vector(2, out3, 2, 8)
            end_vector()

        @block.tensor
        def _(pe):
            start_tensor()
            ffn_in_tensor(0, 0, in1)
            pe.wait_ge(sem("ffn_fflo"), FB)
            project_tensor(0, out1, HB, 2, ffhi, fflo)
            qkv_tensor()
            prompt_tensor()
            decode_tensor()
            mix_tensor()
            pe.wait_ge(sem("m_hlo"), DB)
            project_tensor(1, wo, DB, 1, hhi, hlo)
            ffn_in_tensor(2, 1, in3)
            pe.wait_ge(sem("ffn_fflo"), 2 * FB)
            project_tensor(2, out3, HB, 2, ffhi, fflo)
            end_tensor()


_INS = ["x_prompt", "x_sample", "c_prompt", "c_sample", "cache_win_k", "cache_win_v", "cache_diff_k", "cache_diff_v",
        "page_table", "ln_g", "ln_b", "w_ada", "b_ada", "ffn1_w_in", "ffn1_w_out", "ffn2_w_in", "ffn2_w_out",
        "w_qkv", "w_o", "diff_lambda", "subln_g"]
_CONSTS = ["ident", "rope", "mask_a", "mask_b", "past_a", "new_ab"]
_OUTS = [(1, 512, 1024), (8, 8, 1024), (1, 1, 512, 8, 64), (1, 1, 512, 8, 64), (1, 8, 8, 8, 64), (1, 8, 8, 8, 64),
         (1, 1, 4, 128, 4, 2, 64), (1, 1, 4, 128, 4, 128), (1, 8, 8, 4, 2, 64), (1, 8, 8, 4, 128)]


def kernel(**inputs):
    import concourse.bacc as _bacc
    from concourse.bass_utils import run_bass_kernel_spmd as _run

    nc = _bacc.Bacc("TRN2", target_bir_lowering=False, num_devices=1)
    tables = constants()
    arrays, args = {}, []
    for name in _INS + _CONSTS:
        a = np.ascontiguousarray(inputs[name] if name in _INS else tables[name])
        arrays[f"in_{name}_dram"] = a
        args.append(nc.dram_tensor(f"in_{name}_dram", a.shape, mybir.dt.from_np(a.dtype), kind="ExternalInput").ap())
    for i, shape in enumerate(_OUTS):
        args.append(nc.dram_tensor(f"out_{i}_dram", shape, F32, kind="ExternalOutput").ap())
    n = len(_INS + _CONSTS)
    yp, ys, wkp, wvp, wks, wvs, dkp, dvp, dks, dvs = args[n:]
    build(nc, *args[:n], yp, ys, wkp, wvp, wks, wvs, dkp, dvp, dks, dvs)
    r = _run(nc, [arrays], core_ids=[0])
    return tuple(r.results[0][f"out_{i}_dram"] for i in range(len(_OUTS)))
```

```python
import math
from contextlib import ExitStack

import concourse.bass as bass
import numpy as np
from concourse import mybir

F32 = mybir.dt.float32
F32R = mybir.dt.float32r
I32 = mybir.dt.int32
ALU = mybir.AluOpType
ACT = mybir.ActivationFunctionType
AX_X = mybir.AxisListType.X
ds = bass.ds

P = 128
D = 1024
DB = D // P
NPR = 512
PT_ = NPR // P
NB = 8
NS = 8
NSM = NB * NS
T = NPR + NSM
TH = T // 2
FF = 2816
FB = FF // P
HB = FB // 2
NC_ = 1 + NB
NM = 9
QW = 512
E = 64
PAST = 2048
PAGE = 128
NPAGE = PAST // PAGE
ALPHA = 2.0 ** 0.25
LN_EPS = 1e-5
RMS_EPS = 1e-5
LAM_INIT = 0.8 - 0.6 * math.exp(0.0)
SCALE = E ** -0.5
MASKED = -1e30
WCH = HB * P
DENSE = 512
A_NEAR = DENSE // P
A_FAR = 8
FARW = (PAST - DENSE) // 16
A_KEYS = A_FAR * FARW + A_NEAR * P
A_CHUNKS = (4, 4, 2, 2)
B_CHUNKS = (4, 4, 4, 4)
SW = PAST + NSM


def constants():
    inv = (np.float32(10000.0) ** (-np.arange(0, E, 2, dtype=np.float32) / np.float32(E))).astype(np.float32)
    pos = np.concatenate([np.arange(NPR), np.tile(PAST + np.arange(NS), NB)]).astype(np.float32)
    ang = pos[:, None] * inv[None, :]
    rope = np.zeros((P, PT_ + 1, 2, E // 2), np.float32)
    for t in range(PT_ + 1):
        rows = min(P, T - t * P)
        rope[:rows, t, 0] = np.cos(ang[t * P:t * P + rows])
        rope[:rows, t, 1] = np.sin(ang[t * P:t * P + rows])

    def log_count(delta):
        n = ((delta >= 0) & (delta <= 128)).astype(int)
        n += (delta >= 0) & (delta <= 512) & (delta % 4 == 0)
        n += (delta >= 0) & (delta <= 2048) & (delta % 16 == 0)
        return np.where(n > 0, np.log(np.maximum(n, 1)), MASKED).astype(np.float32)

    row, col = np.arange(P)[:, None], np.arange(NPR)[None, :]
    delta = row + (NPR - P) - col
    causal = np.where(delta >= 0, 0.0, MASKED).astype(np.float32)
    far = (np.arange(A_FAR)[:, None] + 16 * np.arange(FARW)[None, :]).ravel()
    near = (PAST - DENSE + np.arange(A_NEAR)[:, None] + A_NEAR * np.arange(P)[None, :]).ravel()
    keys = np.concatenate([far, near])
    query = (np.arange(P) % NS)[:, None]
    past = log_count(PAST + query - keys[None, :])
    new = np.full((P, 2, NB, NSM), MASKED, np.float32)
    own = query - np.arange(NS)[None, :]
    for b in range(NB):
        new[:, 0, b, b * NS:(b + 1) * NS] = log_count(own)
        new[:, 1, b, b * NS:(b + 1) * NS] = np.where(own >= 0, 0.0, MASKED)
    return {
        "ident": np.eye(P, dtype=np.float32), "rope": rope.reshape(P, -1),
        "mask_a": log_count(delta), "mask_b": causal, "past_a": past, "new_ab": new.reshape(P, -1),
    }


def build(nc, x_prompt, x_sample, c_prompt, c_sample, win_k, win_v, diff_k, diff_v, page_table, ln_g, ln_b,
          w_ada, b_ada, f1_in, f1_out, f2_in, f2_out, w_qkv, w_o, diff_lambda, subln_g,
          ident_d, rope_d, mask_a_d, mask_b_d, past_a_d, new_ab_d,
          y_prompt, y_sample, wkp, wvp, wks, wvs, dkp, dvp, dks, dvs):
    with ExitStack() as ctx:
        sems = {}

        def sem(name):
            if name not in sems:
                sems[name] = ctx.enter_context(nc.semaphore(name))
            return sems[name]

        at = [nc.sbuf_base + (-nc.sbuf_base) % 64]

        def place(name, shape, dt=F32, offset=None):
            size = int(np.prod(shape[1:])) * 4
            where = at[0] if offset is None else offset
            if offset is None:
                at[0] += (size + 63) // 64 * 64
            assert where + size <= nc.sbuf_usable_end, name
            return nc.alloc_sbuf_tensor_at(name, shape, dt, offset=where), where + (size + 63) // 64 * 64

        ident, _ = place("ident", [P, P])
        one_d, _ = place("one_d", [P, P])
        one_v, _ = place("one_v", [P, P])
        modT, _ = place("modT", [P, NM, DB, NC_])
        colT, _ = place("colT", [P, 128])
        stat, _ = place("stat", [P, 64])
        pages, _ = place("pages", [1, NB * NPAGE], I32)
        xT, _ = place("xT", [P, DB, T])
        wreg = [at[0]]
        w32, o = place("w32", [P, 2, WCH])
        wreg.append(o)
        whi, o = place("whi", [P, 2, WCH], F32R)
        wreg.append(o)
        wlo, treg = place("wlo", [P, 2, WCH], F32R)
        tmp, _ = place("tmp", [P, 4, T])
        hreg = at[0]
        hhi, _ = place("hhi", [P, DB, T], F32R)
        hlo, hend = place("hlo", [P, DB, T], F32R)
        freg = at[0]
        ffhi, _ = place("ffhi", [P, FB, T], F32R)
        fflo, fend = place("fflo", [P, FB, T], F32R)
        xtok, o = place("xtok", [P, PT_ + 1, D], offset=freg)
        wada, o = place("wada", [P, 4, DB // 2, D], offset=o)
        assert o <= fend
        ctok, o = place("ctok", [NC_, D], offset=hreg)
        csil, o = place("csil", [NC_, D], offset=o)
        cT, o = place("cT", [P, DB, 32], offset=o)
        rows, o = place("rows", [P, P], offset=o)
        modrow, o = place("modrow", [P, 2, 256], offset=o)
        lamb, o = place("lamb", [P, 4, E], offset=o)
        lamp, o = place("lamp", [P, 2, E], offset=o)
        assert o <= hend
        QT, o = place("QT", [P, 8, T], offset=freg)
        KT, o = place("KT", [P, 8, T], offset=o)
        V, o = place("V", [P, 2, PT_ + 1, QW], offset=o)
        QB, o = place("QB", [P, 2, 4, 32], offset=o)
        PTo = o
        rot, o = place("rot", [P, PT_ + 1, QW], offset=o)
        rab, o = place("rab", [P, 2, QW], offset=o)
        PTd, o3 = place("PTd", [P, NPAGE + 1, P], offset=PTo)
        new_ab, o4 = place("new_ab", [P, 2, NB, NSM], offset=o3)
        o = max(o, o4)
        kv01, o = place("kv01", [P, 2, 4, QW], offset=o)
        ropet, o = place("ropet", [P, PT_ + 1, 2, E // 2], offset=o)
        mask_a, o = place("mask_a", [P, NPR], offset=o)
        mask_b, o = place("mask_b", [P, NPR], offset=o)
        past_a, o = place("past_a", [P, A_KEYS], offset=o)
        assert o <= fend
        kv23, o = place("kv23", [P, 2, 4, QW], offset=hreg)
        KC, o = place("KC", [P, 4, QW], offset=o)
        S0, o = place("S0", [P, SW], offset=o)
        On, o = place("On", [P, P], offset=o)
        zeros, o = place("zeros", [P, NPR], offset=o)
        part, o = place("part", [P, 4, NS], offset=o)
        assert o <= hend
        S1, o = place("S1", [P, SW], offset=treg)
        assert o <= hreg
        S = (S0, S1)
        PTp0, o = place("PTp0", [P, PT_, NPR], offset=wreg[0])
        VH0, o = place("VH0", [P, PT_, P], offset=o)
        assert o <= wreg[1]
        PP, o = place("PP", [P, 4, NPR], offset=wreg[1])
        QP, o = place("QP", [P, 2, 2, P], offset=o)
        assert o <= wreg[2]
        PTp1, o = place("PTp1", [P, PT_, NPR], offset=wreg[2])
        VH1, o = place("VH1", [P, PT_, P], offset=o)
        assert o <= treg
        ytok, o = place("ytok", [P, PT_ + 1, D], offset=freg)

        def kv(slot):
            return kv01[:, slot] if slot < 2 else kv23[:, slot - 2]

        ps = ctx.enter_context(nc.psum_tensor("ps", [P, 8, 512], F32))

        block = ctx.enter_context(nc.Block())

        def pairs(eng, n, body, tail=0):
            body(0, 0)
            body(1, 1)
            with eng.Fori(1, n // 2 - tail) as i:
                body(2 * i, 0)
                body(2 * i + 1, 1)
            for s in range(n - 2 * tail, n):
                body(s, s % 2)

        class Weights:
            def __init__(self, name, chunks, width, before, run=0):
                self.chunks, self.width, self.before, self.base = chunks, width, before, run * chunks
                self.landed = [sem(f"{name}_landed{slot}") for slot in range(2)]
                self.hi, self.lo, self.used = sem(name + "_hi"), sem(name + "_lo"), sem(name + "_used")

        in1 = Weights("w_in", 2 * FB, DB * P, None)
        out1 = Weights("w_out", 2 * DB, HB * P, in1)
        qkv = Weights("w_qkv", 24, 2 * QW, out1)
        wo = Weights("w_o", DB, DB * P, qkv)
        in3 = Weights("w_in", 2 * FB, DB * P, wo, run=1)
        out3 = Weights("w_out", 2 * DB, HB * P, in3, run=1)

        def load_chunk(ph, c, slot, src, nk):
            if not (isinstance(c, int) and c < 2):
                nc.sync.wait_ge(ph.lo, ph.base + c - 1)
            elif ph.before:
                nc.sync.wait_ge(ph.before.lo, ph.before.base + ph.before.chunks - 1 + c)
            dst = w32[:, slot, 0:ph.width].rearrange("p (k n) -> p k n", k=nk)
            nc.sync.dma_start(dst, src).then_inc(ph.landed[slot], 16)

        def split_hi(ph, c, slot):
            n = c // 2 * 16 if isinstance(c, int) else (c - slot) * 8
            nc.scalar.wait_ge(ph.landed[slot], 8 * ph.base + n + 16)
            if not (isinstance(c, int) and c < 2):
                nc.scalar.wait_ge(ph.used, ph.base + c - 1)
            elif ph.before:
                nc.scalar.wait_ge(ph.before.used, ph.before.base + ph.before.chunks - 1 + c)
            w = ph.width
            nc.scalar.activation(whi[:, slot, 0:w], w32[:, slot, 0:w], ACT.Copy).then_inc(ph.hi, 1)

        def split_lo(ph, c, slot):
            nc.vector.wait_ge(ph.hi, ph.base + c + 1)
            w = ph.width
            nc.vector.tensor_tensor(wlo[:, slot, 0:w], w32[:, slot, 0:w], whi[:, slot, 0:w].bitcast(F32),
                                    ALU.subtract).then_inc(ph.lo, 1)

        def chunk_products(ph, slot, nk, xhi, xlo, k0, kall, banks):
            pe = nc.tensor
            m = None
            for k in range(nk):
                kk = k0 + k
                wh = whi[:, slot, k * P:(k + 1) * P]
                wl = wlo[:, slot, k * P:(k + 1) * P]
                for n, (w, x) in enumerate(((wh, xhi), (wh, xlo), (wl, xhi))):
                    for h in range(2):
                        m = pe.matmul(ps[:, banks + h, 0:TH], w, x[:, kk, h * TH:(h + 1) * TH],
                                      start=(kk == 0 and n == 0), stop=(kk == kall - 1 and n == 2))
            m.then_inc(ph.used, 1)

        def modulate_vector(st, i_shift, i_scale):
            eng = nc.vector
            def lo(d):
                eng.wait_ge(sem("step_hhi"), st * DB + d + 1)
                eng.tensor_tensor(hlo[:, d, :], tmp[:, d % 2, :], hhi[:, d, :].bitcast(F32),
                                  ALU.subtract).then_inc(sem("step_hlo"), 1)
            for d in range(DB):
                if st > 0:
                    eng.wait_ge(sem("step_x"), (st - 1) * DB + d + 1)
                else:
                    eng.wait_ge(sem("x_copied"), d + 1)
                    eng.wait_ge(sem("xs_copied"), 1)
                if d >= 2:
                    eng.wait_ge(sem("step_hlo"), st * DB + d - 1)
                eng.tensor_scalar(tmp[:, d % 2, 0:NPR], xT[:, d, 0:NPR], modT[:, i_scale, d, 0:1],
                                  modT[:, i_shift, d, 0:1], ALU.mult, ALU.add).then_inc(sem("step_h"), 1)
                hs = tmp[:, d % 2, NPR:T].rearrange("p (b s) -> p b s", s=NS)
                xs = xT[:, d, NPR:T].rearrange("p (b s) -> p b s", s=NS)
                eng.tensor_tensor(hs, xs, modT[:, i_scale, d, 1:NC_].unsqueeze(2).to_broadcast([P, NB, NS]),
                                  ALU.mult).then_inc(sem("step_hm"), 1)
                eng.wait_ge(sem("step_hm"), st * DB + d + 1)
                eng.tensor_tensor(hs, hs, modT[:, i_shift, d, 1:NC_].unsqueeze(2).to_broadcast([P, NB, NS]),
                                  ALU.add).then_inc(sem("step_h"), 1)
                if d >= 1:
                    lo(d - 1)
            lo(DB - 1)

        def modulate_scalar(st):
            eng = nc.scalar
            for d in range(DB):
                eng.wait_ge(sem("step_h"), st * 2 * DB + 2 * d + 2)
                eng.activation(hhi[:, d, :], tmp[:, d % 2, :], ACT.Copy).then_inc(sem("step_hhi"), 1)

        def scale_residual(st):
            eng = nc.gpsimd
            eng.wait_ge(sem("step_h"), st * 2 * DB + 2 * DB)
            for d in range(DB):
                eng.tensor_scalar(xT[:, d, :], xT[:, d, :], ALPHA, None, ALU.mult).then_inc(sem("step_xa"), 1)

        def project_tensor(st, ph, nk_chunk, n_half, xhi, xlo):
            pe = nc.tensor
            kall = nk_chunk * n_half
            def body(d, par):
                if not (isinstance(d, int) and d < 2):
                    pe.wait_ge(sem("step_res"), st * DB + d - 1)
                for hh in range(n_half):
                    slot = hh if n_half == 2 else par
                    pe.wait_ge(ph.lo, ph.base + n_half * d + hh + 1)
                    chunk_products(ph, slot, nk_chunk, xhi, xlo, hh * nk_chunk, kall, 2 * par)
            pairs(pe, DB, body)
            for d in range(DB):
                pe.wait_ge(sem("step_res"), st * DB + d + 1)
                for h in range(2):
                    m = pe.matmul(ps[:, 4 + h, 0:TH], one_d[:], xT[:, d, h * TH:(h + 1) * TH],
                                  start=(d == 0), stop=(d == DB - 1))
            m.then_inc(sem("step_mean"), 1)
            for d in range(DB):
                pe.wait_ge(sem("step_sq"), st * DB + d + 1)
                for h in range(2):
                    m = pe.matmul(ps[:, 6 + h, 0:TH], one_d[:], tmp[:, d % 2, h * TH:(h + 1) * TH],
                                  start=(d == 0), stop=(d == DB - 1))
                m.then_inc(sem("step_var"), 1)

        def project_vector(st, ph, n_half, i_gate):
            eng = nc.vector
            n = DB * n_half
            split_lo(ph, 0, 0)
            split_lo(ph, 1, 1)
            for d in range(DB):
                if n_half == 2 and 2 * d + 2 < n:
                    split_lo(ph, 2 * d + 2, 0)
                eng.wait_ge(ph.used, ph.base + n_half * (d + 1))
                eng.wait_ge(sem("step_xa"), st * DB + d + 1)
                b = 2 * (d % 2)
                gate = modT[:, i_gate, d, 0:1]
                eng.scalar_tensor_tensor(out=xT[:, d, 0:TH], in0=ps[:, b, 0:TH], scalar=gate, in1=xT[:, d, 0:TH],
                                         op0=ALU.mult, op1=ALU.add)
                eng.scalar_tensor_tensor(out=xT[:, d, TH:NPR], in0=ps[:, b + 1, 0:NPR - TH], scalar=gate,
                                         in1=xT[:, d, TH:NPR], op0=ALU.mult, op1=ALU.add)
                if d >= 1:
                    eng.wait_ge(sem("step_res"), st * DB + d)
                gs = tmp[:, 2, 0:NSM].rearrange("p (b s) -> p b s", s=NS)
                eng.tensor_tensor(gs, ps[:, b + 1, NPR - TH:TH].rearrange("p (b s) -> p b s", s=NS),
                                  modT[:, i_gate, d, 1:NC_].unsqueeze(2).to_broadcast([P, NB, NS]),
                                  ALU.mult).then_inc(sem("step_gs"), 1)
                eng.wait_ge(sem("step_gs"), st * DB + d + 1)
                eng.tensor_tensor(xT[:, d, NPR:T], xT[:, d, NPR:T], tmp[:, 2, 0:NSM],
                                  ALU.add).then_inc(sem("step_res"), 1)
                if n_half == 2 and 2 * d + 3 < n:
                    split_lo(ph, 2 * d + 3, 1)
                if n_half == 1 and d + 2 < n:
                    split_lo(ph, d + 2, d % 2)
            eng.wait_ge(sem("step_mean"), st + 1)
            halves = lambda ap: ap.rearrange("p (h t) -> p h t", h=2)
            for d in range(DB):
                eng.tensor_tensor(halves(xT[:, d, :]), halves(xT[:, d, :]), ps[:, 4:6, 0:TH],
                                  ALU.subtract).then_inc(sem("step_cen"), 1)
            eng.wait_ge(sem("step_var"), st * DB + DB)
            eng.tensor_scalar(halves(tmp[:, 2, :]), ps[:, 6:8, 0:TH], LN_EPS, None, ALU.add).then_inc(sem("step_ve"), 1)
            eng.wait_ge(sem("step_std"), st + 1)
            eng.reciprocal(tmp[:, 3, :], tmp[:, 3, :]).then_inc(sem("step_rs"), 1)
            eng.wait_ge(sem("step_rs"), st + 1)
            for d in range(DB):
                eng.tensor_tensor(xT[:, d, :], xT[:, d, :], tmp[:, 3, :], ALU.mult).then_inc(sem("step_nrm"), 1)

        def project_scalar(st, ph, n_half, i_ln):
            eng = nc.scalar
            for c in range(DB * n_half):
                split_hi(ph, c, c % 2)
            for d in range(DB):
                eng.wait_ge(sem("step_cen"), st * DB + d + 1)
                if d >= 2:
                    eng.wait_ge(sem("step_var"), st * DB + d - 1)
                eng.activation(tmp[:, d % 2, :], xT[:, d, :], ACT.Square).then_inc(sem("step_sq"), 1)
            eng.wait_ge(sem("step_ve"), st + 1)
            eng.activation(tmp[:, 3, :], tmp[:, 2, :], ACT.Sqrt).then_inc(sem("step_std"), 1)
            for d in range(DB):
                eng.wait_ge(sem("step_nrm"), st * DB + d + 1)
                g = colT[:, 72 + i_ln * DB + d:73 + i_ln * DB + d]
                b = colT[:, 96 + i_ln * DB + d:97 + i_ln * DB + d]
                eng.activation(xT[:, d, :], xT[:, d, :], ACT.Identity, bias=b, scale=g).then_inc(sem("step_x"), 1)

        def ffn_in_tensor(st, ffn, ph):
            pe = nc.tensor
            pe.wait_ge(sem("step_hlo"), st * DB + DB)
            def body(j, par):
                for gu in range(2):
                    if not (isinstance(j, int) and j < 2):
                        pe.wait_ge(sem("ffn_mul" if gu else "ffn_silu"), ffn * FB + j - 1)
                    pe.wait_ge(ph.lo, ph.base + 2 * j + gu + 1)
                    chunk_products(ph, gu, DB, hhi, hlo, 0, DB, 4 * par + 2 * gu)
            pairs(pe, FB, body)

        def ffn_in_scalar(st, ffn, ph):
            eng = nc.scalar
            split_hi(ph, 0, 0)
            split_hi(ph, 1, 1)
            def body(j, par):
                last = isinstance(j, int) and j == FB - 1
                if not last:
                    split_hi(ph, 2 * j + 2, 0)
                eng.wait_ge(ph.used, ph.base + 2 * j + 1)
                if not (isinstance(j, int) and j < 2):
                    eng.wait_ge(sem("ffn_mul"), ffn * FB + j - 1)
                eng.activation(tmp[:, par, :].rearrange("p (h t) -> p h t", h=2), ps[:, 4 * par:4 * par + 2, 0:TH],
                               ACT.Silu).then_inc(sem("ffn_silu"), 1)
                if not last:
                    split_hi(ph, 2 * j + 3, 1)
                eng.wait_ge(sem("ffn_mul"), ffn * FB + j + 1)
                eng.activation(ffhi[:, ds(j, 1), :].rearrange("p a t -> p (a t)"), tmp[:, 2 + par, :],
                               ACT.Copy).then_inc(sem("ffn_ffhi"), 1)
            pairs(eng, FB, body, tail=1)

        def ffn_in_vector(st, ffn, ph):
            eng = nc.vector
            split_lo(ph, 0, 0)
            split_lo(ph, 1, 1)
            def body(j, par):
                last = isinstance(j, int) and j == FB - 1
                if not last:
                    split_lo(ph, 2 * j + 2, 0)
                eng.wait_ge(ph.used, ph.base + 2 * j + 2)
                eng.wait_ge(sem("ffn_silu"), ffn * FB + j + 1)
                if not (isinstance(j, int) and j < 2):
                    eng.wait_ge(sem("ffn_fflo"), ffn * FB + j - 1)
                half = lambda ap: ap.rearrange("p (h t) -> p h t", h=2)
                eng.tensor_tensor(half(tmp[:, 2 + par, :]), half(tmp[:, par, :]), ps[:, 4 * par + 2:4 * par + 4, 0:TH],
                                  ALU.mult).then_inc(sem("ffn_mul"), 1)
                if not last:
                    split_lo(ph, 2 * j + 3, 1)
                eng.wait_ge(sem("ffn_ffhi"), ffn * FB + j + 1)
                eng.tensor_tensor(fflo[:, ds(j, 1), :].rearrange("p a t -> p (a t)"), tmp[:, 2 + par, :],
                                  ffhi[:, ds(j, 1), :].rearrange("p a t -> p (a t)").bitcast(F32),
                                  ALU.subtract).then_inc(sem("ffn_fflo"), 1)
            pairs(eng, FB, body, tail=1)

        def ffn_loads(ph_in, ph_out, w_in, w_out):
            eng = nc.sync
            wi = w_in.rearrange("l (k p) n -> p (l k) n", p=P)
            wo_ = w_out.rearrange("l (k p) n -> p (l k) n", p=P)
            def body(j, par):
                for gu in range(2):
                    load_chunk(ph_in, 2 * j + gu, gu, wi[:, :, ds(j * P + gu * FF, P)], DB)
            pairs(eng, FB, body)
            for d in range(DB):
                for hh in range(2):
                    load_chunk(ph_out, 2 * d + hh, hh, wo_[:, hh * HB:(hh + 1) * HB, d * P:(d + 1) * P], HB)

        def start_sync():
            eng = nc.sync
            eng.dma_start(ctok[0:1, :], c_prompt).then_inc(sem("c_landed"), 16)
            eng.dma_start(ctok[1:NC_, :], c_sample).then_inc(sem("c_landed"), 16)
            eng.dma_start(ident[:], ident_d).then_inc(sem("ident_landed"), 16)
            eng.dma_start(rows[0:72, :], b_ada.rearrange("l (r c) -> (l r) c", c=P)).then_inc(sem("rows_landed"), 16)
            eng.dma_start(rows[72:96, :], ln_g.rearrange("l i (r c) -> (l i r) c", c=P)).then_inc(sem("rows_landed"), 16)
            eng.dma_start(rows[96:120, :], ln_b.rearrange("l i (r c) -> (l i r) c", c=P)).then_inc(sem("rows_landed"), 16)
            eng.dma_start(rows[120:121, :], subln_g).then_inc(sem("rows_landed"), 16)
            wa = w_ada.rearrange("l (k p) n -> p (l k) n", p=P)
            for i in range(NM):
                for kh in range(2):
                    n = 2 * i + kh
                    if n >= 4:
                        eng.wait_ge(sem("ada_used"), n - 3)
                    eng.dma_start(wada[:, n % 4], wa[:, kh * 4:kh * 4 + 4, i * D:(i + 1) * D]).then_inc(sem(f"ada_landed{n % 4}"), 16)
                if i == 1:
                    eng.dma_start(xtok[:, 0:PT_, :], x_prompt.rearrange("b (t p) d -> p (b t) d", p=P)).then_inc(sem("x_landed"), 16)
                    eng.dma_start(xtok[0:NSM, PT_, :], x_sample.rearrange("b s d -> (b s) d")).then_inc(sem("x_landed"), 16)
                    eng.dma_start(lamb[:].rearrange("p a b -> p (a b)"),
                                  diff_lambda.rearrange("l a e -> l (a e)").to_broadcast([P, 4 * E])).then_inc(sem("lam_landed"), 16)
                    eng.dma_start(pages[:], page_table.rearrange("b n -> (b n)").unsqueeze(0)).then_inc(sem("pages"), 16)

        def start_pool():
            eng = nc.gpsimd
            eng.memset(cT[:], 0.0).then_inc(sem("pool_set"), 1)
            eng.memset(one_d[:], 1.0 / D).then_inc(sem("pool_set"), 1)
            eng.memset(one_v[:], 1.0 / P).then_inc(sem("pool_set"), 1)

        def start_tensor():
            pe = nc.tensor
            pe.wait_ge(sem("ident_landed"), 16)
            pe.wait_ge(sem("csil"), 1)
            for k in range(DB):
                m = pe.transpose(ps[:, 0, k * 16:k * 16 + NC_], csil[:, k * P:(k + 1) * P], ident[0:NC_, 0:NC_])
            m.then_inc(sem("c_turned"), 1)
            pe.wait_ge(sem("rows_landed"), 64)
            pe.transpose(ps[:, 7, 0:121], rows[0:121, :], ident[0:121, 0:121]).then_inc(sem("rows_turned"), 1)
            pe.wait_ge(sem("cT"), 1)

            def turn_x(k):
                if k >= 2:
                    pe.wait_ge(sem("x_copied"), k - 1)
                for t in range(PT_):
                    m = pe.transpose(ps[:, 4 + k % 2, t * P:(t + 1) * P], xtok[:, t, k * P:(k + 1) * P], ident[:])
                m.then_inc(sem("x_turned"), 1)

            for i in range(NM):
                if i >= 2:
                    pe.wait_ge(sem("mod_row"), i - 1)
                for k in range(DB):
                    if k % 4 == 0:
                        n = 2 * i + k // 4
                        pe.wait_ge(sem(f"ada_landed{n % 4}"), 16 * (n // 4 + 1))
                    for j in range(4):
                        m = pe.matmul(ps[32 * j:32 * j + 32, i % 2, 0:256], cT[:, k, :],
                                      wada[:, n % 4, k % 4, j * 256:(j + 1) * 256], start=(k == 0), stop=(k == DB - 1),
                                      tile_position=(0, 32 * j))
                    if k % 4 == 3:
                        m.then_inc(sem("ada_used"), 1)
                if i == 1:
                    pe.wait_ge(sem("x_landed"), 32)
                if 1 <= i:
                    turn_x(i - 1)
                if i == 1:
                    for k in range(DB):
                        m = pe.transpose(ps[:, 6, k * NSM:(k + 1) * NSM], xtok[0:NSM, PT_, k * P:(k + 1) * P], ident[0:NSM, 0:NSM])
                    m.then_inc(sem("xs_turned"), 1)
                pe.wait_ge(sem("mod_row"), i + 1)
                if i >= 2:
                    pe.wait_ge(sem("mod_bias"), i - 1)
                for h in range(2):
                    m = pe.transpose(ps[:, 2 + i % 2, h * P:(h + 1) * P], modrow[:, i % 2, h * P:(h + 1) * P], ident[:])
                m.then_inc(sem("mod_turned"), 1)

        def start_scalar():
            eng = nc.scalar
            eng.wait_ge(sem("c_landed"), 32)
            eng.activation(csil[:], ctok[:], ACT.Silu).then_inc(sem("csil"), 1)
            eng.wait_ge(sem("pool_set"), 1)
            eng.wait_ge(sem("c_turned"), 1)
            eng.activation(cT[:, :, 0:NC_], ps[:, 0, 0:DB * 16].rearrange("p (k c) -> p k c", c=16)[:, :, 0:NC_],
                           ACT.Copy).then_inc(sem("cT"), 1)
            eng.wait_ge(sem("lam_dots"), 1)
            eng.activation(stat[:, 0:2], stat[:, 0:2], ACT.Exp).then_inc(sem("lam_exp"), 1)
            for i in range(NM):
                eng.wait_ge(sem("ada_used"), 2 * i + 2)
                if i >= 2:
                    eng.wait_ge(sem("mod_turned"), i - 1)
                eng.activation(modrow[:, i % 2, :], ps[:, i % 2, 0:256], ACT.Copy).then_inc(sem("mod_row"), 1)
                if i >= 1:
                    k = i - 1
                    eng.wait_ge(sem("x_turned"), k + 1)
                    eng.activation(xT[:, k, 0:NPR], ps[:, 4 + k % 2, :], ACT.Copy).then_inc(sem("x_copied"), 1)

        def start_vector():
            eng = nc.vector
            eng.wait_ge(sem("lam_landed"), 16)
            l4 = lamb[:].rearrange("p (a b) e -> p a b e", b=2)
            eng.tensor_tensor(lamp[:], l4[:, :, 0, :], l4[:, :, 1, :], ALU.mult).then_inc(sem("lam_mul"), 1)
            eng.wait_ge(sem("lam_mul"), 1)
            eng.reduce_sum(stat[:, 0:2], lamp[:], AX_X).then_inc(sem("lam_dots"), 1)
            eng.wait_ge(sem("rows_turned"), 1)
            eng.tensor_copy(colT[:, 0:121], ps[:, 7, 0:121]).then_inc(sem("cols"), 1)
            eng.wait_ge(sem("cols"), 1)
            eng.wait_ge(sem("xs_turned"), 1)
            eng.tensor_copy(xT[:, :, NPR:T], ps[:, 6, :].rearrange("p (k s) -> p k s", s=NSM)).then_inc(sem("xs_copied"), 1)
            eng.wait_ge(sem("lam_exp"), 1)
            eng.tensor_tensor(stat[:, 2:3], stat[:, 1:2], stat[:, 0:1], ALU.subtract).then_inc(sem("lam_sub"), 1)
            eng.wait_ge(sem("lam_sub"), 1)
            eng.tensor_scalar(stat[:, 3:4], stat[:, 2:3], -LAM_INIT, None, ALU.add).then_inc(sem("lam"), 1)
            eng.tensor_scalar(stat[:, 4:5], colT[:, 120:121], 1.0 - LAM_INIT, None, ALU.mult).then_inc(sem("lam"), 1)
            for i in range(NM):
                eng.wait_ge(sem("mod_turned"), i + 1)
                src = ps[:, 2 + i % 2, 0:256].rearrange("p (h j c) -> p j h c", h=2, j=4)[:, :, :, 0:NC_]
                dst = modT[:, i, :, :].rearrange("p (j h) c -> p j h c", h=2)
                b = colT[:, i * DB:(i + 1) * DB].rearrange("p (j h) -> p j h", h=2).unsqueeze(3).to_broadcast([P, 4, 2, NC_])
                eng.tensor_tensor(dst, src, b, ALU.add).then_inc(sem("mod_bias"), 1)
                eng.wait_ge(sem("mod_bias"), i + 1)
                a, m = {0: (0.0, 1.0), 1: (1.0, 1.0), 2: (0.0, (0.5, 1.0, 0.5)[i // 3])}[i % 3]
                eng.tensor_scalar(modT[:, i, :, :], modT[:, i, :, :], a, m, ALU.add, ALU.mult).then_inc(sem("mods"), 1)
            eng.wait_ge(sem("mods"), NM)

        ROTS = (0, 1, 3, 4)
        VS = (2, 5)

        def qkv_bank(g, t):
            return (5 * g + t) % 6

        def tokens(t):
            return P if t < PT_ else NSM

        def qkv_sync():
            eng = nc.sync
            w = w_qkv.rearrange("l (k p) n -> p (l k) n", p=P)
            outs = {1: (wkp, wks), 2: (wvp, wvs), 4: (dkp, dks), 5: (dvp, dvs)}
            def flat(ap):
                names = "abcdefg"[:len(ap.shape)]
                lead = names[:-2] if ap is not dkp and ap is not dks else names[:-3]
                rest = names[len(lead):]
                return ap.rearrange(f"{' '.join(names)} -> ({' '.join(lead)}) ({' '.join(rest)})")
            def store(g):
                op, os_ = (flat(a) for a in outs[g])
                ready = "rot" if g in ROTS else "vout"
                base = (ROTS if g in ROTS else VS).index(g) * (PT_ + 1)
                for t in range(PT_ + 1):
                    eng.wait_ge(sem(ready), (base + t + 1) * (2 if g in ROTS else 1))
                    n = tokens(t)
                    src = rot[0:n, t, :] if g in ROTS else V[0:n, VS.index(g), t, :]
                    dst = op[t * P:(t + 1) * P, :] if t < PT_ else os_
                    eng.dma_start(dst, src).then_inc(sem(f"kept{g}"), 16)
            for g in range(6):
                for c in range(4):
                    load_chunk(qkv, 4 * g + c, c % 2, w[:, 2 * c:2 * c + 2, g * QW:(g + 1) * QW], 2)
                if g == 0:
                    eng.wait_ge(out1.used, 2 * DB)
                    eng.dma_start(ropet[:].rearrange("p a b c -> p (a b c)"), rope_d).then_inc(sem("tables"), 16)
                    eng.dma_start(mask_a[:], mask_a_d).then_inc(sem("tables"), 16)
                    eng.dma_start(mask_b[:], mask_b_d).then_inc(sem("tables"), 16)
                    eng.dma_start(past_a[:], past_a_d).then_inc(sem("tables"), 16)
                if g - 1 in outs:
                    store(g - 1)
            store(5)

        def turn_rot(g, t):
            pe = nc.tensor
            r = ROTS.index(g) * (PT_ + 1) + t
            pe.wait_ge(sem("rot"), 2 * r + 2)
            if r >= 2:
                pe.wait_ge(sem("qk_copied"), r - 1)
            n = tokens(t)
            for f in range(4):
                m = pe.transpose(ps[:, 6 + r % 2, f * P:f * P + n], rot[0:n, t, f * P:(f + 1) * P], ident[0:n, 0:n])
            m.then_inc(sem("qk_turned"), 1)

        def tile_summed(eng, g, t):
            if t < PT_:
                eng.wait_ge(sem("qkv_sum"), PT_ * g + t + 1)
            else:
                eng.wait_ge(qkv.used, 4 * g + 4)

        def qkv_tensor():
            pe = nc.tensor
            pe.wait_ge(sem("step_hlo"), 1 * DB + DB)
            for g in range(7):
                for c in range(4):
                    if g < 6:
                        slot = c % 2
                        pe.wait_ge(qkv.lo, 4 * g + c + 1)
                        for t in range(PT_ + 1):
                            n = tokens(t)
                            if c == 0 and 5 * g + t >= 6:
                                g0, t0 = divmod(5 * g + t - 6, 5)
                                if g0 in ROTS:
                                    pe.wait_ge(sem("qkv_read"), ROTS.index(g0) * (PT_ + 1) + t0 + 1)
                                else:
                                    pe.wait_ge(sem("vout"), VS.index(g0) * (PT_ + 1) + t0 + 1)
                            for k in range(2):
                                kk = 2 * c + k
                                wh = whi[:, slot, k * QW:(k + 1) * QW]
                                wl = wlo[:, slot, k * QW:(k + 1) * QW]
                                for x, w, n3 in ((hhi, wh, 0), (hlo, wh, 1), (hhi, wl, 2)):
                                    m = pe.matmul(ps[0:n, qkv_bank(g, t), :], x[:, kk, t * P:t * P + n], w,
                                                  start=(kk == 0 and n3 == 0), stop=(kk == DB - 1 and n3 == 2))
                            if c == 3 and t < PT_:
                                m.then_inc(sem("qkv_sum"), 1)
                        m.then_inc(qkv.used, 1)
                    if g - 1 in ROTS and c in (1, 2):
                        for t in ((0, 1, 2), (3, 4))[c - 1]:
                            turn_rot(g - 1, t)

        def qkv_scalar():
            eng = nc.scalar
            def copy_turned(g, t):
                r = ROTS.index(g) * (PT_ + 1) + t
                eng.wait_ge(sem("qk_turned"), r + 1)
                n = tokens(t)
                dst = (QT if g in (0, 3) else KT)[:, 4 * (g // 3):4 * (g // 3) + 4, t * P:t * P + n]
                src = ps[:, 6 + r % 2, :].rearrange("p (f t) -> p f t", f=4)[:, :, 0:n]
                eng.activation(dst, src, ACT.Copy, scale=(SCALE if g in (0, 3) else 1.0)).then_inc(sem("qk_copied"), 1)
            def copy_v(g, t):
                n = tokens(t)
                tile_summed(eng, g, t)
                eng.activation(V[0:n, VS.index(g), t, :], ps[0:n, qkv_bank(g, t), :], ACT.Copy).then_inc(sem("vout"), 1)
            for g in range(6):
                if g - 1 in VS:
                    for t in range(PT_ + 1):
                        copy_v(g - 1, t)
                for c in range(4):
                    split_hi(qkv, 4 * g + c, c % 2)
                    if g - 1 in ROTS and c == 3:
                        for t in range(PT_ + 1):
                            copy_turned(g - 1, t)
            for t in range(PT_ + 1):
                copy_v(5, t)

        def qkv_vector():
            eng = nc.vector
            def rotate(g, t):
                r = ROTS.index(g) * (PT_ + 1) + t
                n = tokens(t)
                tile_summed(eng, g, t)
                if r >= 1:
                    eng.wait_ge(sem("rot"), 2 * r)
                src = ps[0:n, qkv_bank(g, t), :].rearrange("p (h e) -> p h e", e=E // 2)
                tab = lambda i: ropet[0:n, t, i, :].unsqueeze(1).to_broadcast([n, 2 * 8, E // 2])
                half = lambda i: rab[0:n, i, :].rearrange("p (h e) -> p h e", e=E // 2)
                eng.tensor_tensor(half(0), src, tab(0), ALU.mult).then_inc(sem("rope_cos"), 1)
                eng.tensor_tensor(half(1), src, tab(1), ALU.mult).then_inc(sem("qkv_read"), 1)
                eng.wait_ge(sem("rope_cos"), r + 1)
                eng.wait_ge(sem("qkv_read"), r + 1)
                if r >= 5:
                    g0 = ROTS[ROTS.index(g) - 1]
                    eng.wait_ge(sem("qk_turned"), r - 4)
                    if g0 in (1, 4):
                        eng.wait_ge(sem(f"kept{g0}"), 16 * (PT_ + 1))
                q = lambda i: rab[0:n, i, :].rearrange("p (h two e) -> p h two e", two=2, e=E // 2)
                o = rot[0:n, t, :].rearrange("p (h two e) -> p h two e", two=2, e=E // 2)
                eng.tensor_tensor(o[:, :, 0, :], q(0)[:, :, 0, :], q(1)[:, :, 1, :], ALU.subtract).then_inc(sem("rot"), 1)
                eng.tensor_tensor(o[:, :, 1, :], q(0)[:, :, 1, :], q(1)[:, :, 0, :], ALU.add).then_inc(sem("rot"), 1)
            for g in range(6):
                for c in range(4):
                    split_lo(qkv, 4 * g + c, c % 2)
                    if g == 1 and c == 0:
                        eng.wait_ge(sem("tables"), 4 * 16)
                    if g - 1 in ROTS and c < 2:
                        for t in ((0, 1, 2, 3), (4,))[c]:
                            rotate(g - 1, t)

        QUARTERS = 8
        LAG = 5
        DRAIN = 6
        HEADS = 4 * 2 + 4
        CH = (A_CHUNKS, B_CHUNKS)
        WID = (A_KEYS, PAST)
        DMAS = ((1, 1, 1, 1), (4, 4, 4, 4))

        def keys_of(m, tile):
            return FARW if m == 0 and tile < A_FAR else P

        def key0(m, tile):
            return tile * P if m else min(tile, A_FAR) * FARW + max(tile - A_FAR, 0) * P

        def tile0(m, c):
            return sum(CH[m][:c])

        def chunk_keys(m, c):
            return CH[m][c] * keys_of(m, tile0(m, c))

        def landed_at(b, m, c):
            before = sum(DMAS[k][j] for k in range(2) for j in range(4) if j % 2 == c % 2 and (k, j) <= (m, c))
            return 16 * (b * sum(DMAS[k][j] for k in range(2) for j in range(4) if j % 2 == c % 2) + before)

        def positive(n):
            return not isinstance(n, int) or n > 0

        def back(b, i, lag):
            return (b, i - lag) if i >= lag else (b - 1, i - lag + QUARTERS)

        def alive(b):
            return not isinstance(b, int) or 0 <= b < NB

        def mixer_of(b, run):
            return run if not isinstance(b, int) else int(b >= 4)

        def over_sequences(eng, body):
            body(0, 0)
            with eng.Fori(1, 4) as b:
                body(b, 0)
            body(4, 1)
            with eng.Fori(5, NB) as b:
                body(b, 1)
            body(NB, 1)

        def each_sequence(body):
            for b in range(NB + 1):
                body(b, int(b >= 4))

        def quarters(b):
            return range(QUARTERS if alive(b) else DRAIN)

        def step_of(pm, i):
            return divmod(i, 4) if pm == 0 else (i % 2, i // 2)

        def turn_of(pm, b, i):
            return QUARTERS * b + i if pm == 0 else 16 + 4 * b + i // 2

        def is_turn(pm, i):
            return pm == 0 or i % 2 == 1

        def head_of(pm, b, i):
            return 2 * b + i // 4 if pm == 0 else b + 4

        def ends_head(pm, i):
            return i % 4 == 3 if pm == 0 else i == 7

        def turned(pm, i):
            return PTp1 if pm == 0 and i >= 4 else PTp0

        def head_values(pm, i):
            return VH1 if pm == 0 and i >= 4 else VH0

        def attend_sync():
            eng = nc.sync
            far = [w[:, :, 0:PAST - DENSE].rearrange("l b (g j) h e -> (l b) g j (h e)", j=16) for w in (win_k, win_v)]
            near = [w[:, :, PAST - DENSE:PAST].rearrange("l b (p t) h e -> (l b) p t (h e)", t=A_NEAR) for w in (win_k, win_v)]
            pool = [diff_k.rearrange("l n p h c e -> (l n) p (h c e)"), diff_v.rearrange("l n p h v -> (l n) p (h v)")]

            def load(b, i, is_v):
                m, c = divmod(i, 4)
                n, tile = CH[m][c], tile0(m, c)
                if m == 1:
                    page = [eng.value_load(pages[0:1, ds(b * NPAGE + tile + k, 1)], min_val=0,
                                           max_val=diff_k.shape[1] - 1) for k in range(n)]
                q = QUARTERS * b + i
                if positive(q - 1):
                    if is_v:
                        eng.wait_ge(sem("d_pv"), q - 1)
                    else:
                        eng.wait_ge(sem("d_kt"), 4 * q - 4)
                slot = kv(2 * is_v + c % 2)
                s = sem(f"{'kv'[is_v]}_landed{c % 2}")
                if m == 0 and tile < A_FAR:
                    src = far[is_v][ds(b, 1), :, tile:tile + n, :].rearrange("a g j c -> (a g) j c")
                    eng.dma_start(slot[0:FARW, 0:n, :], src).then_inc(s, 16)
                elif m == 0:
                    t0 = tile - A_FAR
                    src = near[is_v][ds(b, 1), :, t0:t0 + n, :].rearrange("a p t c -> (a p) t c")
                    eng.dma_start(slot[:, 0:n, :], src).then_inc(s, 16)
                else:
                    for k in range(n):
                        src = pool[is_v][ds(page[k], 1), :, :].rearrange("a p c -> (a p) c")
                        eng.dma_start(slot[:, k, :], src).then_inc(s, 16)

            def body(b, run):
                for i in quarters(b):
                    if alive(b):
                        load(b, i, 0)
                    if isinstance(b, int) and b == 0 and i == 1:
                        eng.wait_ge(sem("qk_turned"), 4 * (PT_ + 1))
                        eng.wait_ge(sem("kept1"), 16 * (PT_ + 1))
                        eng.wait_ge(sem("kept4"), 16 * (PT_ + 1))
                        eng.dma_start(new_ab[:].rearrange("p a b c -> p (a b c)"), new_ab_d).then_inc(sem("new_masks"), 16)
                    vb, vi = back(b, i, LAG)
                    if alive(vb):
                        load(vb, vi, 1)
            eng.wait_ge(qkv.used, 24)
            eng.wait_ge(sem("pages"), 16)
            over_sequences(eng, body)

        def attend_pool():
            eng = nc.gpsimd
            eng.memset(QB[:], 0.0).then_inc(sem("d_zero"), 1)
            eng.wait_ge(qkv.used, 24)
            eng.memset(QP[:], 0.0).then_inc(sem("d_zero"), 1)
            eng.memset(zeros[:], 0.0).then_inc(sem("d_zero"), 1)
            eng.wait_ge(sem("d_zero"), 3)
            eng.wait_ge(sem("qk_copied"), 4 * (PT_ + 1))
            eng.wait_ge(sem("vout"), 2 * (PT_ + 1))

            def body(b, run):
                pm = mixer_of(b, run)
                for i in quarters(b):
                    if not alive(b):
                        continue
                    m, c = divmod(i, 4)
                    n = QUARTERS * b + i
                    if c == 0:
                        if positive(n - 4):
                            eng.wait_ge(sem("d_sc"), n - 4)
                        for h in range(2):
                            r = slice(h * E, (h + 1) * E)
                            eng.tensor_copy(QB[r, m, :, h * NS:(h + 1) * NS],
                                            QT[r, 4 * m:4 * m + 4, ds(b * NS + NPR, NS)]).then_inc(sem("d_qb"), 1)
                        eng.wait_ge(sem("d_qb"), 4 * b + 2 * m + 2)
                    h, q = step_of(pm, i)
                    r = slice(h * E, (h + 1) * E)
                    if positive(n - 1):
                        eng.wait_ge(sem("p_score"), n - 1)
                    eng.tensor_copy(QP[r, h, q % 2, :], QT[r, ds(b, 1), q * P:(q + 1) * P].rearrange("p a t -> p (a t)")).then_inc(sem("p_query"), 1)
                    eng.wait_ge(sem("p_query"), n + 1)
                    if pm == 1 and i == 6 or pm == 0 and i in (2, 6):
                        hd = head_of(pm, b, i)
                        if positive(hd - (pm == 0)):
                            eng.wait_ge(sem("p_pv"), hd - (pm == 0))
                        if pm == 1:
                            src = V[:, 1, 0:PT_, ds(b * P - 4 * P, P)]
                        else:
                            src = V[:, 0, 0:PT_, ds(b * P + i // 4 * E, E)]
                        eng.tensor_copy(head_values(pm, i)[:, :, 0:(P if pm else E)], src).then_inc(sem("p_values"), 1)
                        eng.wait_ge(sem("p_values"), hd + 1)
            over_sequences(eng, body)

        def attend_tensor():
            pe = nc.tensor
            pe.wait_ge(sem("qk_copied"), 4 * (PT_ + 1))
            pe.wait_ge(sem("vout"), 2 * (PT_ + 1))

            def turn_keys(b, i, f):
                m, c = divmod(i, 4)
                nt, kw = CH[m][c], keys_of(m, tile0(m, c))
                q = QUARTERS * b + i
                if f == 0:
                    pe.wait_ge(sem(f"k_landed{c % 2}"), landed_at(b, m, c))
                if positive(2 * q + f // 2):
                    pe.wait_ge(sem("d_kcv" if f % 2 else "d_kca"), 2 * q + f // 2)
                for k in range(nt):
                    mm = pe.transpose(ps[:, f % 2, k * kw:(k + 1) * kw], kv(c % 2)[0:kw, k, f * P:(f + 1) * P], ident[0:kw, 0:kw])
                mm.then_inc(sem("d_kt"), 1)

            def scores(b, i):
                m, c = divmod(i, 4)
                w, q = chunk_keys(m, c), QUARTERS * b + i
                pe.wait_ge(sem("d_kca"), 2 * q + 2)
                pe.wait_ge(sem("d_kcv"), 2 * q + 2)
                if positive(q):
                    pe.wait_ge(sem("d_smax"), q)
                for f in range(4):
                    mm = pe.matmul(ps[32 * f:32 * f + 32, 2, 0:w], QB[:, m, f, :], KC[:, f, 0:w], start=True, stop=True,
                                   tile_position=(0, 32 * f))
                mm.then_inc(sem("d_sc"), 1)

            def scores_new(b, i):
                m = i // 4
                pe.wait_ge(sem("d_qb"), 4 * b + 2 * m + 2)
                pe.wait_ge(sem("p_max"), QUARTERS * b + i + 1)
                for f in range(4):
                    mm = pe.matmul(ps[32 * f:32 * f + 32, 5, 0:NSM], QB[:, m, f, :], KT[:, 4 * m + f, NPR:T], start=True, stop=True,
                                   tile_position=(0, 32 * f))
                mm.then_inc(sem("d_snew"), 1)

            def turn_weights(b, i, new):
                m, c = divmod(i, 4)
                u = 2 * b + m
                if c == 0 and not new:
                    pe.wait_ge(sem("d_exp"), u + 1)
                if not new and positive(5 * u + c):
                    pe.wait_ge(sem("d_ptc"), 5 * u + c + (c > 0))
                if new:
                    mm = pe.transpose(ps[0:NSM, 3, 0:P], S[m][:, WID[m]:WID[m] + NSM], ident[:])
                else:
                    t0, kw = tile0(m, c), keys_of(m, tile0(m, c))
                    for k in range(CH[m][c]):
                        o = key0(m, t0 + k)
                        mm = pe.transpose(ps[0:kw, 3, k * P:(k + 1) * P], S[m][:, o:o + kw], ident[:])
                mm.then_inc(sem("d_pt"), 1)

            def values(b, i):
                m, c = divmod(i, 4)
                u = 2 * b + m
                pe.wait_ge(sem(f"v_landed{c % 2}"), landed_at(b, m, c))
                pe.wait_ge(sem("d_ptc"), 5 * u + c + 2)
                if c == 0 and positive(2 * u):
                    pe.wait_ge(sem("d_out"), 2 * u)
                for k in range(CH[m][c]):
                    tile = tile0(m, c) + k
                    kw = keys_of(m, tile)
                    for f in range(4):
                        mm = pe.matmul(ps[32 * f:32 * f + 32, 4, 0:P], PTd[0:kw, tile, 32 * f:32 * f + 32],
                                       kv(2 + c % 2)[0:kw, k, f * P:(f + 1) * P], start=(tile == 0), stop=(tile == sum(CH[m]) - 1),
                                       tile_position=(0, 32 * f), skip_group_check=True)
                    if tile == 0:
                        for f in range(4):
                            pe.matmul(ps[32 * f:32 * f + 32, 4, 0:P], PTd[0:NSM, NPAGE, 32 * f:32 * f + 32],
                                      V[0:NSM, m, PT_, f * P:(f + 1) * P], start=False, stop=False,
                                      tile_position=(0, 32 * f), skip_group_check=True)
                mm.then_inc(sem("d_pv"), 1)

            def prompt_score(b, i, pm):
                h, q = step_of(pm, i)
                n, w = QUARTERS * b + i, (q + 1) * P
                pe.wait_ge(sem("p_query"), n + 1)
                if positive(n):
                    pe.wait_ge(sem("p_max"), n)
                if i % 4 == 1:
                    pe.wait_ge(sem("d_new"), 2 * b + i // 4 + 1)
                pe.matmul(ps[:, 5, 0:w], QP[:, h, q % 2, :], KT[:, ds(b, 1), 0:w].rearrange("p a t -> p (a t)"), start=True,
                          stop=True).then_inc(sem("p_score"), 1)

            def prompt_turn(b, i, pm):
                h, q = step_of(pm, i)
                r = turn_of(pm, b, i)
                pe.wait_ge(sem("p_norm"), r + 1)
                if positive(r):
                    pe.wait_ge(sem("p_copied"), r)
                src = (i - pm) % 4
                for kt in range(q + 1):
                    mm = pe.transpose(ps[:, 6, kt * P:(kt + 1) * P], PP[:, src, kt * P:(kt + 1) * P], ident[:])
                mm.then_inc(sem("p_turn"), 1)

            def prompt_values(b, i, pm):
                hd = head_of(pm, b, i)
                pe.wait_ge(sem("p_copied"), PT_ * hd + PT_)
                pe.wait_ge(sem("p_values"), hd + 1)
                if positive(hd):
                    pe.wait_ge(sem("p_out"), hd)
                for kt in range(PT_):
                    wv = P if pm else E
                    out = ps[:, 7, kt * P:NPR] if pm else ps[i // 4 * E:(i // 4 + 1) * E, 7, kt * P:NPR]
                    mm = pe.matmul(out, head_values(pm, i)[:, kt, 0:wv], turned(pm, i)[:, kt, kt * P:NPR], start=(kt == 0), stop=(kt == PT_ - 1),
                                   skip_group_check=True)
                mm.then_inc(sem("p_pv"), 1)

            def body(b, run):
                for i in quarters(b):
                    lb, li = back(b, i, LAG)
                    if alive(b):
                        turn_keys(b, i, 0)
                        turn_keys(b, i, 1)
                    if i % 4 == 1 and alive(b - 1):
                        pe.wait_ge(sem("d_on"), 2 * (b - 1) + i // 4 + 1)
                        pe.transpose(ps[:, 4, P:2 * P], On[:], ident[:]).then_inc(sem("d_ot"), 1)
                    if alive(b):
                        prompt_score(b, i, mixer_of(b, run))
                    if alive(lb):
                        turn_weights(lb, li, False)
                    if alive(b):
                        turn_keys(b, i, 2)
                    if alive(lb) and li % 4 == 0:
                        pe.wait_ge(sem("d_ptc"), 5 * (2 * lb + li // 4) + 1)
                    if alive(b):
                        turn_keys(b, i, 3)
                    if alive(lb) and li % 4 == 0:
                        turn_weights(lb, li, True)
                    if alive(b) and i % 4 == 0:
                        scores_new(b, i)
                    tb, ti = back(b, i, 1)
                    if alive(tb) and is_turn(mixer_of(tb, run), ti):
                        prompt_turn(tb, ti, mixer_of(tb, run))
                    if alive(lb):
                        values(lb, li)
                    if alive(b):
                        scores(b, i)
                    hb, hi_ = back(b, i, 2)
                    if alive(hb) and ends_head(mixer_of(hb, run), hi_):
                        prompt_values(hb, hi_, mixer_of(hb, run))
            over_sequences(pe, body)

        def attend_scalar():
            eng = nc.scalar
            col = lambda k, i: stat[:, k + i % 4:k + i % 4 + 1]

            def evacuate(b, i, f):
                m, c = divmod(i, 4)
                w, q = chunk_keys(m, c), QUARTERS * b + i
                eng.wait_ge(sem("d_kt"), 4 * q + f + 1)
                if f == 0 and positive(q):
                    eng.wait_ge(sem("d_sc"), q)
                eng.activation(KC[:, f, 0:w], ps[:, 0, 0:w], ACT.Copy).then_inc(sem("d_kca"), 1)

            def prompt_exp(b, i, pm):
                n, w = QUARTERS * b + i, (step_of(pm, i)[1] + 1) * P
                eng.wait_ge(sem("p_neg"), n + 1)
                eng.activation(PP[:, i % 4, 0:w], PP[:, i % 4, 0:w], ACT.Exp, bias=col(12, i), scale=1.0,
                               accum_out=col(16, i)).then_inc(sem("p_exp"), 1)

            def prompt_copy(b, i, pm):
                h, q = step_of(pm, i)
                eng.wait_ge(sem("p_turn"), turn_of(pm, b, i) + 1)
                free = head_of(pm, b, i) - (pm == 0)
                if q == 0 and positive(free):
                    eng.wait_ge(sem("p_pv"), free)
                src = ps[:, 6, 0:(q + 1) * P].rearrange("p (k t) -> p k t", t=P)
                eng.activation(turned(pm, i)[:, 0:q + 1, q * P:(q + 1) * P], src, ACT.Copy).then_inc(sem("p_copied"), 1)

            def copy_weights(b, i, new):
                m, c = divmod(i, 4)
                u = 2 * b + m
                g = 1 if new else c + (c > 0)
                eng.wait_ge(sem("d_pt"), 5 * u + g + 1)
                if positive(4 * u + c - 3) and not new:
                    eng.wait_ge(sem("d_pv"), 4 * u + c - 3)
                if new:
                    eng.activation(PTd[0:NSM, NPAGE, :], ps[0:NSM, 3, 0:P], ACT.Copy).then_inc(sem("d_ptc"), 1)
                else:
                    t0, nt, kw = tile0(m, c), CH[m][c], keys_of(m, tile0(m, c))
                    eng.activation(PTd[0:kw, t0:t0 + nt, :], ps[0:kw, 3, 0:nt * P].rearrange("p (t r) -> p t r", r=P),
                                   ACT.Copy).then_inc(sem("d_ptc"), 1)

            def exp(b, m):
                w = WID[m] + NSM
                eng.wait_ge(sem("d_neg"), 2 * b + m + 1)
                eng.activation(S[m][:, 0:w], S[m][:, 0:w], ACT.Exp, bias=stat[:, 41:42], scale=1.0,
                               accum_out=stat[:, 42:43]).then_inc(sem("d_exp"), 1)

            def body(b, run):
                for i in quarters(b):
                    lb, li = back(b, i, LAG)
                    tb, ti = back(b, i, 1)
                    if alive(b):
                        evacuate(b, i, 0)
                        prompt_exp(b, i, mixer_of(b, run))
                    if alive(lb):
                        copy_weights(lb, li, False)
                    if alive(b):
                        evacuate(b, i, 2)
                    if alive(lb) and li % 4 == 0:
                        copy_weights(lb, li, True)
                    if alive(tb) and is_turn(mixer_of(tb, run), ti):
                        prompt_copy(tb, ti, mixer_of(tb, run))
                    if i % 4 == 0 and alive(tb):
                        exp(tb, ti // 4)
            for g in (1, 4):
                eng.wait_ge(sem(f"kept{g}"), 16 * (PT_ + 1))
            over_sequences(eng, body)

        def attend_vector():
            eng = nc.vector
            col = lambda k, i: stat[:, k + i % 4:k + i % 4 + 1]

            def evacuate(b, i, f):
                m, c = divmod(i, 4)
                w, q = chunk_keys(m, c), QUARTERS * b + i
                eng.wait_ge(sem("d_kt"), 4 * q + f + 1)
                if f == 1 and positive(q):
                    eng.wait_ge(sem("d_sc"), q)
                eng.tensor_copy(KC[:, f, 0:w], ps[:, 1, 0:w]).then_inc(sem("d_kcv"), 1)

            def prompt_top(b, i, pm):
                n, w = QUARTERS * b + i, (step_of(pm, i)[1] + 1) * P
                mask = (mask_b if pm else mask_a)[:, NPR - w:NPR]
                if positive(n):
                    eng.wait_ge(sem("p_neg"), n)
                eng.wait_ge(sem("p_score"), n + 1)
                eng.tensor_tensor_reduce(out=PP[:, i % 4, 0:w], in0=ps[:, 5, 0:w], in1=mask, scale=1.0, scalar=MASKED,
                                         op0=ALU.add, op1=ALU.max, accum_out=col(8, i)).then_inc(sem("p_max"), 1)
                eng.wait_ge(sem("p_max"), n + 1)
                eng.tensor_scalar(col(12, i), col(8, i), -1.0, None, ALU.mult).then_inc(sem("p_neg"), 1)

            def prompt_norm(b, i, pm):
                h, q = step_of(pm, i)
                n, w = QUARTERS * b + i, (q + 1) * P
                eng.wait_ge(sem("p_exp"), n + 1)
                eng.reciprocal(col(20, i), col(16, i)).then_inc(sem("p_rl"), 1)
                eng.wait_ge(sem("p_rl"), n + 1)
                own, first = PP[:, i % 4, 0:w], PP[:, (i - 1) % 4, 0:w]
                if pm == 0:
                    eng.tensor_scalar(own, own, col(20, i), None, ALU.mult).then_inc(sem("p_norm"), 1)
                elif h == 1:
                    eng.tensor_scalar(own, own, col(20, i), stat[:, 3:4], ALU.mult, ALU.mult).then_inc(sem("p_second"), 1)
                    eng.wait_ge(sem("p_second"), 4 * b - 16 + q + 1)
                    eng.scalar_tensor_tensor(out=first, in0=first, scalar=col(20, i - 1), in1=own,
                                             op0=ALU.mult, op1=ALU.add).then_inc(sem("p_norm"), 1)

            def prompt_out(b, i, pm):
                h = i // 4
                r = slice(0, P) if pm == 1 else slice(h * E, (h + 1) * E)
                eng.wait_ge(sem("p_pv"), head_of(pm, b, i) + 1)
                eng.tensor_copy(QT[r, ds(b, 1), 0:NPR].rearrange("p a t -> p (a t)"), ps[r, 7, :]).then_inc(sem("p_out"), 1)

            def top(b, i):
                m, c = divmod(i, 4)
                w, o = chunk_keys(m, c), key0(m, tile0(m, c))
                bias = past_a[:, o:o + w] if m == 0 else zeros[:, 0:w]
                eng.wait_ge(sem("d_sc"), QUARTERS * b + i + 1)
                eng.tensor_tensor_reduce(out=S[m][:, o:o + w], in0=ps[:, 2, 0:w], in1=bias, scale=1.0, scalar=MASKED,
                                         op0=ALU.add, op1=ALU.max, accum_out=stat[:, 32 + c:33 + c]).then_inc(sem("d_smax"), 1)

            def body(b, run):
                for i in quarters(b):
                    m, c = divmod(i, 4)
                    u = 2 * b + m
                    o = WID[m]
                    if c == 1 and alive(b - 1):
                        eng.wait_ge(sem("d_rl"), u - 1)
                        eng.wait_ge(sem("d_pv"), 4 * (u - 2) + 4)
                        eng.tensor_scalar(On[:], ps[:, 4, 0:P], stat[:, 43 + m:44 + m], None, ALU.mult).then_inc(sem("d_on"), 1)
                    if alive(b):
                        evacuate(b, i, 1)
                    if c == 1 and alive(b - 1):
                        eng.wait_ge(sem("d_ot"), u - 1)
                        turned_o = ps[:, 4, P:2 * P].rearrange("p (f x) -> p f x", f=4)
                        cols = ds(b * NS + NPR - NS, NS)
                        if m == 0:
                            for h in range(2):
                                r = slice(h * E, (h + 1) * E)
                                eng.tensor_copy(QT[r, 0:4, cols], turned_o[r, :, h * NS:(h + 1) * NS]).then_inc(sem("d_out"), 1)
                        else:
                            eng.tensor_scalar(part[:], turned_o[:, :, NS:2 * NS], stat[:, 3:4], None, ALU.mult).then_inc(sem("d_out"), 1)
                            eng.wait_ge(sem("d_out"), 2 * (u - 2) + 1)
                            eng.tensor_tensor(QT[:, 4:8, cols], part[:], turned_o[:, :, 0:NS], ALU.add).then_inc(sem("d_out"), 1)
                    if alive(b):
                        prompt_top(b, i, mixer_of(b, run))
                    pb, pi = back(b, i, 2)
                    if c == 1 and alive(pb):
                        eng.wait_ge(sem("d_exp"), u)
                        eng.reciprocal(stat[:, 44 - m:45 - m], stat[:, 42:43]).then_inc(sem("d_rl"), 1)
                    if alive(b):
                        evacuate(b, i, 3)
                        if c == 0:
                            eng.wait_ge(sem("d_snew"), u + 1)
                            eng.tensor_tensor(S[m][:, o:o + NSM], ps[:, 5, 0:NSM], new_ab[:, m, ds(b, 1), :].rearrange("p a k -> p (a k)"),
                                              ALU.add).then_inc(sem("d_new"), 1)
                        prompt_norm(b, i, mixer_of(b, run))
                        if c == 1:
                            eng.wait_ge(sem("d_new"), u + 1)
                            eng.reduce_max(stat[:, 36:37], S[m][:, o:o + NSM], AX_X).then_inc(sem("d_mnew"), 1)
                    hb, hi_ = back(b, i, 3)
                    if alive(hb) and ends_head(mixer_of(hb, run), hi_):
                        prompt_out(hb, hi_, mixer_of(hb, run))
                    if alive(b):
                        top(b, i)
                    if alive(b) and c == 3:
                        eng.wait_ge(sem("d_smax"), QUARTERS * b + i + 1)
                        eng.wait_ge(sem("d_mnew"), u + 1)
                        if positive(u):
                            eng.wait_ge(sem("d_neg"), u)
                            eng.wait_ge(sem("d_rl"), u)
                        eng.reduce_max(stat[:, 40:41], stat[:, 32:37], AX_X).then_inc(sem("d_mall"), 1)
                        eng.wait_ge(sem("d_mall"), u + 1)
                        eng.tensor_scalar(stat[:, 41:42], stat[:, 40:41], -1.0, None, ALU.mult).then_inc(sem("d_neg"), 1)
            eng.wait_ge(sem("d_zero"), 3)
            eng.wait_ge(sem("new_masks"), 16)
            each_sequence(body)

        def mix_tensor():
            pe = nc.tensor
            for i in range(4):
                pe.wait_ge(sem("m_sq"), i + 1)
                for h in range(2):
                    m = pe.matmul(ps[:, 2 * i + h, 0:TH], one_v[:], tmp[:, i % 2, h * TH:(h + 1) * TH], start=True, stop=True)
                m.then_inc(sem("m_mean"), 1)

        def mix_scalar():
            eng = nc.scalar
            eng.wait_ge(sem("d_out"), 4 * NB)
            for i in range(4):
                if i >= 2:
                    eng.wait_ge(sem("m_mean"), i - 1)
                eng.activation(tmp[:, i % 2, :], QT[:, 4 + i, :], ACT.Square).then_inc(sem("m_sq"), 1)
            for i in range(4):
                eng.wait_ge(sem("m_ve"), i + 1)
                eng.activation(tmp[:, 2 + i % 2, :], tmp[:, 2 + i % 2, :], ACT.Sqrt).then_inc(sem("m_std"), 1)
            for d in range(DB):
                if d >= 4:
                    eng.wait_ge(sem("m_rms"), d - 3)
                eng.activation(hhi[:, d, :], QT[:, d, :], ACT.Copy).then_inc(sem("m_hhi"), 1)

        def mix_vector():
            eng = nc.vector
            for i in range(4):
                eng.wait_ge(sem("m_mean"), i + 1)
                if i >= 2:
                    eng.wait_ge(sem("m_rms"), i - 1)
                eng.tensor_scalar(tmp[:, 2 + i % 2, :].rearrange("p (h t) -> p h t", h=2), ps[:, 2 * i:2 * i + 2, 0:TH],
                                  RMS_EPS, None, ALU.add).then_inc(sem("m_ve"), 1)
                eng.wait_ge(sem("m_std"), i + 1)
                eng.reciprocal(tmp[:, 2 + i % 2, :], tmp[:, 2 + i % 2, :]).then_inc(sem("m_rs"), 1)
                eng.wait_ge(sem("m_rs"), i + 1)
                eng.scalar_tensor_tensor(out=QT[:, 4 + i, :], in0=QT[:, 4 + i, :], scalar=stat[:, 4:5], in1=tmp[:, 2 + i % 2, :],
                                         op0=ALU.mult, op1=ALU.mult).then_inc(sem("m_rms"), 1)
            for d in range(DB):
                eng.wait_ge(sem("m_hhi"), d + 1)
                eng.tensor_tensor(hlo[:, d, :], QT[:, d, :], hhi[:, d, :].bitcast(F32), ALU.subtract).then_inc(sem("m_hlo"), 1)

        def end_tensor():
            pe = nc.tensor
            pe.wait_ge(sem("step_x"), 2 * DB + DB)
            for t in range(PT_ + 1):
                n = tokens(t)
                for kg in range(2):
                    i = 2 * t + kg
                    if i >= 8:
                        pe.wait_ge(sem("y_copied"), i - 7)
                    for k in range(4):
                        m = pe.transpose(ps[0:n, i % 8, k * P:(k + 1) * P], xT[:, 4 * kg + k, t * P:t * P + n], ident[:])
                    m.then_inc(sem("y_turned"), 1)

        def end_vector():
            eng = nc.vector
            for i in range(2 * (PT_ + 1)):
                t, kg = divmod(i, 2)
                n = tokens(t)
                eng.wait_ge(sem("y_turned"), i + 1)
                eng.tensor_copy(ytok[0:n, t, kg * 512:(kg + 1) * 512], ps[0:n, i % 8, :]).then_inc(sem("y_copied"), 1)

        def end_sync():
            eng = nc.sync
            for t in range(PT_ + 1):
                eng.wait_ge(sem("y_copied"), 2 * t + 2)
                dst = y_prompt[0, t * P:(t + 1) * P, :] if t < PT_ else y_sample.rearrange("b s d -> (b s) d")
                eng.dma_start(dst, ytok[0:tokens(t), t, :]).then_inc(sem("y_kept"), 16)
            eng.wait_ge(sem("y_kept"), 16 * (PT_ + 1))
            for g in (1, 2, 4, 5):
                eng.wait_ge(sem(f"kept{g}"), 16 * (PT_ + 1))

        @block.sync
        def _(sp):
            start_sync()
            wo_v = w_o.rearrange("l (k p) n -> p (l k) n", p=P)
            ffn_loads(in1, out1, f1_in, f1_out)
            qkv_sync()
            attend_sync()
            sp.wait_ge(sem("p_pv"), HEADS)
            for d in range(DB):
                load_chunk(wo, d, d % 2, wo_v[:, :, d * P:(d + 1) * P], DB)
            ffn_loads(in3, out3, f2_in, f2_out)
            end_sync()

        @block.gpsimd
        def _(pool):
            start_pool()
            scale_residual(0)
            scale_residual(1)
            attend_pool()
            scale_residual(2)

        @block.scalar
        def _(act):
            start_scalar()
            modulate_scalar(0)
            ffn_in_scalar(0, 0, in1)
            project_scalar(0, out1, 2, 0)
            modulate_scalar(1)
            qkv_scalar()
            attend_scalar()
            mix_scalar()
            project_scalar(1, wo, 1, 1)
            modulate_scalar(2)
            ffn_in_scalar(2, 1, in3)
            project_scalar(2, out3, 2, 2)

        @block.vector
        def _(dve):
            start_vector()
            modulate_vector(0, 0, 1)
            ffn_in_vector(0, 0, in1)
            project_vector(0, out1, 2, 2)
            modulate_vector(1, 3, 4)
            qkv_vector()
            attend_vector()
            mix_vector()
            project_vector(1, wo, 1, 5)
            modulate_vector(2, 6, 7)
            ffn_in_vector(2, 1, in3)
            project_vector(2, out3, 2, 8)
            end_vector()

        @block.tensor
        def _(pe):
            start_tensor()
            ffn_in_tensor(0, 0, in1)
            pe.wait_ge(sem("ffn_fflo"), FB)
            project_tensor(0, out1, HB, 2, ffhi, fflo)
            qkv_tensor()
            attend_tensor()
            mix_tensor()
            pe.wait_ge(sem("m_hlo"), DB)
            project_tensor(1, wo, DB, 1, hhi, hlo)
            ffn_in_tensor(2, 1, in3)
            pe.wait_ge(sem("ffn_fflo"), 2 * FB)
            project_tensor(2, out3, HB, 2, ffhi, fflo)
            end_tensor()


_INS = ["x_prompt", "x_sample", "c_prompt", "c_sample", "cache_win_k", "cache_win_v", "cache_diff_k", "cache_diff_v",
        "page_table", "ln_g", "ln_b", "w_ada", "b_ada", "ffn1_w_in", "ffn1_w_out", "ffn2_w_in", "ffn2_w_out",
        "w_qkv", "w_o", "diff_lambda", "subln_g"]
_CONSTS = ["ident", "rope", "mask_a", "mask_b", "past_a", "new_ab"]
_OUTS = [(1, 512, 1024), (8, 8, 1024), (1, 1, 512, 8, 64), (1, 1, 512, 8, 64), (1, 8, 8, 8, 64), (1, 8, 8, 8, 64),
         (1, 1, 4, 128, 4, 2, 64), (1, 1, 4, 128, 4, 128), (1, 8, 8, 4, 2, 64), (1, 8, 8, 4, 128)]


def kernel(**inputs):
    import concourse.bacc as _bacc
    from concourse.bass_utils import run_bass_kernel_spmd as _run

    nc = _bacc.Bacc("TRN2", target_bir_lowering=False, num_devices=1)
    tables = constants()
    arrays, args = {}, []
    for name in _INS + _CONSTS:
        a = np.ascontiguousarray(inputs[name] if name in _INS else tables[name])
        arrays[f"in_{name}_dram"] = a
        args.append(nc.dram_tensor(f"in_{name}_dram", a.shape, mybir.dt.from_np(a.dtype), kind="ExternalInput").ap())
    for i, shape in enumerate(_OUTS):
        args.append(nc.dram_tensor(f"out_{i}_dram", shape, F32, kind="ExternalOutput").ap())
    n = len(_INS + _CONSTS)
    yp, ys, wkp, wvp, wks, wvs, dkp, dvp, dks, dvs = args[n:]
    build(nc, *args[:n], yp, ys, wkp, wvp, wks, wvs, dkp, dvp, dks, dvs)
    r = _run(nc, [arrays], core_ids=[0])
    return tuple(r.results[0][f"out_{i}_dram"] for i in range(len(_OUTS)))
```

```python
import math
from contextlib import ExitStack

import concourse.bass as bass
import numpy as np
from concourse import mybir

F32 = mybir.dt.float32
F32R = mybir.dt.float32r
I32 = mybir.dt.int32
ALU = mybir.AluOpType
ACT = mybir.ActivationFunctionType
AX_X = mybir.AxisListType.X
ds = bass.ds

P = 128
D = 1024
DB = D // P
NPR = 512
PT_ = NPR // P
NB = 8
NS = 8
NSM = NB * NS
T = NPR + NSM
TH = T // 2
FF = 2816
FB = FF // P
HB = FB // 2
NC_ = 1 + NB
NM = 9
QW = 512
E = 64
PAST = 2048
PAGE = 128
NPAGE = PAST // PAGE
ALPHA = 2.0 ** 0.25
LN_EPS = 1e-5
RMS_EPS = 1e-5
LAM_INIT = 0.8 - 0.6 * math.exp(0.0)
SCALE = E ** -0.5
MASKED = -1e30
WCH = HB * P
DENSE = 512
A_NEAR = DENSE // P
A_FAR = 8
FARW = (PAST - DENSE) // 16
A_KEYS = A_FAR * FARW + A_NEAR * P
A_CHUNKS = (4, 4, 2, 2)
B_CHUNKS = (4, 4, 4, 4)
SW = PAST + NSM


def constants():
    inv = (np.float32(10000.0) ** (-np.arange(0, E, 2, dtype=np.float32) / np.float32(E))).astype(np.float32)
    pos = np.concatenate([np.arange(NPR), np.tile(PAST + np.arange(NS), NB)]).astype(np.float32)
    ang = pos[:, None] * inv[None, :]
    rope = np.zeros((P, PT_ + 1, 2, E // 2), np.float32)
    for t in range(PT_ + 1):
        rows = min(P, T - t * P)
        rope[:rows, t, 0] = np.cos(ang[t * P:t * P + rows])
        rope[:rows, t, 1] = np.sin(ang[t * P:t * P + rows])

    def log_count(delta):
        n = ((delta >= 0) & (delta <= 128)).astype(int)
        n += (delta >= 0) & (delta <= 512) & (delta % 4 == 0)
        n += (delta >= 0) & (delta <= 2048) & (delta % 16 == 0)
        return np.where(n > 0, np.log(np.maximum(n, 1)), MASKED).astype(np.float32)

    row, col = np.arange(P)[:, None], np.arange(NPR)[None, :]
    delta = row + (NPR - P) - col
    causal = np.where(delta >= 0, 0.0, MASKED).astype(np.float32)
    far = (np.arange(A_FAR)[:, None] + 16 * np.arange(FARW)[None, :]).ravel()
    near = (PAST - DENSE + np.arange(A_NEAR)[:, None] + A_NEAR * np.arange(P)[None, :]).ravel()
    keys = np.concatenate([far, near])
    query = (np.arange(P) % NS)[:, None]
    past = log_count(PAST + query - keys[None, :])
    new = np.full((P, 2, NB, NSM), MASKED, np.float32)
    own = query - np.arange(NS)[None, :]
    for b in range(NB):
        new[:, 0, b, b * NS:(b + 1) * NS] = log_count(own)
        new[:, 1, b, b * NS:(b + 1) * NS] = np.where(own >= 0, 0.0, MASKED)
    return {
        "ident": np.eye(P, dtype=np.float32), "rope": rope.reshape(P, -1),
        "mask_a": log_count(delta), "mask_b": causal, "past_a": past, "new_ab": new.reshape(P, -1),
    }


def build(nc, x_prompt, x_sample, c_prompt, c_sample, win_k, win_v, diff_k, diff_v, page_table, ln_g, ln_b,
          w_ada, b_ada, f1_in, f1_out, f2_in, f2_out, w_qkv, w_o, diff_lambda, subln_g,
          ident_d, rope_d, mask_a_d, mask_b_d, past_a_d, new_ab_d,
          y_prompt, y_sample, wkp, wvp, wks, wvs, dkp, dvp, dks, dvs):
    with ExitStack() as ctx:
        sems = {}

        def sem(name):
            if name not in sems:
                sems[name] = ctx.enter_context(nc.semaphore(name))
            return sems[name]

        at = [nc.sbuf_base + (-nc.sbuf_base) % 64]

        def place(name, shape, dt=F32, offset=None):
            size = int(np.prod(shape[1:])) * 4
            where = at[0] if offset is None else offset
            if offset is None:
                at[0] += (size + 63) // 64 * 64
            assert where + size <= nc.sbuf_usable_end, name
            return nc.alloc_sbuf_tensor_at(name, shape, dt, offset=where), where + (size + 63) // 64 * 64

        ident, _ = place("ident", [P, P])
        one_d, _ = place("one_d", [P, P])
        one_v, _ = place("one_v", [P, P])
        modT, _ = place("modT", [P, NM, DB, NC_])
        colT, _ = place("colT", [P, 128])
        stat, _ = place("stat", [P, 64])
        colA, _ = place("colA", [P, 48])
        fuse, _ = place("fuse", [P, DB, NC_])
        pages, _ = place("pages", [1, NB * NPAGE], I32)
        xT, _ = place("xT", [P, DB, T])
        wreg = [at[0]]
        w32, o = place("w32", [P, 2, WCH])
        wreg.append(o)
        whi, o = place("whi", [P, 2, WCH], F32R)
        wreg.append(o)
        wlo, treg = place("wlo", [P, 2, WCH], F32R)
        tmp, _ = place("tmp", [P, 4, T])
        hreg = at[0]
        hhi, _ = place("hhi", [P, DB, T], F32R)
        hlo, hend = place("hlo", [P, DB, T], F32R)
        freg = at[0]
        ffhi, _ = place("ffhi", [P, FB, T], F32R)
        fflo, fend = place("fflo", [P, FB, T], F32R)
        xtok, o = place("xtok", [P, PT_ + 1, D], offset=freg)
        wada, o = place("wada", [P, 4, DB // 2, D], offset=o)
        assert o <= fend
        ctok, o = place("ctok", [NC_, D], offset=hreg)
        csil, o = place("csil", [NC_, D], offset=o)
        cT, o = place("cT", [P, DB, 32], offset=o)
        rows, o = place("rows", [P, P], offset=o)
        modrow, o = place("modrow", [P, 2, 256], offset=o)
        lamb, o = place("lamb", [P, 4, E], offset=o)
        lamp, o = place("lamp", [P, 2, E], offset=o)
        assert o <= hend
        QT, o = place("QT", [P, 8, T], offset=freg)
        KT, o = place("KT", [P, 8, T], offset=o)
        V, o = place("V", [P, 2, PT_ + 1, QW], offset=o)
        QB, o = place("QB", [P, 2, 4, 32], offset=o)
        PTo = o
        rot, o = place("rot", [P, PT_ + 1, QW], offset=o)
        rab, o = place("rab", [P, 2, QW], offset=o)
        PTd, o3 = place("PTd", [P, NPAGE + 1, P], offset=PTo)
        new_ab, o4 = place("new_ab", [P, 2, NB, NSM], offset=o3)
        o = max(o, o4)
        kv01, o = place("kv01", [P, 2, 4, QW], offset=o)
        ropet, o = place("ropet", [P, PT_ + 1, 2, E // 2], offset=o)
        mask_a, o = place("mask_a", [P, NPR], offset=o)
        mask_b, o = place("mask_b", [P, NPR], offset=o)
        past_a, o = place("past_a", [P, A_KEYS], offset=o)
        assert o <= fend
        kv23, o = place("kv23", [P, 2, 4, QW], offset=hreg)
        KC, o = place("KC", [P, 4, QW], offset=o)
        S0, o = place("S0", [P, SW], offset=o)
        On, o = place("On", [P, P], offset=o)
        zeros, o = place("zeros", [P, NPR], offset=o)
        part, o = place("part", [P, 4, NS], offset=o)
        assert o <= hend
        S1, o = place("S1", [P, SW], offset=treg)
        assert o <= hreg
        S = (S0, S1)
        PTp0, o = place("PTp0", [P, PT_, NPR], offset=wreg[0])
        VH0, o = place("VH0", [P, PT_, P], offset=o)
        assert o <= wreg[1]
        PP, o = place("PP", [P, 4, NPR], offset=wreg[1])
        QP, o = place("QP", [P, 2, 2, P], offset=o)
        assert o <= wreg[2]
        PTp1, o = place("PTp1", [P, PT_, NPR], offset=wreg[2])
        VH1, o = place("VH1", [P, PT_, P], offset=o)
        assert o <= treg
        ytok, o = place("ytok", [P, PT_ + 1, D], offset=freg)

        def kv(slot):
            return kv01[:, slot] if slot < 2 else kv23[:, slot - 2]

        ps = ctx.enter_context(nc.psum_tensor("ps", [P, 8, 512], F32))

        block = ctx.enter_context(nc.Block())

        def pairs(eng, n, body, tail=0):
            body(0, 0)
            body(1, 1)
            with eng.Fori(1, n // 2 - tail) as i:
                body(2 * i, 0)
                body(2 * i + 1, 1)
            for s in range(n - 2 * tail, n):
                body(s, s % 2)

        class Weights:
            def __init__(self, name, chunks, width, before, run=0):
                self.chunks, self.width, self.before, self.base = chunks, width, before, run * chunks
                self.landed = [sem(f"{name}_landed{slot}") for slot in range(2)]
                self.hi, self.lo, self.used = sem(name + "_hi"), sem(name + "_lo"), sem(name + "_used")

        in1 = Weights("w_in", 2 * FB, DB * P, None)
        out1 = Weights("w_out", 2 * DB, HB * P, in1)
        qkv = Weights("w_qkv", 24, 2 * QW, out1)
        wo = Weights("w_o", DB, DB * P, qkv)
        in3 = Weights("w_in", 2 * FB, DB * P, wo, run=1)
        out3 = Weights("w_out", 2 * DB, HB * P, in3, run=1)

        def load_chunk(ph, c, slot, src, nk):
            if not (isinstance(c, int) and c < 2):
                nc.sync.wait_ge(ph.lo, ph.base + c - 1)
            elif ph.before:
                nc.sync.wait_ge(ph.before.lo, ph.before.base + ph.before.chunks - 1 + c)
            dst = w32[:, slot, 0:ph.width].rearrange("p (k n) -> p k n", k=nk)
            nc.sync.dma_start(dst, src).then_inc(ph.landed[slot], 16)

        def split_hi(ph, c, slot):
            n = c // 2 * 16 if isinstance(c, int) else (c - slot) * 8
            nc.scalar.wait_ge(ph.landed[slot], 8 * ph.base + n + 16)
            if not (isinstance(c, int) and c < 2):
                nc.scalar.wait_ge(ph.used, ph.base + c - 1)
            elif ph.before:
                nc.scalar.wait_ge(ph.before.used, ph.before.base + ph.before.chunks - 1 + c)
            w = ph.width
            nc.scalar.activation(whi[:, slot, 0:w], w32[:, slot, 0:w], ACT.Copy).then_inc(ph.hi, 1)

        def split_lo(ph, c, slot):
            nc.vector.wait_ge(ph.hi, ph.base + c + 1)
            w = ph.width
            nc.vector.tensor_tensor(wlo[:, slot, 0:w], w32[:, slot, 0:w], whi[:, slot, 0:w].bitcast(F32),
                                    ALU.subtract).then_inc(ph.lo, 1)

        def chunk_products(ph, slot, nk, xhi, xlo, k0, kall, banks, halves=None):
            pe = nc.tensor
            m = None
            for k in range(nk):
                kk = k0 + k
                if halves:
                    pe.wait_ge(sem(halves[0]), halves[1] + kk + 1)
                wh = whi[:, slot, k * P:(k + 1) * P]
                wl = wlo[:, slot, k * P:(k + 1) * P]
                for n, (w, x) in enumerate(((wh, xhi), (wh, xlo), (wl, xhi))):
                    for h in range(2):
                        m = pe.matmul(ps[:, banks + h, 0:TH], w, x[:, kk, h * TH:(h + 1) * TH],
                                      start=(kk == 0 and n == 0), stop=(kk == kall - 1 and n == 2))
            m.then_inc(ph.used, 1)

        def fuse_affine(st):
            eng = nc.gpsimd
            a, b = modT[:, 3 * st + 1, :, :], modT[:, 3 * st, :, :]
            wide = lambda c: colT[:, c + (st - 1) * DB:c + st * DB].unsqueeze(2).to_broadcast([P, DB, NC_])
            eng.tensor_tensor(fuse[:], a, wide(96), ALU.mult).then_inc(sem("fused"), 1)
            eng.wait_ge(sem("fused"), 3 * st - 2)
            eng.tensor_tensor(b, b, fuse[:], ALU.add).then_inc(sem("fused"), 1)
            eng.tensor_tensor(a, a, wide(72), ALU.mult).then_inc(sem("fused"), 1)
            eng.wait_ge(sem("fused"), 3 * st)

        def modulate_vector(st):
            eng = nc.vector
            def normalise(d):
                if st > 0:
                    eng.tensor_tensor(xT[:, d, 0:NPR], xT[:, d, 0:NPR], tmp[:, 3, 0:NPR], ALU.mult).then_inc(sem("step_nrm"), 1)
            if st > 0:
                eng.tensor_tensor(xT[:, :, NPR:T], xT[:, :, NPR:T], tmp[:, 3, NPR:T].unsqueeze(1).to_broadcast([P, DB, NSM]),
                                  ALU.mult).then_inc(sem("step_snrm"), 1)
            normalise(0)
            for d in range(DB):
                if d + 1 < DB:
                    normalise(d + 1)
                eng.wait_ge(sem("step_hhi"), st * DB + d + 1)
                if d >= 2:
                    eng.wait_ge(sem("step_hlo"), st * DB + d - 1)
                eng.scalar_tensor_tensor(out=tmp[:, d % 2, 0:NPR], in0=xT[:, d, 0:NPR], scalar=modT[:, 3 * st + 1, d, 0:1],
                                         in1=hhi[:, d, 0:NPR].bitcast(F32), op0=ALU.mult,
                                         op1=ALU.subtract).then_inc(sem("step_rest"), 1)
                if d == 3:
                    eng.wait_ge(sem("step_shi"), st + 1)
                    eng.tensor_tensor(hlo[:, :, NPR:T], tmp[:, 2, 0:DB * NSM].rearrange("p (d s) -> p d s", s=NSM),
                                      hhi[:, :, NPR:T].bitcast(F32), ALU.subtract).then_inc(sem("step_slo"), 1)

        def modulate_scalar(st):
            eng = nc.scalar
            def lower(d):
                eng.wait_ge(sem("step_rest"), st * DB + d + 1)
                eng.activation(hlo[:, d, 0:NPR], tmp[:, d % 2, 0:NPR], ACT.Identity, bias=modT[:, 3 * st, d, 0:1],
                               scale=1.0).then_inc(sem("step_hlo"), 1)
            if st == 0:
                eng.wait_ge(sem("mods"), 2)
            else:
                eng.wait_ge(sem("fused"), 3 * st)
            for d in range(DB):
                if st > 0:
                    eng.wait_ge(sem("step_nrm"), (st - 1) * DB + d + 1)
                else:
                    eng.wait_ge(sem("x_copied"), d + 1)
                eng.activation(hhi[:, d, 0:NPR], xT[:, d, 0:NPR], ACT.Identity, bias=modT[:, 3 * st, d, 0:1],
                               scale=modT[:, 3 * st + 1, d, 0:1]).then_inc(sem("step_hhi"), 1)
                if d >= 1:
                    lower(d - 1)
                if d == 3:
                    eng.wait_ge(sem("step_sh"), 2 * st + 2)
                    eng.activation(hhi[:, :, NPR:T], tmp[:, 2, 0:DB * NSM].rearrange("p (d s) -> p d s", s=NSM),
                                   ACT.Copy).then_inc(sem("step_shi"), 1)
            lower(DB - 1)

        def modulate_pool(st):
            eng = nc.gpsimd
            if st == 0:
                eng.wait_ge(sem("xs_copied"), 1)
                eng.wait_ge(sem("mods"), 2)
            else:
                eng.wait_ge(sem("step_snrm"), st)
            hs = tmp[:, 2, 0:DB * NSM].rearrange("p (d b s) -> p d b s", b=NB, s=NS)
            xs = xT[:, :, NPR:T].rearrange("p d (b s) -> p d b s", s=NS)
            wide = lambda i: modT[:, i, :, 1:NC_].unsqueeze(3).to_broadcast([P, DB, NB, NS])
            eng.tensor_tensor(hs, xs, wide(3 * st + 1), ALU.mult).then_inc(sem("step_sh"), 1)
            eng.wait_ge(sem("step_sh"), 2 * st + 1)
            eng.tensor_tensor(hs, hs, wide(3 * st), ALU.add).then_inc(sem("step_sh"), 1)
            eng.wait_ge(sem("step_sh"), 2 * st + 2)
            eng.wait_ge(sem("step_rest"), st * DB + DB)
            for d in range(DB):
                g = colA[:, (st - 1) * DB + d:(st - 1) * DB + d + 1] if st else ALPHA
                b = colA[:, 24 + (st - 1) * DB + d:25 + (st - 1) * DB + d] if st else 0.0
                eng.tensor_scalar(xT[:, d, :], xT[:, d, :], g, b, ALU.mult, ALU.add).then_inc(sem("step_xa"), 1)

        def project_tensor(st, ph, nk_chunk, n_half, xhi, xlo, halves=None):
            pe = nc.tensor
            kall = nk_chunk * n_half
            def body(d, par):
                if not (isinstance(d, int) and d < 2):
                    pe.wait_ge(sem("step_res"), st * DB + d - 1)
                for hh in range(n_half):
                    slot = hh if n_half == 2 else par
                    pe.wait_ge(ph.lo, ph.base + n_half * d + hh + 1)
                    first = isinstance(d, int) and d == 0
                    chunk_products(ph, slot, nk_chunk, xhi, xlo, hh * nk_chunk, kall, 2 * par, halves if first else None)
            pairs(pe, DB, body)
            pe.wait_ge(sem("step_acc"), (st + 1) * (DB - 1))
            for h in range(2):
                m = pe.matmul(ps[:, 4 + h, 0:TH], one_d[:], tmp[:, 3, h * TH:(h + 1) * TH], start=True, stop=True)
            m.then_inc(sem("step_mean"), 1)
            for d in range(DB):
                pe.wait_ge(sem("step_sq"), st * DB + d + 1)
                for h in range(2):
                    m = pe.matmul(ps[:, 6 + h, 0:TH], one_d[:], tmp[:, d % 3, h * TH:(h + 1) * TH],
                                  start=(d == 0), stop=(d == DB - 1))
                m.then_inc(sem("step_var"), 1)

        def project_vector(st, ph, n_half, i_gate, after):
            eng = nc.vector
            n = DB * n_half
            if n_half == 2:
                split_lo(ph, 0, 0)
                split_lo(ph, 1, 1)
            for d in range(DB):
                if n_half == 2 and 2 * d + 2 < n:
                    split_lo(ph, 2 * d + 2, 0)
                eng.wait_ge(ph.used, ph.base + n_half * (d + 1))
                eng.wait_ge(sem("step_xa"), st * DB + d + 1)
                b = 2 * (d % 2)
                gate = modT[:, i_gate, d, 0:1]
                eng.scalar_tensor_tensor(out=xT[:, d, 0:TH], in0=ps[:, b, 0:TH], scalar=gate, in1=xT[:, d, 0:TH],
                                         op0=ALU.mult, op1=ALU.add)
                eng.scalar_tensor_tensor(out=xT[:, d, TH:NPR], in0=ps[:, b + 1, 0:NPR - TH], scalar=gate,
                                         in1=xT[:, d, TH:NPR], op0=ALU.mult, op1=ALU.add)
                if d >= 1:
                    eng.wait_ge(sem("step_res"), st * DB + d)
                gs = tmp[:, 2, 0:NSM].rearrange("p (b s) -> p b s", s=NS)
                eng.tensor_tensor(gs, ps[:, b + 1, NPR - TH:TH].rearrange("p (b s) -> p b s", s=NS),
                                  modT[:, i_gate, d, 1:NC_].unsqueeze(2).to_broadcast([P, NB, NS]),
                                  ALU.mult).then_inc(sem("step_gs"), 1)
                eng.wait_ge(sem("step_gs"), st * DB + d + 1)
                eng.tensor_tensor(xT[:, d, NPR:T], xT[:, d, NPR:T], tmp[:, 2, 0:NSM],
                                  ALU.add).then_inc(sem("step_res"), 1)
                if n_half == 2 and 2 * d + 3 < n:
                    split_lo(ph, 2 * d + 3, 1)
                if n_half == 1 and d + 2 < n:
                    split_lo(ph, d + 2, d % 2)
                if d >= 1:
                    if d >= 2:
                        eng.wait_ge(sem("step_acc"), st * (DB - 1) + d - 1)
                    eng.wait_ge(sem("step_res"), st * DB + d + 1)
                    eng.tensor_tensor(tmp[:, 3, :], xT[:, 0, :] if d == 1 else tmp[:, 3, :], xT[:, d, :],
                                      ALU.add).then_inc(sem("step_acc"), 1)
            if after:
                split_lo(after, 0, 0)
            eng.wait_ge(sem("step_mean"), st + 1)
            halves = lambda ap: ap.rearrange("p (h t) -> p h t", h=2)
            for d in range(DB):
                eng.tensor_tensor(halves(xT[:, d, :]), halves(xT[:, d, :]), ps[:, 4:6, 0:TH],
                                  ALU.subtract).then_inc(sem("step_cen"), 1)
            if after:
                split_lo(after, 1, 1)
            eng.wait_ge(sem("step_std"), st + 1)
            eng.reciprocal(tmp[:, 3, :], tmp[:, 3, :]).then_inc(sem("step_rs"), 1)
            eng.wait_ge(sem("step_rs"), st + 1)
            if st == 2:
                for d in range(DB):
                    eng.tensor_tensor(xT[:, d, :], xT[:, d, :], tmp[:, 3, :], ALU.mult).then_inc(sem("step_nrm"), 1)

        def project_scalar(st, ph, n_half, i_ln, after):
            eng = nc.scalar
            for c in range(0 if n_half == 2 else 2, DB * n_half):
                split_hi(ph, c, c % 2)
            if after:
                split_hi(after, 0, 0)
                split_hi(after, 1, 1)
            for d in range(DB):
                eng.wait_ge(sem("step_cen"), st * DB + d + 1)
                if d >= 3:
                    eng.wait_ge(sem("step_var"), st * DB + d - 2)
                eng.activation(tmp[:, d % 3, :], xT[:, d, :], ACT.Square).then_inc(sem("step_sq"), 1)
            eng.wait_ge(sem("step_var"), st * DB + DB)
            eng.activation(tmp[:, 3, :].rearrange("p (h t) -> p h t", h=2), ps[:, 6:8, 0:TH], ACT.Sqrt,
                           bias=stat[:, 5:6], scale=1.0).then_inc(sem("step_std"), 1)
            for d in range(DB if st == 2 else 0):
                eng.wait_ge(sem("step_nrm"), st * DB + d + 1)
                g = colT[:, 72 + i_ln * DB + d:73 + i_ln * DB + d]
                b = colT[:, 96 + i_ln * DB + d:97 + i_ln * DB + d]
                eng.activation(xT[:, d, :], xT[:, d, :], ACT.Identity, bias=b, scale=g).then_inc(sem("step_x"), 1)

        def ffn_in_tensor(st, ffn, ph):
            pe = nc.tensor
            pe.wait_ge(sem("step_slo"), st + 1)
            def body(j, par):
                for gu in range(2):
                    if not (isinstance(j, int) and j < 2):
                        pe.wait_ge(sem("ffn_mul" if gu else "ffn_silu"), ffn * FB + j - 1)
                    pe.wait_ge(ph.lo, ph.base + 2 * j + gu + 1)
                    first = isinstance(j, int) and j == gu == 0
                    chunk_products(ph, gu, DB, hhi, hlo, 0, DB, 4 * par + 2 * gu, ("step_hlo", st * DB) if first else None)
            pairs(pe, FB, body)

        def ffn_in_scalar(st, ffn, ph):
            eng = nc.scalar
            def body(j, par):
                last = isinstance(j, int) and j == FB - 1
                if not last:
                    split_hi(ph, 2 * j + 2, 0)
                eng.wait_ge(ph.used, ph.base + 2 * j + 1)
                if not (isinstance(j, int) and j < 2):
                    eng.wait_ge(sem("ffn_mul"), ffn * FB + j - 1)
                eng.activation(tmp[:, par, :].rearrange("p (h t) -> p h t", h=2), ps[:, 4 * par:4 * par + 2, 0:TH],
                               ACT.Silu).then_inc(sem("ffn_silu"), 1)
                if not last:
                    split_hi(ph, 2 * j + 3, 1)
                eng.wait_ge(sem("ffn_mul"), ffn * FB + j + 1)
                eng.activation(ffhi[:, ds(j, 1), :].rearrange("p a t -> p (a t)"), tmp[:, 2 + par, :],
                               ACT.Copy).then_inc(sem("ffn_ffhi"), 1)
            pairs(eng, FB, body, tail=1)

        def ffn_in_vector(st, ffn, ph):
            eng = nc.vector
            def body(j, par):
                last = isinstance(j, int) and j == FB - 1
                if not last:
                    split_lo(ph, 2 * j + 2, 0)
                eng.wait_ge(ph.used, ph.base + 2 * j + 2)
                eng.wait_ge(sem("ffn_silu"), ffn * FB + j + 1)
                if not (isinstance(j, int) and j < 2):
                    eng.wait_ge(sem("ffn_fflo"), ffn * FB + j - 1)
                half = lambda ap: ap.rearrange("p (h t) -> p h t", h=2)
                eng.tensor_tensor(half(tmp[:, 2 + par, :]), half(tmp[:, par, :]), ps[:, 4 * par + 2:4 * par + 4, 0:TH],
                                  ALU.mult).then_inc(sem("ffn_mul"), 1)
                if not last:
                    split_lo(ph, 2 * j + 3, 1)
                eng.wait_ge(sem("ffn_ffhi"), ffn * FB + j + 1)
                eng.tensor_tensor(fflo[:, ds(j, 1), :].rearrange("p a t -> p (a t)"), tmp[:, 2 + par, :],
                                  ffhi[:, ds(j, 1), :].rearrange("p a t -> p (a t)").bitcast(F32),
                                  ALU.subtract).then_inc(sem("ffn_fflo"), 1)
            pairs(eng, FB, body, tail=1)

        def ffn_loads(ph_in, ph_out, w_in, w_out):
            eng = nc.sync
            wi = w_in.rearrange("l (k p) n -> p (l k) n", p=P)
            wo_ = w_out.rearrange("l (k p) n -> p (l k) n", p=P)
            def body(j, par):
                for gu in range(2):
                    load_chunk(ph_in, 2 * j + gu, gu, wi[:, :, ds(j * P + gu * FF, P)], DB)
            pairs(eng, FB, body)
            for d in range(DB):
                for hh in range(2):
                    load_chunk(ph_out, 2 * d + hh, hh, wo_[:, hh * HB:(hh + 1) * HB, d * P:(d + 1) * P], HB)

        def start_sync():
            eng = nc.sync
            eng.dma_start(ctok[0:1, :], c_prompt).then_inc(sem("c_landed"), 16)
            eng.dma_start(ctok[1:NC_, :], c_sample).then_inc(sem("c_landed"), 16)
            eng.dma_start(ident[:], ident_d).then_inc(sem("ident_landed"), 16)
            eng.dma_start(rows[0:72, :], b_ada.rearrange("l (r c) -> (l r) c", c=P)).then_inc(sem("rows_landed"), 16)
            eng.dma_start(rows[72:96, :], ln_g.rearrange("l i (r c) -> (l i r) c", c=P)).then_inc(sem("rows_landed"), 16)
            eng.dma_start(rows[96:120, :], ln_b.rearrange("l i (r c) -> (l i r) c", c=P)).then_inc(sem("rows_landed"), 16)
            eng.dma_start(rows[120:121, :], subln_g).then_inc(sem("rows_landed"), 16)
            wa = w_ada.rearrange("l (k p) n -> p (l k) n", p=P)
            for i in range(NM):
                for kh in range(2):
                    n = 2 * i + kh
                    if n >= 4:
                        eng.wait_ge(sem("ada_used"), n - 3)
                    eng.dma_start(wada[:, n % 4], wa[:, kh * 4:kh * 4 + 4, i * D:(i + 1) * D]).then_inc(sem(f"ada_landed{n % 4}"), 16)
                if i == 1:
                    eng.dma_start(xtok[:, 0:PT_, :], x_prompt.rearrange("b (t p) d -> p (b t) d", p=P)).then_inc(sem("x_landed"), 16)
                    eng.dma_start(xtok[0:NSM, PT_, :], x_sample.rearrange("b s d -> (b s) d")).then_inc(sem("x_landed"), 16)
                    eng.dma_start(lamb[:].rearrange("p a b -> p (a b)"),
                                  diff_lambda.rearrange("l a e -> l (a e)").to_broadcast([P, 4 * E])).then_inc(sem("lam_landed"), 16)
                    eng.dma_start(pages[:], page_table.rearrange("b n -> (b n)").unsqueeze(0)).then_inc(sem("pages"), 16)

        def start_pool():
            eng = nc.gpsimd
            eng.memset(cT[:], 0.0).then_inc(sem("pool_set"), 1)
            eng.memset(one_d[:], 1.0 / D).then_inc(sem("pool_set"), 1)
            eng.memset(one_v[:], 1.0 / P).then_inc(sem("pool_set"), 1)
            eng.memset(stat[:, 5:6], LN_EPS).then_inc(sem("pool_set"), 1)

        def start_tensor():
            pe = nc.tensor
            pe.wait_ge(sem("ident_landed"), 16)
            pe.wait_ge(sem("csil"), 1)
            for k in range(DB):
                m = pe.transpose(ps[:, 0, k * 16:k * 16 + NC_], csil[:, k * P:(k + 1) * P], ident[0:NC_, 0:NC_])
            m.then_inc(sem("c_turned"), 1)
            pe.wait_ge(sem("rows_landed"), 64)
            pe.transpose(ps[:, 7, 0:121], rows[0:121, :], ident[0:121, 0:121]).then_inc(sem("rows_turned"), 1)
            pe.wait_ge(sem("cT"), 1)

            def turn_x(k):
                if k >= 2:
                    pe.wait_ge(sem("x_copied"), k - 1)
                for t in range(PT_):
                    m = pe.transpose(ps[:, 4 + k % 2, t * P:(t + 1) * P], xtok[:, t, k * P:(k + 1) * P], ident[:])
                m.then_inc(sem("x_turned"), 1)

            for i in range(NM):
                if i >= 2:
                    pe.wait_ge(sem("mod_row"), i - 1)
                for k in range(DB):
                    if k % 4 == 0:
                        n = 2 * i + k // 4
                        pe.wait_ge(sem(f"ada_landed{n % 4}"), 16 * (n // 4 + 1))
                    for j in range(4):
                        m = pe.matmul(ps[32 * j:32 * j + 32, i % 2, 0:256], cT[:, k, :],
                                      wada[:, n % 4, k % 4, j * 256:(j + 1) * 256], start=(k == 0), stop=(k == DB - 1),
                                      tile_position=(0, 32 * j))
                    if k % 4 == 3:
                        m.then_inc(sem("ada_used"), 1)
                if i == 1:
                    pe.wait_ge(sem("x_landed"), 32)
                if 1 <= i:
                    turn_x(i - 1)
                if i == 1:
                    for k in range(DB):
                        m = pe.transpose(ps[:, 6, k * NSM:(k + 1) * NSM], xtok[0:NSM, PT_, k * P:(k + 1) * P], ident[0:NSM, 0:NSM])
                    m.then_inc(sem("xs_turned"), 1)
                pe.wait_ge(sem("mod_row"), i + 1)
                if i >= 2:
                    pe.wait_ge(sem("mod_bias"), i - 1)
                for h in range(2):
                    m = pe.transpose(ps[:, 2 + i % 2, h * P:(h + 1) * P], modrow[:, i % 2, h * P:(h + 1) * P], ident[:])
                m.then_inc(sem("mod_turned"), 1)

        def start_scalar():
            eng = nc.scalar
            eng.wait_ge(sem("c_landed"), 32)
            eng.activation(csil[:], ctok[:], ACT.Silu).then_inc(sem("csil"), 1)
            eng.wait_ge(sem("pool_set"), 1)
            eng.wait_ge(sem("c_turned"), 1)
            eng.activation(cT[:, :, 0:NC_], ps[:, 0, 0:DB * 16].rearrange("p (k c) -> p k c", c=16)[:, :, 0:NC_],
                           ACT.Copy).then_inc(sem("cT"), 1)
            eng.wait_ge(sem("lam_dots"), 1)
            eng.activation(stat[:, 0:2], stat[:, 0:2], ACT.Exp).then_inc(sem("lam_exp"), 1)
            for i in range(NM):
                eng.wait_ge(sem("ada_used"), 2 * i + 2)
                if i >= 2:
                    eng.wait_ge(sem("mod_turned"), i - 1)
                eng.activation(modrow[:, i % 2, :], ps[:, i % 2, 0:256], ACT.Copy).then_inc(sem("mod_row"), 1)
                if i >= 1:
                    k = i - 1
                    eng.wait_ge(sem("x_turned"), k + 1)
                    eng.activation(xT[:, k, 0:NPR], ps[:, 4 + k % 2, :], ACT.Copy).then_inc(sem("x_copied"), 1)

        def start_vector():
            eng = nc.vector
            eng.wait_ge(sem("lam_landed"), 16)
            l4 = lamb[:].rearrange("p (a b) e -> p a b e", b=2)
            eng.tensor_tensor(lamp[:], l4[:, :, 0, :], l4[:, :, 1, :], ALU.mult).then_inc(sem("lam_mul"), 1)
            eng.wait_ge(sem("lam_mul"), 1)
            eng.reduce_sum(stat[:, 0:2], lamp[:], AX_X).then_inc(sem("lam_dots"), 1)
            eng.wait_ge(sem("rows_turned"), 1)
            eng.tensor_copy(colT[:, 0:121], ps[:, 7, 0:121]).then_inc(sem("cols"), 1)
            eng.wait_ge(sem("cols"), 1)
            eng.wait_ge(sem("xs_turned"), 1)
            eng.tensor_copy(xT[:, :, NPR:T], ps[:, 6, :].rearrange("p (k s) -> p k s", s=NSM)).then_inc(sem("xs_copied"), 1)
            eng.wait_ge(sem("lam_exp"), 1)
            eng.tensor_tensor(stat[:, 2:3], stat[:, 1:2], stat[:, 0:1], ALU.subtract).then_inc(sem("lam_sub"), 1)
            eng.wait_ge(sem("lam_sub"), 1)
            eng.tensor_scalar(stat[:, 3:4], stat[:, 2:3], -LAM_INIT, None, ALU.add).then_inc(sem("lam"), 1)
            eng.tensor_scalar(stat[:, 4:5], colT[:, 120:121], 1.0 - LAM_INIT, None, ALU.mult).then_inc(sem("lam"), 1)
            for i in range(NM):
                eng.wait_ge(sem("mod_turned"), i + 1)
                src = ps[:, 2 + i % 2, 0:256].rearrange("p (h j c) -> p j h c", h=2, j=4)[:, :, :, 0:NC_]
                dst = modT[:, i, :, :].rearrange("p (j h) c -> p j h c", h=2)
                b = colT[:, i * DB:(i + 1) * DB].rearrange("p (j h) -> p j h", h=2).unsqueeze(3).to_broadcast([P, 4, 2, NC_])
                eng.tensor_tensor(dst, src, b, ALU.add).then_inc(sem("mod_bias"), 1)
                eng.wait_ge(sem("mod_bias"), i + 1)
                a, m = {0: (0.0, 1.0), 1: (1.0, 1.0), 2: (0.0, (0.5, 1.0, 0.5)[i // 3])}[i % 3]
                eng.tensor_scalar(modT[:, i, :, :], modT[:, i, :, :], a, m, ALU.add, ALU.mult).then_inc(sem("mods"), 1)
            eng.wait_ge(sem("mods"), NM)

        ROTS = (0, 1, 3, 4)
        VS = (2, 5)

        def qkv_bank(g, t):
            return (5 * g + t) % 6

        def tokens(t):
            return P if t < PT_ else NSM

        def qkv_sync():
            eng = nc.sync
            w = w_qkv.rearrange("l (k p) n -> p (l k) n", p=P)
            outs = {1: (wkp, wks), 2: (wvp, wvs), 4: (dkp, dks), 5: (dvp, dvs)}
            def flat(ap):
                names = "abcdefg"[:len(ap.shape)]
                lead = names[:-2] if ap is not dkp and ap is not dks else names[:-3]
                rest = names[len(lead):]
                return ap.rearrange(f"{' '.join(names)} -> ({' '.join(lead)}) ({' '.join(rest)})")
            def store(g):
                op, os_ = (flat(a) for a in outs[g])
                ready = "rot" if g in ROTS else "vout"
                base = (ROTS if g in ROTS else VS).index(g) * (PT_ + 1)
                for t in range(PT_ + 1):
                    eng.wait_ge(sem(ready), (base + t + 1) * (2 if g in ROTS else 1))
                    n = tokens(t)
                    src = rot[0:n, t, :] if g in ROTS else V[0:n, VS.index(g), t, :]
                    dst = op[t * P:(t + 1) * P, :] if t < PT_ else os_
                    eng.dma_start(dst, src).then_inc(sem(f"kept{g}"), 16)
            for g in range(6):
                for c in range(4):
                    load_chunk(qkv, 4 * g + c, c % 2, w[:, 2 * c:2 * c + 2, g * QW:(g + 1) * QW], 2)
                if g == 0:
                    eng.wait_ge(out1.used, 2 * DB)
                    eng.dma_start(ropet[:].rearrange("p a b c -> p (a b c)"), rope_d).then_inc(sem("tables"), 16)
                    eng.dma_start(mask_a[:], mask_a_d).then_inc(sem("tables"), 16)
                    eng.dma_start(mask_b[:], mask_b_d).then_inc(sem("tables"), 16)
                    eng.dma_start(past_a[:], past_a_d).then_inc(sem("tables"), 16)
                if g - 1 in outs:
                    store(g - 1)
            store(5)

        def turn_rot(g, t):
            pe = nc.tensor
            r = ROTS.index(g) * (PT_ + 1) + t
            pe.wait_ge(sem("rot"), 2 * r + 2)
            if r >= 2:
                pe.wait_ge(sem("qk_copied"), r - 1)
            n = tokens(t)
            for f in range(4):
                m = pe.transpose(ps[:, 6 + r % 2, f * P:f * P + n], rot[0:n, t, f * P:(f + 1) * P], ident[0:n, 0:n])
            m.then_inc(sem("qk_turned"), 1)

        def tile_summed(eng, g, t):
            if t < PT_:
                eng.wait_ge(sem("qkv_sum"), PT_ * g + t + 1)
            else:
                eng.wait_ge(qkv.used, 4 * g + 4)

        def qkv_tensor():
            pe = nc.tensor
            pe.wait_ge(sem("step_slo"), 2)
            for g in range(7):
                for c in range(4):
                    if g < 6:
                        slot = c % 2
                        pe.wait_ge(qkv.lo, 4 * g + c + 1)
                        if g == 0:
                            pe.wait_ge(sem("step_hlo"), DB + 2 * c + 2)
                        for t in range(PT_ + 1):
                            n = tokens(t)
                            if c == 0 and 5 * g + t >= 6:
                                g0, t0 = divmod(5 * g + t - 6, 5)
                                if g0 in ROTS:
                                    pe.wait_ge(sem("qkv_read"), ROTS.index(g0) * (PT_ + 1) + t0 + 1)
                                else:
                                    pe.wait_ge(sem("vout"), VS.index(g0) * (PT_ + 1) + t0 + 1)
                            for k in range(2):
                                kk = 2 * c + k
                                wh = whi[:, slot, k * QW:(k + 1) * QW]
                                wl = wlo[:, slot, k * QW:(k + 1) * QW]
                                for x, w, n3 in ((hhi, wh, 0), (hlo, wh, 1), (hhi, wl, 2)):
                                    m = pe.matmul(ps[0:n, qkv_bank(g, t), :], x[:, kk, t * P:t * P + n], w,
                                                  start=(kk == 0 and n3 == 0), stop=(kk == DB - 1 and n3 == 2))
                            if c == 3 and t < PT_:
                                m.then_inc(sem("qkv_sum"), 1)
                        m.then_inc(qkv.used, 1)
                    if g - 1 in ROTS and c in (1, 2):
                        for t in ((0, 1, 2), (3, 4))[c - 1]:
                            turn_rot(g - 1, t)

        def qkv_scalar():
            eng = nc.scalar
            def copy_turned(g, t):
                r = ROTS.index(g) * (PT_ + 1) + t
                eng.wait_ge(sem("qk_turned"), r + 1)
                n = tokens(t)
                dst = (QT if g in (0, 3) else KT)[:, 4 * (g // 3):4 * (g // 3) + 4, t * P:t * P + n]
                src = ps[:, 6 + r % 2, :].rearrange("p (f t) -> p f t", f=4)[:, :, 0:n]
                eng.activation(dst, src, ACT.Copy, scale=(SCALE if g in (0, 3) else 1.0)).then_inc(sem("qk_copied"), 1)
            def copy_v(g, t):
                n = tokens(t)
                tile_summed(eng, g, t)
                eng.activation(V[0:n, VS.index(g), t, :], ps[0:n, qkv_bank(g, t), :], ACT.Copy).then_inc(sem("vout"), 1)
            for g in range(6):
                if g - 1 in VS:
                    for t in range(PT_ + 1):
                        copy_v(g - 1, t)
                for c in range(4):
                    if 4 * g + c >= 2:
                        split_hi(qkv, 4 * g + c, c % 2)
                    if g - 1 in ROTS and c == 3:
                        for t in range(PT_ + 1):
                            copy_turned(g - 1, t)
            for t in range(PT_ + 1):
                copy_v(5, t)

        def qkv_vector():
            eng = nc.vector
            def rotate(g, t):
                r = ROTS.index(g) * (PT_ + 1) + t
                n = tokens(t)
                tile_summed(eng, g, t)
                if r >= 1:
                    eng.wait_ge(sem("rot"), 2 * r)
                src = ps[0:n, qkv_bank(g, t), :].rearrange("p (h e) -> p h e", e=E // 2)
                tab = lambda i: ropet[0:n, t, i, :].unsqueeze(1).to_broadcast([n, 2 * 8, E // 2])
                half = lambda i: rab[0:n, i, :].rearrange("p (h e) -> p h e", e=E // 2)
                eng.tensor_tensor(half(0), src, tab(0), ALU.mult).then_inc(sem("rope_cos"), 1)
                eng.tensor_tensor(half(1), src, tab(1), ALU.mult).then_inc(sem("qkv_read"), 1)
                eng.wait_ge(sem("rope_cos"), r + 1)
                eng.wait_ge(sem("qkv_read"), r + 1)
                if r >= 5:
                    g0 = ROTS[ROTS.index(g) - 1]
                    eng.wait_ge(sem("qk_turned"), r - 4)
                    if g0 in (1, 4):
                        eng.wait_ge(sem(f"kept{g0}"), 16 * (PT_ + 1))
                q = lambda i: rab[0:n, i, :].rearrange("p (h two e) -> p h two e", two=2, e=E // 2)
                o = rot[0:n, t, :].rearrange("p (h two e) -> p h two e", two=2, e=E // 2)
                eng.tensor_tensor(o[:, :, 0, :], q(0)[:, :, 0, :], q(1)[:, :, 1, :], ALU.subtract).then_inc(sem("rot"), 1)
                eng.tensor_tensor(o[:, :, 1, :], q(0)[:, :, 1, :], q(1)[:, :, 0, :], ALU.add).then_inc(sem("rot"), 1)
            for g in range(6):
                for c in range(4):
                    if 4 * g + c >= 2:
                        split_lo(qkv, 4 * g + c, c % 2)
                    if g == 1 and c == 0:
                        eng.wait_ge(sem("tables"), 4 * 16)
                    if g - 1 in ROTS and c < 2:
                        for t in ((0, 1, 2, 3), (4,))[c]:
                            rotate(g - 1, t)

        QUARTERS = 8
        LAG = 5
        DRAIN = 6
        HEADS = 4 * 2 + 4
        CH = (A_CHUNKS, B_CHUNKS)
        WID = (A_KEYS, PAST)
        DMAS = ((1, 1, 1, 1), (4, 4, 4, 4))

        def keys_of(m, tile):
            return FARW if m == 0 and tile < A_FAR else P

        def key0(m, tile):
            return tile * P if m else min(tile, A_FAR) * FARW + max(tile - A_FAR, 0) * P

        def tile0(m, c):
            return sum(CH[m][:c])

        def chunk_keys(m, c):
            return CH[m][c] * keys_of(m, tile0(m, c))

        def landed_at(b, m, c):
            before = sum(DMAS[k][j] for k in range(2) for j in range(4) if j % 2 == c % 2 and (k, j) <= (m, c))
            return 16 * (b * sum(DMAS[k][j] for k in range(2) for j in range(4) if j % 2 == c % 2) + before)

        def positive(n):
            return not isinstance(n, int) or n > 0

        def back(b, i, lag):
            return (b, i - lag) if i >= lag else (b - 1, i - lag + QUARTERS)

        def alive(b):
            return not isinstance(b, int) or 0 <= b < NB

        def mixer_of(b, run):
            return run if not isinstance(b, int) else int(b >= 4)

        def over_sequences(eng, body):
            body(0, 0)
            with eng.Fori(1, 4) as b:
                body(b, 0)
            body(4, 1)
            with eng.Fori(5, NB) as b:
                body(b, 1)
            body(NB, 1)

        def each_sequence(body):
            for b in range(NB + 1):
                body(b, int(b >= 4))

        def quarters(b):
            return range(QUARTERS if alive(b) else DRAIN)

        def step_of(pm, i):
            return divmod(i, 4) if pm == 0 else (i % 2, i // 2)

        def turn_of(pm, b, i):
            return QUARTERS * b + i if pm == 0 else 16 + 4 * b + i // 2

        def is_turn(pm, i):
            return pm == 0 or i % 2 == 1

        def head_of(pm, b, i):
            return 2 * b + i // 4 if pm == 0 else b + 4

        def ends_head(pm, i):
            return i % 4 == 3 if pm == 0 else i == 7

        def turned(pm, i):
            return PTp1 if pm == 0 and i >= 4 else PTp0

        def head_values(pm, i):
            return VH1 if pm == 0 and i >= 4 else VH0

        def norm_head(b, i, run, at_quarter):
            return run == 1 and not (isinstance(b, int) and b == 4) and i == at_quarter

        rms = VH1[:].rearrange("p a b -> p (a b)")

        def attend_sync():
            eng = nc.sync
            far = [w[:, :, 0:PAST - DENSE].rearrange("l b (g j) h e -> (l b) g j (h e)", j=16) for w in (win_k, win_v)]
            near = [w[:, :, PAST - DENSE:PAST].rearrange("l b (p t) h e -> (l b) p t (h e)", t=A_NEAR) for w in (win_k, win_v)]
            pool = [diff_k.rearrange("l n p h c e -> (l n) p (h c e)"), diff_v.rearrange("l n p h v -> (l n) p (h v)")]

            def load(b, i, is_v):
                m, c = divmod(i, 4)
                n, tile = CH[m][c], tile0(m, c)
                if m == 1:
                    page = [eng.value_load(pages[0:1, ds(b * NPAGE + tile + k, 1)], min_val=0,
                                           max_val=diff_k.shape[1] - 1) for k in range(n)]
                q = QUARTERS * b + i
                if positive(q - 1):
                    if is_v:
                        eng.wait_ge(sem("d_pv"), q - 1)
                    else:
                        eng.wait_ge(sem("d_kt"), 4 * q - 4)
                slot = kv(2 * is_v + c % 2)
                s = sem(f"{'kv'[is_v]}_landed{c % 2}")
                if m == 0 and tile < A_FAR:
                    src = far[is_v][ds(b, 1), :, tile:tile + n, :].rearrange("a g j c -> (a g) j c")
                    eng.dma_start(slot[0:FARW, 0:n, :], src).then_inc(s, 16)
                elif m == 0:
                    t0 = tile - A_FAR
                    src = near[is_v][ds(b, 1), :, t0:t0 + n, :].rearrange("a p t c -> (a p) t c")
                    eng.dma_start(slot[:, 0:n, :], src).then_inc(s, 16)
                else:
                    for k in range(n):
                        src = pool[is_v][ds(page[k], 1), :, :].rearrange("a p c -> (a p) c")
                        eng.dma_start(slot[:, k, :], src).then_inc(s, 16)

            def body(b, run):
                for i in quarters(b):
                    if alive(b):
                        load(b, i, 0)
                    if isinstance(b, int) and b == 0 and i == 1:
                        eng.wait_ge(sem("qk_turned"), 4 * (PT_ + 1))
                        eng.wait_ge(sem("kept1"), 16 * (PT_ + 1))
                        eng.wait_ge(sem("kept4"), 16 * (PT_ + 1))
                        eng.dma_start(new_ab[:].rearrange("p a b c -> p (a b c)"), new_ab_d).then_inc(sem("new_masks"), 16)
                    vb, vi = back(b, i, LAG)
                    if alive(vb):
                        load(vb, vi, 1)
            eng.wait_ge(qkv.used, 24)
            eng.wait_ge(sem("pages"), 16)
            over_sequences(eng, body)

        def attend_pool():
            eng = nc.gpsimd
            eng.memset(QB[:], 0.0).then_inc(sem("d_zero"), 1)
            eng.wait_ge(qkv.used, 24)
            eng.memset(QP[:], 0.0).then_inc(sem("d_zero"), 1)
            eng.memset(zeros[:], 0.0).then_inc(sem("d_zero"), 1)
            eng.wait_ge(sem("d_zero"), 3)
            eng.wait_ge(sem("qk_copied"), 4 * (PT_ + 1))
            eng.wait_ge(sem("vout"), 2 * (PT_ + 1))

            def body(b, run):
                pm = mixer_of(b, run)
                for i in quarters(b):
                    if not alive(b):
                        continue
                    m, c = divmod(i, 4)
                    n = QUARTERS * b + i
                    if c == 0:
                        if positive(n - 4):
                            eng.wait_ge(sem("d_sc"), n - 4)
                        for h in range(2):
                            r = slice(h * E, (h + 1) * E)
                            eng.tensor_copy(QB[r, m, :, h * NS:(h + 1) * NS],
                                            QT[r, 4 * m:4 * m + 4, ds(b * NS + NPR, NS)]).then_inc(sem("d_qb"), 1)
                        eng.wait_ge(sem("d_qb"), 4 * b + 2 * m + 2)
                    h, q = step_of(pm, i)
                    r = slice(h * E, (h + 1) * E)
                    if positive(n - 1):
                        eng.wait_ge(sem("p_score"), n - 1)
                    eng.tensor_copy(QP[r, h, q % 2, :], QT[r, ds(b, 1), q * P:(q + 1) * P].rearrange("p a t -> p (a t)")).then_inc(sem("p_query"), 1)
                    eng.wait_ge(sem("p_query"), n + 1)
                    if pm == 1 and i == 6 or pm == 0 and i in (2, 6):
                        hd = head_of(pm, b, i)
                        if positive(hd - (pm == 0)):
                            eng.wait_ge(sem("p_pv"), hd - (pm == 0))
                        if pm == 1:
                            src = V[:, 1, 0:PT_, ds(b * P - 4 * P, P)]
                        else:
                            src = V[:, 0, 0:PT_, ds(b * P + i // 4 * E, E)]
                        eng.tensor_copy(head_values(pm, i)[:, :, 0:(P if pm else E)], src).then_inc(sem("p_values"), 1)
                        eng.wait_ge(sem("p_values"), hd + 1)
            over_sequences(eng, body)

        def attend_tensor():
            pe = nc.tensor
            pe.wait_ge(sem("qk_copied"), 4 * (PT_ + 1))
            pe.wait_ge(sem("vout"), 2 * (PT_ + 1))

            def turn_keys(b, i, f):
                m, c = divmod(i, 4)
                nt, kw = CH[m][c], keys_of(m, tile0(m, c))
                q = QUARTERS * b + i
                if f == 0:
                    pe.wait_ge(sem(f"k_landed{c % 2}"), landed_at(b, m, c))
                if positive(2 * q + f // 2):
                    pe.wait_ge(sem("d_kcv" if f % 2 else "d_kca"), 2 * q + f // 2)
                for k in range(nt):
                    mm = pe.transpose(ps[:, f % 2, k * kw:(k + 1) * kw], kv(c % 2)[0:kw, k, f * P:(f + 1) * P], ident[0:kw, 0:kw])
                mm.then_inc(sem("d_kt"), 1)

            def scores(b, i):
                m, c = divmod(i, 4)
                w, q = chunk_keys(m, c), QUARTERS * b + i
                pe.wait_ge(sem("d_kca"), 2 * q + 2)
                pe.wait_ge(sem("d_kcv"), 2 * q + 2)
                if positive(q):
                    pe.wait_ge(sem("d_smax"), q)
                for f in range(4):
                    mm = pe.matmul(ps[32 * f:32 * f + 32, 2, 0:w], QB[:, m, f, :], KC[:, f, 0:w], start=True, stop=True,
                                   tile_position=(0, 32 * f))
                mm.then_inc(sem("d_sc"), 1)

            def scores_new(b, i):
                m = i // 4
                pe.wait_ge(sem("d_qb"), 4 * b + 2 * m + 2)
                pe.wait_ge(sem("p_max"), QUARTERS * b + i + 1)
                for f in range(4):
                    mm = pe.matmul(ps[32 * f:32 * f + 32, 5, 0:NSM], QB[:, m, f, :], KT[:, 4 * m + f, NPR:T], start=True, stop=True,
                                   tile_position=(0, 32 * f))
                mm.then_inc(sem("d_snew"), 1)

            def turn_weights(b, i, new):
                m, c = divmod(i, 4)
                u = 2 * b + m
                if c == 0 and not new:
                    pe.wait_ge(sem("d_exp"), u + 1)
                if not new and positive(5 * u + c):
                    pe.wait_ge(sem("d_ptc"), 5 * u + c + (c > 0))
                if new:
                    mm = pe.transpose(ps[0:NSM, 3, 0:P], S[m][:, WID[m]:WID[m] + NSM], ident[:])
                else:
                    t0, kw = tile0(m, c), keys_of(m, tile0(m, c))
                    for k in range(CH[m][c]):
                        o = key0(m, t0 + k)
                        mm = pe.transpose(ps[0:kw, 3, k * P:(k + 1) * P], S[m][:, o:o + kw], ident[:])
                mm.then_inc(sem("d_pt"), 1)

            def values(b, i):
                m, c = divmod(i, 4)
                u = 2 * b + m
                pe.wait_ge(sem(f"v_landed{c % 2}"), landed_at(b, m, c))
                pe.wait_ge(sem("d_ptc"), 5 * u + c + 2)
                if c == 0 and positive(2 * u):
                    pe.wait_ge(sem("d_out"), 2 * u)
                for k in range(CH[m][c]):
                    tile = tile0(m, c) + k
                    kw = keys_of(m, tile)
                    for f in range(4):
                        mm = pe.matmul(ps[32 * f:32 * f + 32, 4, 0:P], PTd[0:kw, tile, 32 * f:32 * f + 32],
                                       kv(2 + c % 2)[0:kw, k, f * P:(f + 1) * P], start=(tile == 0), stop=(tile == sum(CH[m]) - 1),
                                       tile_position=(0, 32 * f), skip_group_check=True)
                    if tile == 0:
                        for f in range(4):
                            pe.matmul(ps[32 * f:32 * f + 32, 4, 0:P], PTd[0:NSM, NPAGE, 32 * f:32 * f + 32],
                                      V[0:NSM, m, PT_, f * P:(f + 1) * P], start=False, stop=False,
                                      tile_position=(0, 32 * f), skip_group_check=True)
                mm.then_inc(sem("d_pv"), 1)

            def prompt_score(b, i, pm):
                h, q = step_of(pm, i)
                n, w = QUARTERS * b + i, (q + 1) * P
                pe.wait_ge(sem("p_query"), n + 1)
                if positive(n):
                    pe.wait_ge(sem("p_max"), n)
                if i % 4 == 1:
                    pe.wait_ge(sem("d_new"), 2 * b + i // 4 + 1)
                pe.matmul(ps[:, 5, 0:w], QP[:, h, q % 2, :], KT[:, ds(b, 1), 0:w].rearrange("p a t -> p (a t)"), start=True,
                          stop=True).then_inc(sem("p_score"), 1)

            def prompt_turn(b, i, pm):
                h, q = step_of(pm, i)
                r = turn_of(pm, b, i)
                pe.wait_ge(sem("p_norm"), r + 1)
                if positive(r):
                    pe.wait_ge(sem("p_copied"), r)
                src = (i - pm) % 4
                for kt in range(q + 1):
                    mm = pe.transpose(ps[:, 6, kt * P:(kt + 1) * P], PP[:, src, kt * P:(kt + 1) * P], ident[:])
                mm.then_inc(sem("p_turn"), 1)

            def prompt_values(b, i, pm):
                hd = head_of(pm, b, i)
                pe.wait_ge(sem("p_copied"), PT_ * hd + PT_)
                pe.wait_ge(sem("p_values"), hd + 1)
                if pm == 1 and positive(b - 4):
                    pe.wait_ge(sem("r_std"), b - 4)
                if positive(hd):
                    pe.wait_ge(sem("p_out"), hd)
                for kt in range(PT_):
                    wv = P if pm else E
                    out = ps[:, 7, kt * P:NPR] if pm else ps[i // 4 * E:(i // 4 + 1) * E, 7, kt * P:NPR]
                    mm = pe.matmul(out, head_values(pm, i)[:, kt, 0:wv], turned(pm, i)[:, kt, kt * P:NPR], start=(kt == 0), stop=(kt == PT_ - 1),
                                   skip_group_check=True)
                mm.then_inc(sem("p_pv"), 1)

            def body(b, run):
                for i in quarters(b):
                    lb, li = back(b, i, LAG)
                    if alive(b):
                        turn_keys(b, i, 0)
                        turn_keys(b, i, 1)
                    if i % 4 == 1 and alive(b - 1):
                        pe.wait_ge(sem("d_on"), 2 * (b - 1) + i // 4 + 1)
                        pe.transpose(ps[:, 4, P:2 * P], On[:], ident[:]).then_inc(sem("d_ot"), 1)
                    if alive(b):
                        prompt_score(b, i, mixer_of(b, run))
                    if alive(lb):
                        turn_weights(lb, li, False)
                    if alive(b):
                        turn_keys(b, i, 2)
                    if alive(lb) and li % 4 == 0:
                        pe.wait_ge(sem("d_ptc"), 5 * (2 * lb + li // 4) + 1)
                    if alive(b):
                        turn_keys(b, i, 3)
                    if alive(lb) and li % 4 == 0:
                        turn_weights(lb, li, True)
                    if alive(b) and i % 4 == 0:
                        scores_new(b, i)
                    tb, ti = back(b, i, 1)
                    if alive(tb) and is_turn(mixer_of(tb, run), ti):
                        prompt_turn(tb, ti, mixer_of(tb, run))
                    if alive(lb):
                        values(lb, li)
                    if alive(b):
                        scores(b, i)
                    hb, hi_ = back(b, i, 2)
                    if alive(hb) and ends_head(mixer_of(hb, run), hi_):
                        prompt_values(hb, hi_, mixer_of(hb, run))
                    if norm_head(b, i, run, 3):
                        pe.wait_ge(sem("r_sq"), b - 4)
                        pe.matmul(ps[:, 7, :], one_v[:], rms, start=True, stop=True).then_inc(sem("r_mean"), 1)
            over_sequences(pe, body)

        def attend_scalar():
            eng = nc.scalar
            col = lambda k, i: stat[:, k + i % 4:k + i % 4 + 1]

            def evacuate(b, i, f):
                m, c = divmod(i, 4)
                w, q = chunk_keys(m, c), QUARTERS * b + i
                eng.wait_ge(sem("d_kt"), 4 * q + f + 1)
                if f == 0 and positive(q):
                    eng.wait_ge(sem("d_sc"), q)
                eng.activation(KC[:, f, 0:w], ps[:, 0, 0:w], ACT.Copy).then_inc(sem("d_kca"), 1)

            def prompt_exp(b, i, pm):
                n, w = QUARTERS * b + i, (step_of(pm, i)[1] + 1) * P
                eng.wait_ge(sem("p_neg"), n + 1)
                eng.activation(PP[:, i % 4, 0:w], PP[:, i % 4, 0:w], ACT.Exp, bias=col(12, i), scale=1.0,
                               accum_out=col(16, i)).then_inc(sem("p_exp"), 1)

            def prompt_copy(b, i, pm):
                h, q = step_of(pm, i)
                eng.wait_ge(sem("p_turn"), turn_of(pm, b, i) + 1)
                free = head_of(pm, b, i) - (pm == 0)
                if q == 0 and positive(free):
                    eng.wait_ge(sem("p_pv"), free)
                src = ps[:, 6, 0:(q + 1) * P].rearrange("p (k t) -> p k t", t=P)
                eng.activation(turned(pm, i)[:, 0:q + 1, q * P:(q + 1) * P], src, ACT.Copy).then_inc(sem("p_copied"), 1)

            def copy_weights(b, i, new):
                m, c = divmod(i, 4)
                u = 2 * b + m
                g = 1 if new else c + (c > 0)
                eng.wait_ge(sem("d_pt"), 5 * u + g + 1)
                if positive(4 * u + c - 3) and not new:
                    eng.wait_ge(sem("d_pv"), 4 * u + c - 3)
                if new:
                    eng.activation(PTd[0:NSM, NPAGE, :], ps[0:NSM, 3, 0:P], ACT.Copy).then_inc(sem("d_ptc"), 1)
                else:
                    t0, nt, kw = tile0(m, c), CH[m][c], keys_of(m, tile0(m, c))
                    eng.activation(PTd[0:kw, t0:t0 + nt, :], ps[0:kw, 3, 0:nt * P].rearrange("p (t r) -> p t r", r=P),
                                   ACT.Copy).then_inc(sem("d_ptc"), 1)

            def exp(b, m):
                w = WID[m] + NSM
                eng.wait_ge(sem("d_neg"), 2 * b + m + 1)
                eng.activation(S[m][:, 0:w], S[m][:, 0:w], ACT.Exp, bias=stat[:, 41:42], scale=1.0,
                               accum_out=stat[:, 42:43]).then_inc(sem("d_exp"), 1)

            def body(b, run):
                for i in quarters(b):
                    lb, li = back(b, i, LAG)
                    tb, ti = back(b, i, 1)
                    if alive(b):
                        evacuate(b, i, 0)
                        prompt_exp(b, i, mixer_of(b, run))
                    if alive(lb):
                        copy_weights(lb, li, False)
                    if alive(b):
                        evacuate(b, i, 2)
                    if alive(lb) and li % 4 == 0:
                        copy_weights(lb, li, True)
                    if alive(tb) and is_turn(mixer_of(tb, run), ti):
                        prompt_copy(tb, ti, mixer_of(tb, run))
                    if i % 4 == 0 and alive(tb):
                        exp(tb, ti // 4)
                    if norm_head(b, i, run, 3):
                        eng.wait_ge(sem("p_out"), b + 4)
                        eng.activation(rms, QT[:, ds(b - 1, 1), 0:NPR].rearrange("p a t -> p (a t)"), ACT.Square).then_inc(sem("r_sq"), 1)
                    if norm_head(b, i, run, 4):
                        eng.wait_ge(sem("r_mean"), b - 4)
                        eng.activation(rms, ps[:, 7, :], ACT.Sqrt, bias=stat[:, 5:6], scale=1.0).then_inc(sem("r_std"), 1)
            for g in (1, 4):
                eng.wait_ge(sem(f"kept{g}"), 16 * (PT_ + 1))
            over_sequences(eng, body)

        def attend_vector():
            eng = nc.vector
            col = lambda k, i: stat[:, k + i % 4:k + i % 4 + 1]

            def evacuate(b, i, f):
                m, c = divmod(i, 4)
                w, q = chunk_keys(m, c), QUARTERS * b + i
                eng.wait_ge(sem("d_kt"), 4 * q + f + 1)
                if f == 1 and positive(q):
                    eng.wait_ge(sem("d_sc"), q)
                eng.tensor_copy(KC[:, f, 0:w], ps[:, 1, 0:w]).then_inc(sem("d_kcv"), 1)

            def prompt_top(b, i, pm):
                n, w = QUARTERS * b + i, (step_of(pm, i)[1] + 1) * P
                mask = (mask_b if pm else mask_a)[:, NPR - w:NPR]
                if positive(n):
                    eng.wait_ge(sem("p_neg"), n)
                eng.wait_ge(sem("p_score"), n + 1)
                eng.tensor_tensor_reduce(out=PP[:, i % 4, 0:w], in0=ps[:, 5, 0:w], in1=mask, scale=1.0, scalar=MASKED,
                                         op0=ALU.add, op1=ALU.max, accum_out=col(8, i)).then_inc(sem("p_max"), 1)
                eng.wait_ge(sem("p_max"), n + 1)
                eng.tensor_scalar(col(12, i), col(8, i), -1.0, None, ALU.mult).then_inc(sem("p_neg"), 1)

            def prompt_norm(b, i, pm):
                h, q = step_of(pm, i)
                n, w = QUARTERS * b + i, (q + 1) * P
                eng.wait_ge(sem("p_exp"), n + 1)
                eng.reciprocal(col(20, i), col(16, i)).then_inc(sem("p_rl"), 1)
                eng.wait_ge(sem("p_rl"), n + 1)
                own, first = PP[:, i % 4, 0:w], PP[:, (i - 1) % 4, 0:w]
                if pm == 0:
                    eng.tensor_scalar(own, own, col(20, i), None, ALU.mult).then_inc(sem("p_norm"), 1)
                elif h == 1:
                    eng.tensor_scalar(own, own, col(20, i), stat[:, 3:4], ALU.mult, ALU.mult).then_inc(sem("p_second"), 1)
                    eng.wait_ge(sem("p_second"), 4 * b - 16 + q + 1)
                    eng.scalar_tensor_tensor(out=first, in0=first, scalar=col(20, i - 1), in1=own,
                                             op0=ALU.mult, op1=ALU.add).then_inc(sem("p_norm"), 1)

            def prompt_out(b, i, pm):
                h = i // 4
                r = slice(0, P) if pm == 1 else slice(h * E, (h + 1) * E)
                eng.wait_ge(sem("p_pv"), head_of(pm, b, i) + 1)
                eng.tensor_copy(QT[r, ds(b, 1), 0:NPR].rearrange("p a t -> p (a t)"), ps[r, 7, :]).then_inc(sem("p_out"), 1)

            def top(b, i):
                m, c = divmod(i, 4)
                w, o = chunk_keys(m, c), key0(m, tile0(m, c))
                bias = past_a[:, o:o + w] if m == 0 else zeros[:, 0:w]
                eng.wait_ge(sem("d_sc"), QUARTERS * b + i + 1)
                eng.tensor_tensor_reduce(out=S[m][:, o:o + w], in0=ps[:, 2, 0:w], in1=bias, scale=1.0, scalar=MASKED,
                                         op0=ALU.add, op1=ALU.max, accum_out=stat[:, 32 + c:33 + c]).then_inc(sem("d_smax"), 1)

            def body(b, run):
                for i in quarters(b):
                    m, c = divmod(i, 4)
                    u = 2 * b + m
                    o = WID[m]
                    if c == 1 and alive(b - 1):
                        eng.wait_ge(sem("d_rl"), u - 1)
                        eng.wait_ge(sem("d_pv"), 4 * (u - 2) + 4)
                        eng.tensor_scalar(On[:], ps[:, 4, 0:P], stat[:, 43 + m:44 + m], None, ALU.mult).then_inc(sem("d_on"), 1)
                    if alive(b):
                        evacuate(b, i, 1)
                    if c == 1 and alive(b - 1):
                        eng.wait_ge(sem("d_ot"), u - 1)
                        turned_o = ps[:, 4, P:2 * P].rearrange("p (f x) -> p f x", f=4)
                        cols = ds(b * NS + NPR - NS, NS)
                        if m == 0:
                            for h in range(2):
                                r = slice(h * E, (h + 1) * E)
                                eng.tensor_copy(QT[r, 0:4, cols], turned_o[r, :, h * NS:(h + 1) * NS]).then_inc(sem("d_out"), 1)
                        else:
                            eng.tensor_scalar(part[:], turned_o[:, :, NS:2 * NS], stat[:, 3:4], None, ALU.mult).then_inc(sem("d_out"), 1)
                            eng.wait_ge(sem("d_out"), 2 * (u - 2) + 1)
                            eng.tensor_tensor(QT[:, 4:8, cols], part[:], turned_o[:, :, 0:NS], ALU.add).then_inc(sem("d_out"), 1)
                    if alive(b):
                        prompt_top(b, i, mixer_of(b, run))
                    pb, pi = back(b, i, 2)
                    if c == 1 and alive(pb):
                        eng.wait_ge(sem("d_exp"), u)
                        eng.reciprocal(stat[:, 44 - m:45 - m], stat[:, 42:43]).then_inc(sem("d_rl"), 1)
                    if alive(b):
                        evacuate(b, i, 3)
                        if c == 0:
                            eng.wait_ge(sem("d_snew"), u + 1)
                            eng.tensor_tensor(S[m][:, o:o + NSM], ps[:, 5, 0:NSM], new_ab[:, m, ds(b, 1), :].rearrange("p a k -> p (a k)"),
                                              ALU.add).then_inc(sem("d_new"), 1)
                        prompt_norm(b, i, mixer_of(b, run))
                        if c == 1:
                            eng.wait_ge(sem("d_new"), u + 1)
                            eng.reduce_max(stat[:, 36:37], S[m][:, o:o + NSM], AX_X).then_inc(sem("d_mnew"), 1)
                    hb, hi_ = back(b, i, 3)
                    if alive(hb) and ends_head(mixer_of(hb, run), hi_):
                        prompt_out(hb, hi_, mixer_of(hb, run))
                    for part_ in range(2):
                        if norm_head(b, i, run, 4 + part_):
                            half = slice(part_ * NPR // 2, (part_ + 1) * NPR // 2)
                            eng.wait_ge(sem("r_std"), b - 4)
                            eng.reciprocal(rms[:, half], rms[:, half]).then_inc(sem("r_rs"), 1)
                    if alive(b):
                        top(b, i)
                    if norm_head(b, i, run, 5):
                        eng.wait_ge(sem("r_rs"), 2 * b - 8)
                        head = QT[:, ds(b - 1, 1), 0:NPR].rearrange("p a t -> p (a t)")
                        eng.scalar_tensor_tensor(out=head, in0=head, scalar=stat[:, 4:5], in1=rms,
                                                 op0=ALU.mult, op1=ALU.mult).then_inc(sem("r_rms"), 1)
                    if alive(b) and c == 3:
                        eng.wait_ge(sem("d_smax"), QUARTERS * b + i + 1)
                        eng.wait_ge(sem("d_mnew"), u + 1)
                        if positive(u):
                            eng.wait_ge(sem("d_neg"), u)
                            eng.wait_ge(sem("d_rl"), u)
                        eng.reduce_max(stat[:, 40:41], stat[:, 32:37], AX_X).then_inc(sem("d_mall"), 1)
                        eng.wait_ge(sem("d_mall"), u + 1)
                        eng.tensor_scalar(stat[:, 41:42], stat[:, 40:41], -1.0, None, ALU.mult).then_inc(sem("d_neg"), 1)
            eng.wait_ge(sem("d_zero"), 3)
            eng.wait_ge(sem("new_masks"), 16)
            each_sequence(body)

        def mix_tensor():
            pe = nc.tensor
            pe.wait_ge(sem("m_sq"), 1)
            pe.matmul(ps[:, 0, 0:4 * NSM], one_v[:], tmp[:, 0, 0:4 * NSM], start=True, stop=True).then_inc(sem("m_mean"), 1)

        def mix_scalar():
            eng = nc.scalar
            def upper(d):
                eng.activation(hhi[:, d, :], QT[:, d, :], ACT.Copy).then_inc(sem("m_hhi"), 1)
            eng.wait_ge(sem("d_out"), 4 * NB)
            eng.activation(tmp[:, 0, 0:4 * NSM].rearrange("p (f s) -> p f s", f=4), QT[:, 4:8, NPR:T],
                           ACT.Square).then_inc(sem("m_sq"), 1)
            upper(0)
            upper(1)
            eng.wait_ge(sem("m_mean"), 1)
            eng.activation(tmp[:, 1, 0:4 * NSM], ps[:, 0, 0:4 * NSM], ACT.Sqrt, bias=stat[:, 5:6], scale=1.0).then_inc(sem("m_std"), 1)
            upper(2)
            upper(3)
            split_hi(wo, 0, 0)
            split_hi(wo, 1, 1)
            eng.wait_ge(sem("m_rms"), 1)
            eng.wait_ge(sem("r_rms"), 4)
            for d in range(4, DB):
                upper(d)

        def mix_vector():
            eng = nc.vector
            def lower(d):
                eng.wait_ge(sem("m_hhi"), d + 1)
                eng.tensor_tensor(hlo[:, d, :], QT[:, d, :], hhi[:, d, :].bitcast(F32), ALU.subtract).then_inc(sem("m_hlo"), 1)
            lower(0)
            lower(1)
            eng.wait_ge(sem("m_std"), 1)
            eng.reciprocal(tmp[:, 1, 0:4 * NSM], tmp[:, 1, 0:4 * NSM]).then_inc(sem("m_rs"), 1)
            eng.wait_ge(sem("m_rs"), 1)
            eng.scalar_tensor_tensor(out=QT[:, 4:8, NPR:T], in0=QT[:, 4:8, NPR:T], scalar=stat[:, 4:5],
                                     in1=tmp[:, 1, 0:4 * NSM].rearrange("p (f s) -> p f s", f=4),
                                     op0=ALU.mult, op1=ALU.mult).then_inc(sem("m_rms"), 1)
            split_lo(wo, 0, 0)
            lower(2)
            lower(3)
            for d in range(4, DB):
                lower(d)
            split_lo(wo, 1, 1)

        def end_tensor():
            pe = nc.tensor
            for i in range(2 * (PT_ + 1)):
                kg, t = divmod(i, PT_ + 1)
                n = tokens(t)
                if t == 0:
                    pe.wait_ge(sem("step_x"), 4 * kg + 4)
                if i >= 8:
                    pe.wait_ge(sem(f"y_copied{i % 2}"), (i - 8) // 2 + 1)
                for k in range(4):
                    m = pe.transpose(ps[0:n, i % 8, k * P:(k + 1) * P], xT[:, 4 * kg + k, t * P:t * P + n], ident[:])
                m.then_inc(sem("y_turned"), 1)

        def end_copy(eng, i):
            kg, t = divmod(i, PT_ + 1)
            n = tokens(t)
            eng.wait_ge(sem("y_turned"), i + 1)
            dst, src = ytok[0:n, t, kg * 512:(kg + 1) * 512], ps[0:n, i % 8, :]
            m = eng.tensor_copy(dst, src) if i % 2 == 0 else eng.activation(dst, src, ACT.Copy)
            m.then_inc(sem(f"y_copied{i % 2}"), 1)

        def end_vector():
            for i in range(0, 2 * (PT_ + 1), 2):
                end_copy(nc.vector, i)

        def end_scalar():
            for i in range(1, 2 * (PT_ + 1), 2):
                end_copy(nc.scalar, i)

        def end_sync():
            eng = nc.sync
            for i in range(2 * (PT_ + 1)):
                kg, t = divmod(i, PT_ + 1)
                eng.wait_ge(sem(f"y_copied{i % 2}"), i // 2 + 1)
                cols = slice(kg * 512, (kg + 1) * 512)
                dst = y_prompt[0, t * P:(t + 1) * P, cols] if t < PT_ else y_sample.rearrange("b s d -> (b s) d")[:, cols]
                eng.dma_start(dst, ytok[0:tokens(t), t, cols]).then_inc(sem("y_kept"), 16)
            eng.wait_ge(sem("y_kept"), 2 * 16 * (PT_ + 1))
            for g in (1, 2, 4, 5):
                eng.wait_ge(sem(f"kept{g}"), 16 * (PT_ + 1))

        @block.sync
        def _(sp):
            start_sync()
            wo_v = w_o.rearrange("l (k p) n -> p (l k) n", p=P)
            ffn_loads(in1, out1, f1_in, f1_out)
            qkv_sync()
            attend_sync()
            sp.wait_ge(sem("p_pv"), HEADS)
            for d in range(DB):
                load_chunk(wo, d, d % 2, wo_v[:, :, d * P:(d + 1) * P], DB)
            ffn_loads(in3, out3, f2_in, f2_out)
            end_sync()

        @block.gpsimd
        def _(pool):
            start_pool()
            modulate_pool(0)
            pool.wait_ge(sem("mods"), NM)
            pool.wait_ge(sem("step_xa"), DB)
            pool.tensor_scalar(colA[:], colT[:, 72:120], ALPHA, None, ALU.mult).then_inc(sem("cols_a"), 1)
            pool.wait_ge(sem("cols_a"), 1)
            fuse_affine(1)
            fuse_affine(2)
            modulate_pool(1)
            attend_pool()
            modulate_pool(2)

        @block.scalar
        def _(act):
            start_scalar()
            split_hi(in1, 0, 0)
            split_hi(in1, 1, 1)
            modulate_scalar(0)
            ffn_in_scalar(0, 0, in1)
            project_scalar(0, out1, 2, 0, qkv)
            modulate_scalar(1)
            qkv_scalar()
            attend_scalar()
            mix_scalar()
            project_scalar(1, wo, 1, 1, in3)
            modulate_scalar(2)
            ffn_in_scalar(2, 1, in3)
            project_scalar(2, out3, 2, 2, None)
            end_scalar()

        @block.vector
        def _(dve):
            start_vector()
            split_lo(in1, 0, 0)
            split_lo(in1, 1, 1)
            modulate_vector(0)
            ffn_in_vector(0, 0, in1)
            project_vector(0, out1, 2, 2, qkv)
            modulate_vector(1)
            qkv_vector()
            attend_vector()
            mix_vector()
            project_vector(1, wo, 1, 5, in3)
            modulate_vector(2)
            ffn_in_vector(2, 1, in3)
            project_vector(2, out3, 2, 8, None)
            end_vector()

        @block.tensor
        def _(pe):
            start_tensor()
            ffn_in_tensor(0, 0, in1)
            pe.wait_ge(sem("ffn_fflo"), FB)
            project_tensor(0, out1, HB, 2, ffhi, fflo)
            qkv_tensor()
            attend_tensor()
            mix_tensor()
            project_tensor(1, wo, DB, 1, hhi, hlo, ("m_hlo", 0))
            ffn_in_tensor(2, 1, in3)
            pe.wait_ge(sem("ffn_fflo"), 2 * FB)
            project_tensor(2, out3, HB, 2, ffhi, fflo)
            end_tensor()


_INS = ["x_prompt", "x_sample", "c_prompt", "c_sample", "cache_win_k", "cache_win_v", "cache_diff_k", "cache_diff_v",
        "page_table", "ln_g", "ln_b", "w_ada", "b_ada", "ffn1_w_in", "ffn1_w_out", "ffn2_w_in", "ffn2_w_out",
        "w_qkv", "w_o", "diff_lambda", "subln_g"]
_CONSTS = ["ident", "rope", "mask_a", "mask_b", "past_a", "new_ab"]
_OUTS = [(1, 512, 1024), (8, 8, 1024), (1, 1, 512, 8, 64), (1, 1, 512, 8, 64), (1, 8, 8, 8, 64), (1, 8, 8, 8, 64),
         (1, 1, 4, 128, 4, 2, 64), (1, 1, 4, 128, 4, 128), (1, 8, 8, 4, 2, 64), (1, 8, 8, 4, 128)]


def kernel(**inputs):
    import concourse.bacc as _bacc
    from concourse.bass_utils import run_bass_kernel_spmd as _run

    nc = _bacc.Bacc("TRN2", target_bir_lowering=False, num_devices=1)
    tables = constants()
    arrays, args = {}, []
    for name in _INS + _CONSTS:
        a = np.ascontiguousarray(inputs[name] if name in _INS else tables[name])
        arrays[f"in_{name}_dram"] = a
        args.append(nc.dram_tensor(f"in_{name}_dram", a.shape, mybir.dt.from_np(a.dtype), kind="ExternalInput").ap())
    for i, shape in enumerate(_OUTS):
        args.append(nc.dram_tensor(f"out_{i}_dram", shape, F32, kind="ExternalOutput").ap())
    n = len(_INS + _CONSTS)
    yp, ys, wkp, wvp, wks, wvs, dkp, dvp, dks, dvs = args[n:]
    build(nc, *args[:n], yp, ys, wkp, wvp, wks, wvs, dkp, dvp, dks, dvs)
    r = _run(nc, [arrays], core_ids=[0])
    return tuple(r.results[0][f"out_{i}_dram"] for i in range(len(_OUTS)))
```
